# Optimizing a Trainium2 kernel written in Bass

```python
import math
import jax
import jax.numpy as jnp
from jax import lax
import numpy as np

"""Hybrid decoder block (Hymba-style parallel head groups): Mamba-2 SSD heads and GLA heads
read the same RMS-normalised stream through ONE combined input projection, their outputs are
concatenated over head groups into ONE output projection, followed by a top-4-of-32 clamped
SwiGLU mixture of experts (gpt-oss style). 16 learned meta tokens are prepended and dropped.
Inputs: x (BATCH, SEQ, D_MODEL) float32 plus parameters. Output: (BATCH, SEQ, D_MODEL)."""

D_MODEL = 1024
BATCH = 1
SEQ = 256
DEPTH = 1

N_META = 16
EPS = 1e-5
SSD_HEAD_DIM = 64
SSD_WIDTH = D_MODEL
SSD_HEADS = SSD_WIDTH // SSD_HEAD_DIM
SSD_GROUPS = 2
SSD_STATE = 128
SSD_CONV = 4
SSD_CHUNK = 128
GLA_HEADS = 4
GLA_K_WIDTH = D_MODEL // 2
GLA_V_WIDTH = D_MODEL
GLA_KEY_DIM = GLA_K_WIDTH // GLA_HEADS
GLA_VAL_DIM = GLA_V_WIDTH // GLA_HEADS
GLA_RANK = 16
GLA_TAU = 16.0
GLA_CHUNK = 16
MIX_WIDTH = SSD_WIDTH + GLA_V_WIDTH
XBC_WIDTH = SSD_WIDTH + 2 * SSD_GROUPS * SSD_STATE
IN_WIDTH = SSD_WIDTH + XBC_WIDTH + SSD_HEADS + 2 * GLA_K_WIDTH + 2 * GLA_V_WIDTH + GLA_RANK
N_EXPERTS = 32
TOP_K = 4
D_FF = D_MODEL
SWIGLU_LIMIT = 7.0
SWIGLU_ALPHA = 1.702
MOE_BLOCK = 256

kernel_name = "hymba_ssd_gla_moe_block"

def rms_norm(t, w):
    tf = t.astype(jnp.float32)
    tf = tf * lax.rsqrt(jnp.mean(tf * tf, axis=-1, keepdims=True) + EPS)
    return (tf * w.astype(jnp.float32)).astype(t.dtype)

def causal_depthwise_conv(u, w, b):
    c = u.shape[-1]
    out = lax.conv_general_dilated(u, w[:, None, :].astype(u.dtype), window_strides=(1,),
                                   padding=[(SSD_CONV - 1, 0)],
                                   dimension_numbers=('NWC', 'WIO', 'NWC'),
                                   feature_group_count=c)
    return out + b

def ssd_chunked(x, dt, a, bm, cm):
    b, lp, g, hg, p = x.shape
    n = bm.shape[-1]
    nc = lp // SSD_CHUNK
    q = SSD_CHUNK
    x = x.reshape(b, nc, q, g, hg, p)
    dt = dt.reshape(b, nc, q, g, hg)
    bm = bm.reshape(b, nc, q, g, n)
    cm = cm.reshape(b, nc, q, g, n)
    a_cs = jnp.cumsum(dt * a, axis=2)
    dtx = x * dt[..., None]
    acs_t = jnp.moveaxis(a_cs, 2, -1)
    seg = acs_t[..., :, None] - acs_t[..., None, :]
    causal = jnp.tril(jnp.ones((q, q), dtype=bool))
    decay = jnp.exp(jnp.where(causal, seg, -jnp.inf))
    cb = jnp.einsum('bclgn,bcsgn->bcgls', cm, bm)
    y_diag = jnp.einsum('bcghls,bcsghp->bclghp', cb[:, :, :, None] * decay, dtx)
    decay_to_end = jnp.exp(a_cs[:, :, -1:] - a_cs)
    states = jnp.einsum('bcsgn,bcsghp->bcghpn', bm, dtx * decay_to_end[..., None])
    chunk_decay = jnp.exp(a_cs[:, :, -1])

    def step(h, inp):
        dec, st = inp
        return dec[..., None, None] * h + st, h

    h0 = jnp.zeros((b, g, hg, p, n), states.dtype)
    _, h_prev = lax.scan(step, h0, (jnp.moveaxis(chunk_decay, 1, 0), jnp.moveaxis(states, 1, 0)))
    h_prev = jnp.moveaxis(h_prev, 0, 1)
    y_off = jnp.einsum('bclgn,bcghpn->bclghp', cm, h_prev) * jnp.exp(a_cs)[..., None]
    return (y_diag + y_off).reshape(b, lp, g, hg, p)

def gla_chunked(q, k, v, log_a):
    b, l, h, dk = q.shape
    dv = v.shape[-1]
    nc = l // GLA_CHUNK
    c = GLA_CHUNK
    q = q.reshape(b, nc, c, h, dk)
    k = k.reshape(b, nc, c, h, dk)
    v = v.reshape(b, nc, c, h, dv)
    g_cs = jnp.cumsum(log_a.reshape(b, nc, c, h, dk), axis=2)
    q_dec = q * jnp.exp(g_cs)
    k_inv = k * jnp.exp(-g_cs)
    k_end = k * jnp.exp(g_cs[:, :, -1:] - g_cs)
    causal = jnp.tril(jnp.ones((c, c), dtype=bool))
    scores = jnp.einsum('bclhd,bcshd->bchls', q_dec, k_inv)
    o_intra = jnp.einsum('bchls,bcshv->bclhv', jnp.where(causal, scores, 0.0), v)
    chunk_decay = jnp.exp(g_cs[:, :, -1])

    def step(s, inp):
        qd, ke, vc, dec = inp
        o = jnp.einsum('blhd,bhdv->blhv', qd, s)
        s = dec[..., None] * s + jnp.einsum('blhd,blhv->bhdv', ke, vc)
        return s, o

    s0 = jnp.zeros((b, h, dk, dv), jnp.float32)
    _, o_inter = lax.scan(step, s0, (jnp.moveaxis(q_dec, 1, 0), jnp.moveaxis(k_end, 1, 0),
                                     jnp.moveaxis(v, 1, 0), jnp.moveaxis(chunk_decay, 1, 0)))
    o = o_intra + jnp.moveaxis(o_inter, 0, 1)
    return o.reshape(b, l, h, dv)

def hybrid_mixer(u, w_in, conv_w, conv_b, dt_bias, a_log, d_skip, ssd_norm_w,
                 w_decay_up, b_decay, gla_norm_w, w_out):
    b, l, _ = u.shape
    proj = u @ w_in
    cuts = np.cumsum([SSD_WIDTH, XBC_WIDTH, SSD_HEADS, GLA_K_WIDTH, GLA_K_WIDTH,
                      GLA_V_WIDTH, GLA_V_WIDTH]).tolist()
    z, xbc, dt_raw, q, k, v, g_out, a_lr = jnp.split(proj, cuts, axis=-1)

    xbc = jax.nn.silu(causal_depthwise_conv(xbc, conv_w, conv_b))
    xs, bm, cm = jnp.split(xbc, [SSD_WIDTH, SSD_WIDTH + SSD_GROUPS * SSD_STATE], axis=-1)
    dt = jax.nn.softplus(dt_raw.astype(jnp.float32) + dt_bias.astype(jnp.float32))
    a = -jnp.exp(a_log.astype(jnp.float32))
    pad = SSD_CHUNK - N_META
    lp = l + pad
    hg = SSD_HEADS // SSD_GROUPS

    def pad_front(t):
        return jnp.pad(t, ((0, 0), (pad, 0)) + ((0, 0),) * (t.ndim - 2))

    y = ssd_chunked(pad_front(xs).reshape(b, lp, SSD_GROUPS, hg, SSD_HEAD_DIM),
                    pad_front(dt).reshape(b, lp, SSD_GROUPS, hg),
                    a.reshape(SSD_GROUPS, hg),
                    pad_front(bm).reshape(b, lp, SSD_GROUPS, SSD_STATE),
                    pad_front(cm).reshape(b, lp, SSD_GROUPS, SSD_STATE))
    y = y[:, pad:].reshape(b, l, SSD_HEADS, SSD_HEAD_DIM) \
        + d_skip[:, None] * xs.reshape(b, l, SSD_HEADS, SSD_HEAD_DIM)
    gsz = SSD_WIDTH // SSD_GROUPS
    y = y.reshape(b, l, SSD_GROUPS, gsz) * jax.nn.silu(z).reshape(b, l, SSD_GROUPS, gsz)
    y_ssd = rms_norm(y, ssd_norm_w.reshape(SSD_GROUPS, gsz)).reshape(b, l, SSD_WIDTH)

    log_a = jax.nn.log_sigmoid((a_lr @ w_decay_up + b_decay).astype(jnp.float32)) / GLA_TAU
    o = gla_chunked((q * GLA_KEY_DIM ** -0.5).reshape(b, l, GLA_HEADS, GLA_KEY_DIM),
                    k.reshape(b, l, GLA_HEADS, GLA_KEY_DIM),
                    v.reshape(b, l, GLA_HEADS, GLA_VAL_DIM),
                    log_a.reshape(b, l, GLA_HEADS, GLA_KEY_DIM))
    o = rms_norm(o, gla_norm_w) * jax.nn.silu(g_out.astype(jnp.float32)).reshape(b, l, GLA_HEADS, GLA_VAL_DIM)
    y_gla = o.reshape(b, l, GLA_V_WIDTH)

    mixed = jnp.concatenate([y_ssd.astype(u.dtype), y_gla.astype(u.dtype)], axis=-1)
    return mixed @ w_out

def moe_ffn(t, w_router, b_router, w_gate_up, b_gate_up, w_down, b_down):
    n, d = t.shape
    logits = (t @ w_router + b_router).astype(jnp.float32)
    top_logits, top_idx = lax.top_k(logits, TOP_K)
    gates = jax.nn.softmax(top_logits, axis=-1)
    m = n * TOP_K
    expert_flat = top_idx.reshape(m)
    order = jnp.argsort(expert_flat)
    expert_sorted = expert_flat[order]
    counts = jnp.bincount(expert_flat, length=N_EXPERTS)
    padded = (counts + MOE_BLOCK - 1) // MOE_BLOCK * MOE_BLOCK
    start = jnp.cumsum(counts) - counts
    pend = jnp.cumsum(padded)
    pstart = pend - padded
    dest_sorted = (pstart[expert_sorted] + jnp.arange(m) - start[expert_sorted]).astype(jnp.int32)
    n_blocks = -(-m // MOE_BLOCK) + N_EXPERTS
    rows = n_blocks * MOE_BLOCK
    src_token = jnp.full((rows,), n, jnp.int32).at[dest_sorted].set((order // TOP_K).astype(jnp.int32))
    t_pad = jnp.concatenate([t, jnp.zeros((1, d), t.dtype)], axis=0)
    buf = t_pad[src_token].reshape(n_blocks, MOE_BLOCK, d)
    block_expert = jnp.minimum(jnp.searchsorted(pend, jnp.arange(n_blocks) * MOE_BLOCK, side='right'),
                               N_EXPERTS - 1)

    def expert_block(args):
        xb, e = args
        hgu = xb @ w_gate_up[e] + b_gate_up[e]
        gate, up = jnp.split(hgu, 2, axis=-1)
        gate = jnp.minimum(gate, SWIGLU_LIMIT)
        up = jnp.clip(up, -SWIGLU_LIMIT, SWIGLU_LIMIT)
        act = gate * jax.nn.sigmoid(SWIGLU_ALPHA * gate)
        return ((up + 1.0) * act) @ w_down[e] + b_down[e]

    y_buf = lax.map(expert_block, (buf, block_expert)).reshape(rows, d)
    dest = jnp.zeros((m,), jnp.int32).at[order].set(dest_sorted)
    y = y_buf[dest].reshape(n, TOP_K, d)
    return jnp.einsum('nk,nkd->nd', gates.astype(t.dtype), y)

def setup_inputs(seed: int = 0) -> dict:
    key = jax.random.key(seed)
    ks = jax.random.split(key, 24)
    f32 = jnp.float32
    nrm = lambda k, shape, scale: jax.random.normal(k, shape, f32) * scale
    dt = jnp.exp(jax.random.uniform(ks[6], (DEPTH, SSD_HEADS), f32)
                 * (math.log(0.1) - math.log(1e-3)) + math.log(1e-3))
    return {
        'x': nrm(ks[0], (BATCH, SEQ, D_MODEL), 1.0),
        'meta_tokens': nrm(ks[1], (N_META, D_MODEL), 1.0),
        'mix_norm_w': 1.0 + nrm(ks[2], (DEPTH, D_MODEL), 0.02),
        'w_in': nrm(ks[3], (DEPTH, D_MODEL, IN_WIDTH), D_MODEL ** -0.5),
        'conv_w': nrm(ks[4], (DEPTH, SSD_CONV, XBC_WIDTH), SSD_CONV ** -0.5),
        'conv_b': nrm(ks[5], (DEPTH, XBC_WIDTH), 0.01),
        'dt_bias': dt + jnp.log(-jnp.expm1(-dt)),
        'a_log': jnp.log(jax.random.uniform(ks[7], (DEPTH, SSD_HEADS), f32, 1.0, 16.0)),
        'd_skip': 1.0 + nrm(ks[8], (DEPTH, SSD_HEADS), 0.1),
        'ssd_norm_w': 1.0 + nrm(ks[9], (DEPTH, SSD_WIDTH), 0.02),
        'w_decay_up': nrm(ks[10], (DEPTH, GLA_RANK, GLA_K_WIDTH), GLA_RANK ** -0.5),
        'b_decay': nrm(ks[11], (DEPTH, GLA_K_WIDTH), 0.01),
        'gla_norm_w': 1.0 + nrm(ks[12], (DEPTH, GLA_VAL_DIM), 0.02),
        'w_out': nrm(ks[13], (DEPTH, MIX_WIDTH, D_MODEL), MIX_WIDTH ** -0.5),
        'ffn_norm_w': 1.0 + nrm(ks[14], (DEPTH, D_MODEL), 0.02),
        'w_router': nrm(ks[15], (DEPTH, D_MODEL, N_EXPERTS), D_MODEL ** -0.5),
        'b_router': nrm(ks[16], (DEPTH, N_EXPERTS), 0.01),
        'w_gate_up': nrm(ks[17], (DEPTH, N_EXPERTS, D_MODEL, 2 * D_FF), D_MODEL ** -0.5),
        'b_gate_up': nrm(ks[18], (DEPTH, N_EXPERTS, 2 * D_FF), 0.01),
        'w_down': nrm(ks[19], (DEPTH, N_EXPERTS, D_FF, D_MODEL), D_FF ** -0.5),
        'b_down': nrm(ks[20], (DEPTH, N_EXPERTS, D_MODEL), 0.01),
        'final_norm_w': 1.0 + nrm(ks[21], (D_MODEL,), 0.02),
    }

def reference(x, meta_tokens, mix_norm_w, w_in, conv_w, conv_b, dt_bias, a_log, d_skip,
              ssd_norm_w, w_decay_up, b_decay, gla_norm_w, w_out, ffn_norm_w, w_router,
              b_router, w_gate_up, b_gate_up, w_down, b_down, final_norm_w):
    b = x.shape[0]
    meta = jnp.broadcast_to(meta_tokens[None].astype(x.dtype), (b, N_META, D_MODEL))
    h = jnp.concatenate([meta, x], axis=1)
    for i in range(DEPTH):
        h = h + hybrid_mixer(rms_norm(h, mix_norm_w[i]), w_in[i], conv_w[i], conv_b[i],
                             dt_bias[i], a_log[i], d_skip[i], ssd_norm_w[i], w_decay_up[i],
                             b_decay[i], gla_norm_w[i], w_out[i])
        if i == DEPTH - 1:
            h = h[:, N_META:]
        bb, ll, dd = h.shape
        ffn = moe_ffn(rms_norm(h, ffn_norm_w[i]).reshape(bb * ll, dd), w_router[i], b_router[i],
                      w_gate_up[i], b_gate_up[i], w_down[i], b_down[i])
        h = h + ffn.reshape(bb, ll, dd)
    return rms_norm(h, final_norm_w)


_drawn_inputs = setup_inputs


def setup_inputs(seed=0):
    import zlib

    import numpy as np

    out = dict(_drawn_inputs(seed))
    spreads = {}
    factors = {'conv_b': 2.823,
     'b_decay': 5.173,
     'gla_norm_w': 2.747,
     'b_gate_up': 8.0,
     'b_down': 8.0,
     'final_norm_w': 7.57,
     'b_router': 2.935}
    for name, (base, spread) in spreads.items():
        noise = np.random.default_rng([zlib.crc32(name.encode()), seed]).standard_normal(out[name].shape)
        drawn = base * np.exp(spread * noise) if base else spread * noise
        out[name] = jnp.asarray(drawn.astype(out[name].dtype))
    for name, factor in factors.items():
        out[name] = (out[name] * factor).astype(out[name].dtype)
    return out
```

```python
from contextlib import ExitStack

import concourse.bass as bass
from concourse import mybir

F32 = mybir.dt.float32
BF16 = mybir.dt.bfloat16
I32 = mybir.dt.int32
U32 = mybir.dt.uint32
ALU = mybir.AluOpType
ACT = mybir.ActivationFunctionType
AX_X = mybir.AxisListType.X

P = 128
D = 1024
KC = D // P
META = 16
SEQ = 256
T = META + SEQ
EPS = 1e-5
HEADS = 16
HD = 64
XBC0 = D
DT0 = XBC0 + D + 512
Q0 = DT0 + HEADS
K0 = Q0 + 512
V0 = K0 + 512
G0 = V0 + D
ALR0 = G0 + D
RANK = 16
GH = 4
CH = 16
NCH = T // CH
TAU = 16.0
NE = 32
TOPK = 4
LIMIT = 7.0
ALPHA = 1.702
SLOTS = 64
SWEEPS = SEQ // SLOTS
RING = 6
SLOT = 4096
CAUSAL = 1e30

TILES = [(0, 256, 0), (256, 144, 112), (400, 16, 240)]
PACK = 416

PANELS = [XBC0 + D, XBC0, XBC0 + 512, Q0, K0, V0, V0 + 512, 0, 512, G0, G0 + 512]
NP = len(PANELS)
MIX_FILLS = NP + 4
FIRST = 8
NPJ = FIRST + 4 * NP
OWNER = "V" * 7 + "A" + "V" * 12 + "V" * 8 + "A" * 8 + "A" * 16
B_C, XS, QQ, KK, VV, ZZ, GG = 8, 12, 20, 24, 28, 36, 44
HEAD_STEPS = {n: [n - 21] for n in range(21, 33)}
HEAD_STEPS.update({33: [12, 13], 34: [14, 15], 35: [16, 17]})
GLA_STEPS = {36 + i: range(1 + 4 * i, 5 + 4 * i) for i in range(4)}
OT_STEPS = {41: [0, 1], 42: [2, 3, 4], 43: [5, 6, 7]}


def freed(n, owner):
    return OWNER[:n + 1].count(owner)


def hybrid_moe_kernel(nc, x, meta, mix_w, w_in, conv_w, conv_b, dt_bias, a_log, d_skip, ssd_w, w_up,
                      b_decay, gla_w, w_out, ffn_w, w_router, b_router, w_gu, b_gu, w_dn, b_dn, fin_w, out):
    with ExitStack() as ctx:
        def sb(name, shape, dt=F32):
            return ctx.enter_context(nc.sbuf_tensor(name, shape, dt))

        def sem(name):
            return ctx.enter_context(nc.semaphore(name))

        ring = sb("ring", [P, RING, SLOT])
        ident = sb("ident", [P, P])
        ones = sb("ones", [P, P])
        before = sb("before", [P, P])
        minmask = sb("minmask", [P, PACK])
        causal = sb("causal", [P, PACK])
        slot_no = sb("slot_no", [P, 2, SLOTS])
        par_rows = sb("par_rows", [P, P])
        par = sb("par", [P, P])
        wsm = sb("wsm", [P, KC, 2 * HEADS])
        small = sb("small", [P, 64])
        acsT = sb("acsT", [HEADS, 384])
        keycols = sb("keycols", [P, 6, HEADS])
        dec = sb("dec", [P, GH, NCH])
        ssx = sb("ssx", [P, 8])
        reg_x = sb("reg_x", [P, 3 * D])
        reg_u = sb("reg_u", [P, KC * T])
        reg_c = sb("reg_c", [P, 12 * T + P])
        reg_v = sb("reg_v", [P, KC * T + P])
        reg_r = sb("reg_r", [P, 3 * D])
        reg_q = sb("reg_q", [P, GH * SEQ])
        reg_a = sb("reg_a", [P, 2 * GH * T])
        reg_s = sb("reg_s", [P, 6 * PACK])
        reg_m = sb("reg_m", [P, 16 * SEQ])
        tmp = sb("tmp", [P, 2, SEQ])
        sq = sb("sq", [P, 2, SEQ])

        junk = reg_r[:, 0:D]
        headrow = reg_r[0:HEADS, D:3 * D].rearrange("p (h n) -> p h n", h=HEADS)
        resets = reg_s[:, 0:GH * T]
        dta = reg_m[0:HEADS, 0:4 * T].rearrange("p (a n) -> p a n", a=4)
        wup = reg_m[0:RANK, 4 * T:4 * T + 512]
        spread = reg_m[0:HEADS, 4 * T + 512:4 * T + 512 + D]
        dtT = reg_q[0:HEADS, 0:384]
        alr = reg_q[0:RANK, 384:384 + T]
        rstd = reg_s[:, 0:6 * SEQ].rearrange("p (a n) -> p a n", a=6)
        x_rows = reg_x[:, 0:2 * D].rearrange("p (t n) -> p t n", t=2)
        meta_rows = reg_x[0:META, 2 * D:3 * D]
        dtx = reg_x[:, :].rearrange("p (t n) -> p t n", t=3)
        kx = reg_x[:, :].rearrange("p (b h n) -> p b h n", b=2, h=GH)
        uT = reg_u[:, :].rearrange("p (k n) -> p k n", k=KC)
        xbc = reg_c[:, 0:12 * T].rearrange("p (c n) -> p c n", c=12)
        vT = reg_v[:, 0:KC * T].rearrange("p (c n) -> p c n", c=KC)
        v_rows = reg_r[:, :].rearrange("p (t n) -> p t n", t=3)
        qd = reg_q[:, :].rearrange("p (h n) -> p h n", h=GH)
        ga = reg_a[:, 0:GH * T]
        gc = reg_a[:, GH * T:2 * GH * T]
        gb = reg_m[:, 8 * SEQ:8 * SEQ + GH * T] if GH * T <= 8 * SEQ else None
        seg = reg_s[:, 0:2 * PACK].rearrange("p (b n) -> p b n", b=2)
        mh = reg_s[:, 2 * PACK:4 * PACK].rearrange("p (b n) -> p b n", b=2)
        cb = reg_s[:, 4 * PACK:6 * PACK].rearrange("p (b n) -> p b n", b=2)
        sc = reg_s[:, 0:4 * PACK].rearrange("p (h n) -> p h n", h=GH)
        mixed = reg_m[:, :].rearrange("p (c n) -> p c n", c=16)

        def by_head(ap):
            return ap.rearrange("p (h n) -> p h n", h=GH)

        xn = reg_c[:, 0:2 * D].rearrange("p (t n) -> p t n", t=2)
        ffnw = reg_c[:, 2 * D:3 * D]
        xnT = reg_u[:, 0:KC * SEQ].rearrange("p (k n) -> p k n", k=KC)
        bgu = reg_v[:, 0:2 * D]
        parts = reg_r[:, :].bitcast(BF16).rearrange("p (i t n) -> p i t n", i=3, t=2)
        bdn = reg_q[0:NE, 0:D]
        finw = reg_m[:, 0:D]
        gateS, sigS, upS, actS = (reg_a[:, i * 512:(i + 1) * 512] for i in range(4))
        xg = reg_s[:, 0:512].rearrange("p (k s) -> p k s", k=KC)
        actT = reg_s[:, 512:1024].rearrange("p (j h s) -> p j h s", j=4, h=2)
        yS = reg_s[:, 1024:1536]
        gT = reg_s[:, 1536:1792]
        pg = reg_s[:, 1792:2048].rearrange("p (t s) -> p t s", t=2)
        pick = reg_s[:, 2048:2112].bitcast(BF16).rearrange("p (t s) -> p t s", t=2)
        esel = reg_s[:, 2112:2176]
        wr = sb("wr", [P, KC, NE])
        br = sb("br", [P, NE])
        expert_no = sb("expert_no", [P, NE])
        lg = sb("lg", [P, 2, NE])
        m8 = sb("m8", [P, 2, 8])
        i8 = sb("i8", [P, 2, 8], U32)
        i8f = sb("i8f", [P, 2, 8])
        ge = sb("ge", [P, 2, TOPK])
        chosen = sb("chosen", [P, 2, NE])
        gates = sb("gates", [P, 2, NE + 1])
        rank = sb("rank", [P, 2, NE + 1])
        rt = sb("rt", [P, 2, NE])
        gatesT = sb("gatesT", [NE, SEQ])
        most = sb("most", [P, 1], I32)

        bk = [ctx.enter_context(nc.psum_tensor(f"bank{i}", [P, 512], F32)) for i in range(8)]

        x_in = sem("x_in")
        par_in = sem("par_in")
        small_in = sem("small_in")
        wsm_in = sem("wsm_in")
        ffnw_in = sem("ffnw_in")
        x_again = sem("x_again")
        late_in = sem("late_in")
        cleared = sem("cleared")
        router_in = sem("router_in")
        filled = [sem(f"filled{i}") for i in range(RING)]
        used = sem("used")
        consts = sem("consts")
        zeroed = sem("zeroed")
        v_link = sem("v_link")
        a_link = sem("a_link")
        ssx_a = sem("ssx_a")
        ssx_v = sem("ssx_v")
        x_norm = sem("x_norm")
        par_t = sem("par_t")
        pj_full = sem("pj_full")
        pj_v = sem("pj_v")
        pj_a = sem("pj_a")
        sp_v = sem("sp_v")
        sp_a = sem("sp_a")
        cols_v = sem("cols_v")
        cols_t = sem("cols_t")
        dec_t = sem("dec_t")
        dec_v = sem("dec_v")
        dec_a = sem("dec_a")
        conv_v = sem("conv_v")
        silu_a = sem("silu_a")
        cb_t = sem("cb_t")
        cb_v = sem("cb_v")
        xs_t = sem("xs_t")
        xs_v = sem("xs_v")
        bc_t = sem("bc_t")
        seg_v = sem("seg_v")
        exp_a = sem("exp_a")
        m_v = sem("m_v")
        y_t = sem("y_t")
        y_v = sem("y_v")
        qd_v = sem("qd_v")
        vt_t = sem("vt_t")
        vt_a = sem("vt_a")
        kx_v = sem("kx_v")
        kx_t = sem("kx_t")
        sc_v = sem("sc_v")
        o_t = sem("o_t")
        o_a = sem("o_a")
        z_v = sem("z_v")
        sq_g = sem("sq_g")
        ss_t = sem("ss_t")
        ms_v = sem("ms_v")
        ms_a = sem("ms_a")
        mix_v = sem("mix_v")
        h_v = sem("h_v")
        xn_v = sem("xn_v")
        xt_t = sem("xt_t")
        xt_a = sem("xt_a")
        part_a = sem("part_a")
        part_v = sem("part_v")
        lg_t = sem("lg_t")
        top_v = sem("top_v")
        top_a = sem("top_a")
        sel_v = sem("sel_v")
        rank_t = sem("rank_t")
        table_v = sem("table_v")
        pick_v = sem("pick_v")
        gath_t = sem("gath_t")
        xg_a = sem("xg_a")
        esel_v = sem("esel_v")
        gu_t = sem("gu_t")
        clip_v = sem("clip_v")
        sig_a = sem("sig_a")
        act_v = sem("act_v")
        pg_v = sem("pg_v")
        pg_t = sem("pg_t")
        gt_a = sem("gt_a")
        at_t = sem("at_t")
        at_v = sem("at_v")
        yd_t = sem("yd_t")
        ys_a = sem("ys_a")
        comb_t = sem("comb_t")
        shift_v = sem("shift_v")
        fin_v = sem("fin_v")
        fin_a = sem("fin_a")
        stored = sem("stored")

        def tile_queries(t):
            c0, n, q0 = TILES[t]
            return slice(c0, c0 + n), slice(q0, SEQ)

        def sweeps(eng, one_sweep, most_ready):
            one_sweep(0)
            eng.wait_ge(table_v, most_ready)
            count = eng.value_load(most[0:1, 0:1])
            with eng.If(count > SLOTS):
                with eng.Fori(1, SWEEPS) as p:
                    one_sweep(p)

        MIXED_USED = 6
        MOST = 4
        block = ctx.enter_context(nc.Block())

        @block.sync
        def _(sp):
            sp.dma_start(x_rows, x[0].rearrange("(t p) n -> p t n", p=P)).then_inc(x_in, 16)
            sp.dma_start(meta_rows, meta).then_inc(x_in, 16)
            sp.dma_start(wsm[:, :, 0:HEADS],
                         w_in[0, :, DT0:Q0].rearrange("(k p) n -> p k n", p=P)).then_inc(wsm_in, 16)
            sp.dma_start(wsm[:, :, HEADS:],
                         w_in[0, :, ALR0:ALR0 + RANK].rearrange("(k p) n -> p k n", p=P)).then_inc(wsm_in, 16)
            for f in range(MIX_FILLS):
                if f >= RING:
                    sp.wait_ge(pj_full, FIRST + 4 * (f - RING + 1))
                if f < NP:
                    c = PANELS[f]
                    sp.dma_start(ring[:, f % RING, :].rearrange("p (k n) -> p k n", k=KC),
                                 w_in[0, :, c:c + 512].rearrange("(k p) n -> p k n", p=P)).then_inc(filled[f % RING], 16)
                else:
                    r = (f - NP) * 512
                    sp.dma_start(ring[:, f % RING, :].rearrange("p (k n) -> p k n", k=4),
                                 w_out[0, r:r + 512, :].rearrange("(k p) n -> p k n", p=P)).then_inc(filled[f % RING], 16)

            def sweep(p):
                with sp.Fori(0, NE) as e:
                    for i in range(RING):
                        s = (MIX_FILLS + i) % RING
                        sp.wait_ge(used, e * RING + (p * NE * RING + i + 1))
                        if i < 4:
                            src = w_gu[0, bass.ds(e, 1), i * 256:(i + 1) * 256, :].rearrange("o (k p) n -> p (o k) n", p=P)
                            dst = ring[:, s, :].rearrange("p (k n) -> p k n", k=2)
                        else:
                            src = w_dn[0, bass.ds(e, 1), (i - 4) * 512:(i - 3) * 512, :].rearrange("o (k p) n -> p (o k) n", p=P)
                            dst = ring[:, s, :].rearrange("p (k n) -> p k n", k=4)
                        sp.dma_start(dst, src).then_inc(filled[s], 16)

            sweeps(sp, sweep, MOST)
            sp.wait_ge(fin_v, 4)
            sp.dma_start(out[0].rearrange("(t p) n -> p t n", p=P), xn).then_inc(stored, 16)
            sp.wait_ge(stored, 16)

        @block.gpsimd
        def _(pool):
            g = nc.gpsimd
            g.memset(ident[:, :], 0.0).then_inc(consts, 1)
            g.memset(ones[:, :], 1.0).then_inc(consts, 1)
            g.memset(par_rows[:, :], 0.0).then_inc(consts, 1)
            pool.wait_ge(consts, 3)
            g.affine_select(out=ident[:, :], in_=ident[:, :], compare_op=ALU.not_equal, fill=1.0, base=0,
                            pattern=[[-1, P]], channel_multiplier=1).then_inc(consts, 1)
            r = 0
            for src, n in ((mix_w.rearrange("a (c p) -> (a c) p", p=P), 8),
                           (conv_w.rearrange("a t (c p) -> (a t c) p", p=P), 48),
                           (conv_b.rearrange("a (c p) -> (a c) p", p=P), 12),
                           (ssd_w.rearrange("a (c p) -> (a c) p", p=P), 8),
                           (b_decay.rearrange("a (c p) -> (a c) p", p=P), 4),
                           (gla_w.rearrange("a (c p) -> (a c) p", p=P), 2)):
                g.dma_start(par_rows[r:r + n, :], src).then_inc(par_in, 16)
                r += n
            g.dma_start(small[0:HEADS, 3:4], d_skip.rearrange("a h -> h a")).then_inc(small_in, 16)
            g.dma_start(small[0:HEADS, 0:1], dt_bias.rearrange("a h -> h a")).then_inc(small_in, 16)
            g.dma_start(small[0:HEADS, 1:2], a_log.rearrange("a h -> h a")).then_inc(small_in, 16)
            g.dma_start(wup, w_up[0]).then_inc(small_in, 16)
            g.memset(minmask[:, :], 0.0).then_inc(consts, 1)
            g.memset(causal[:, :], 1.0).then_inc(consts, 1)
            g.memset(before[:, :], 1.0).then_inc(consts, 1)
            g.memset(resets, 1.0).then_inc(consts, 1)
            pool.wait_ge(consts, 8)
            for m, fill in ((minmask, -CAUSAL), (causal, 0.0)):
                for t, base in enumerate((META, 0, 0)):
                    cols, _ = tile_queries(t)
                    g.affine_select(out=m[:, cols], in_=m[:, cols], compare_op=ALU.is_ge, fill=fill, base=base,
                                    pattern=[[1, TILES[t][1]]], channel_multiplier=-1).then_inc(consts, 1)
            g.affine_select(out=before[:, :], in_=before[:, :], compare_op=ALU.is_gt, fill=0.0, base=0,
                            pattern=[[1, P]], channel_multiplier=-1).then_inc(consts, 1)
            g.affine_select(out=resets.rearrange("p (c n) -> p c n", n=CH), in_=resets.rearrange("p (c n) -> p c n", n=CH),
                            compare_op=ALU.is_gt, fill=0.0, base=0, pattern=[[0, GH * NCH], [1, CH]],
                            channel_multiplier=0).then_inc(consts, 1)
            g.iota(slot_no[:, :, :], [[0, 2], [1, SLOTS]], base=0, channel_multiplier=0,
                   allow_small_or_imprecise_dtypes=True).then_inc(consts, 1)
            g.iota(expert_no[:, :], [[1, NE]], base=0, channel_multiplier=0,
                   allow_small_or_imprecise_dtypes=True).then_inc(consts, 1)
            g.dma_start(wr[:, :, :], w_router[0].rearrange("(k p) n -> p k n", p=P)).then_inc(router_in, 16)
            g.dma_start(br[:, :], b_router.broadcast_to([P, NE])).then_inc(router_in, 16)
            for c in range(8):
                pool.wait_ge(z_v, c + 1)
                if c >= 2:
                    pool.wait_ge(ss_t, c - 1)
                g.tensor_tensor(sq[:, c % 2, :], mixed[:, c, :], mixed[:, c, :], ALU.mult).then_inc(sq_g, 1)
            pool.wait_ge(y_v, 8)
            g.dma_start(ffnw, ffn_w.broadcast_to([P, D])).then_inc(ffnw_in, 16)
            pool.wait_ge(kx_t, NCH - 1)
            g.dma_start(x_rows, x[0].rearrange("(t p) n -> p t n", p=P)).then_inc(x_again, 16)
            pool.wait_ge(vt_t, 6)
            pool.wait_ge(zeroed, 1)
            g.dma_start(bgu[0:NE, :], b_gu[0]).then_inc(late_in, 16)
            for c in range(8):
                pool.wait_ge(o_a, c + 1)
                pool.wait_ge(ss_t, c + 7)
                g.tensor_tensor(sq[:, c % 2, :], mixed[:, 8 + c, :], mixed[:, 8 + c, :], ALU.mult).then_inc(sq_g, 1)
            g.dma_start(bdn, b_dn[0]).then_inc(late_in, 16)
            pool.wait_ge(used, MIXED_USED)
            g.dma_start(finw, fin_w.unsqueeze(0).broadcast_to([P, D])).then_inc(late_in, 16)

        @block.tensor
        def _(pe):
            mm = nc.tensor.matmul
            tr = nc.tensor.transpose

            pe.wait_ge(consts, 4)
            pe.wait_ge(par_in, 6 * 16)
            tr(bk[7][:, 0:P], par_rows[:, :], ident[:, :]).then_inc(par_t, 1)
            for n in range(6):
                t = n // 2
                pe.wait_ge(x_norm, t + 1)
                if n >= 2:
                    pe.wait_ge(pj_v, freed(n - 2, "V"))
                for j in range(4):
                    c = (4 * (n % 2) + j) * P
                    if t == 0:
                        last = tr(bk[n % 2][:, j * P:j * P + META], meta_rows[:, c:c + P], ident[0:META, 0:META])
                    else:
                        last = tr(bk[n % 2][:, j * P:(j + 1) * P], x_rows[:, t - 1, c:c + P], ident[:, :])
                last.then_inc(pj_full, 1)

            def bank_free(n):
                pe.wait_ge(pj_v if OWNER[n - 2] == "V" else pj_a, freed(n - 2, OWNER[n - 2]))

            pe.wait_ge(pj_v, 6)
            pe.wait_ge(wsm_in, 32)
            for n in (6, 7):
                bank_free(n)
                for k in range(KC):
                    last = mm(bk[n % 2][0:16, 0:T], wsm[:, k, (n - 6) * 16:(n - 5) * 16], uT[:, k, :],
                              start=(k == 0), stop=(k == KC - 1))
                last.then_inc(pj_full, 1)

            pe.wait_ge(cols_v, 1)
            pe.wait_ge(small_in, 64)
            for c in range(8):
                last = mm(bk[7][:, P + c:P + c + 1], spread[:, c * P:(c + 1) * P], small[0:HEADS, 3:4], start=True, stop=True)
            last.then_inc(par_t, 1)

            def decay_up():
                pe.wait_ge(pj_a, 1)
                pe.wait_ge(small_in, 64)
                for h in range(GH):
                    if h >= 2:
                        pe.wait_ge(dec_v, h - 1)
                    mm(bk[2 + h % 2][:, 0:T], wup[:, h * P:(h + 1) * P], alr, start=True, stop=True).then_inc(dec_t, 1)

            def key_columns():
                pe.wait_ge(cols_v, 3)
                for i, src in enumerate((acsT, dtT)):
                    for t in range(3):
                        last = tr(bk[6][:, (3 * i + t) * 16:(3 * i + t + 1) * 16], src[:, t * P:(t + 1) * P], ident[0:16, 0:16])
                last.then_inc(cols_t, 1)

            def c_times_b():
                pe.wait_ge(silu_a, 4)
                for g in range(2):
                    b0 = (8 + g) * T
                    for t in range(3):
                        cols, q = tile_queries(t)
                        last = mm(bk[4 + g][:, cols], reg_c[:, b0 + t * P:b0 + (t + 1) * P],
                                  xbc[:, 10 + g, META + q.start:], start=True, stop=True)
                    last.then_inc(cb_t, 1)

            def xs_rows(g):
                t, half = g // 2, g % 2
                if g == 0:
                    pe.wait_ge(silu_a, 12)
                    pe.wait_ge(cb_v, 2)
                if g >= 2:
                    pe.wait_ge(xs_v, g - 1)
                for j in range(4):
                    c = (4 * half + j) * T + t * P
                    last = tr(bk[4 + g % 2][:, j * P:(j + 1) * P], reg_c[:, c:c + P], ident[:, :])
                last.then_inc(xs_t, 1)

            def head_step(s):
                if s < HEADS:
                    if s >= 2:
                        pe.wait_ge(seg_v, 3 * (s - 1))
                    else:
                        pe.wait_ge(dec_v, GH)
                        pe.wait_ge(cols_v, 4)
                    mm(bk[2 + s % 2][:, 0:SEQ], headrow[:, s, :], acsT[:, META:T], start=True, stop=True).then_inc(bc_t, 1)
                if s >= 2:
                    h = s - 2
                    pe.wait_ge(m_v, h + 1)
                    if h % 2 == 0 and h >= 4:
                        pe.wait_ge(y_v, h // 2 - 1)
                    if h == 0:
                        pe.wait_ge(xs_v, 6)
                    r = HD * (h % 2)
                    for t in range(3):
                        cols, q = tile_queries(t)
                        last = mm(bk[6 + h // 2 % 2][r:r + HD, q], dtx[:, t, h * HD:(h + 1) * HD], mh[:, h % 2, cols],
                                  start=(t == 0), stop=(t == 2), skip_group_check=True)
                    last.then_inc(y_t, 1)

            def v_to_rows(g):
                t, half = g // 2, g % 2
                if g == 0:
                    pe.wait_ge(pj_a, freed(VV + 7, "A"))
                else:
                    pe.wait_ge(vt_a, g)
                for j in range(4):
                    c = (4 * half + j) * T + t * P
                    last = tr(bk[5][:, j * P:(j + 1) * P], reg_v[:, c:c + P], ident[:, :])
                last.then_inc(vt_t, 1)

            SCB = (2, 3, 6, 7)

            def gla_scores(j):
                pe.wait_ge(kx_v, j)
                if j == 1:
                    pe.wait_ge(y_v, 8)
                for h in range(GH):
                    q = qd[:, h, (j - 1) * CH:j * CH]
                    for t in range(3):
                        c0, n, q0 = TILES[t]
                        if (j - 1) * CH >= q0:
                            c = c0 + (j - 1) * CH - q0
                            last = mm(bk[SCB[h]][:, c:c + CH], kx[:, j % 2, h, t * P:(t + 1) * P], q, start=True, stop=True)
                last.then_inc(kx_t, 1)

            def gla_out(i):
                h = i // 2
                pe.wait_ge(sc_v, GH)
                if i == 0:
                    pe.wait_ge(vt_a, 6)
                if i >= 2:
                    pe.wait_ge(o_a, i - 1)
                for t in range(3):
                    cols, q = tile_queries(t)
                    last = mm(bk[2 + i % 2][:, q], v_rows[:, t, i * P:(i + 1) * P], sc[:, h, cols],
                              start=(t == 0), stop=(t == 2), skip_group_check=True)
                last.then_inc(o_t, 1)

            def sum_squares(c):
                pe.wait_ge(sq_g, c + 1)
                if c < 8:
                    if c == 0:
                        pe.wait_ge(xs_v, 6)
                    o, first, final = bk[4][:, (c // 4) * SEQ:(c // 4 + 1) * SEQ], c % 4 == 0, c % 4 == 3
                else:
                    h = (c - 8) // 2
                    o, first, final = bk[6 + h // 2][:, (h % 2) * SEQ:(h % 2 + 1) * SEQ], c % 2 == 0, c % 2 == 1
                mm(o, ones[:, :], sq[:, c % 2, :], start=first, stop=final).then_inc(ss_t, 1)

            for n in range(FIRST, NPJ):
                m = n - FIRST
                f = m // 4
                if m % 4 == 0:
                    pe.wait_ge(filled[f % RING], 16 * (f // RING + 1))
                bank_free(n)
                panel = ring[:, f % RING, :].rearrange("p (k c) -> p k c", k=KC)
                t0 = 0 if n < QQ or KK <= n < ZZ else META
                for k in range(KC):
                    last = mm(bk[n % 2][:, 0:T - t0], panel[:, k, (m % 4) * P:(m % 4 + 1) * P], uT[:, k, t0:],
                              start=(k == 0), stop=(k == KC - 1))
                last.then_inc(pj_full, 1)
                if n == 9:
                    decay_up()
                if n == 14:
                    key_columns()
                    c_times_b()
                if n in (20, 21):
                    for g in range(3 * (n - 20), 3 * (n - 19)):
                        xs_rows(g)
                for s in HEAD_STEPS.get(n, ()):
                    head_step(s)
                if ZZ <= n < ZZ + 6:
                    v_to_rows(n - ZZ)
                for j in GLA_STEPS.get(n, ()):
                    gla_scores(j)
                if ZZ + 2 <= n < ZZ + 8:
                    sum_squares(n - ZZ - 2)
                for i in OT_STEPS.get(n, ()):
                    gla_out(i)
                if n in (GG, GG + 1):
                    sum_squares(6 + n - GG)
                if GG + 2 <= n < GG + 6:
                    sum_squares(8 + 2 * (n - GG - 2))
                    sum_squares(9 + 2 * (n - GG - 2))

            for f in range(NP, MIX_FILLS):
                pe.wait_ge(filled[f % RING], 16 * (f // RING + 1))
                w = ring[:, f % RING, :].rearrange("p (k c) -> p k c", k=4)
                for kk in range(4):
                    k = 4 * (f - NP) + kk
                    pe.wait_ge(mix_v, k + 1)
                    for t in range(2):
                        for half in range(2):
                            last = mm(bk[4 + 2 * t + half][:, :], mixed[:, k, t * P:(t + 1) * P], w[:, kk, half * 512:(half + 1) * 512],
                                      start=(k == 0), stop=(k == 15))
                    if f == NP and kk < 2:
                        last.then_inc(used, 1)
                last.then_inc(used, 1)

            for i in range(4):
                t, half = i // 2, i % 2
                pe.wait_ge(xn_v, t + 1)
                for j in range(4):
                    c = (4 * half + j) * P
                    last = tr(bk[i][:, j * P:(j + 1) * P], xn[:, t, c:c + P], ident[:, :])
                last.then_inc(xt_t, 1)
            pe.wait_ge(xt_a, 4)
            pe.wait_ge(router_in, 32)
            for t in range(2):
                for k in range(KC):
                    last = mm(bk[0][:, t * NE:(t + 1) * NE], xnT[:, k, t * P:(t + 1) * P], wr[:, k, :],
                              start=(k == 0), stop=(k == KC - 1))
            last.then_inc(lg_t, 1)
            pe.wait_ge(sel_v, 1)
            mm(bk[1][:, 0:NE], before[:, :], chosen[:, 0, :], start=True, stop=True)
            mm(bk[1][:, NE:2 * NE], ones[:, :], chosen[:, 0, :], start=True, stop=False)
            mm(bk[1][:, NE:2 * NE], before[:, :], chosen[:, 1, :], start=False, stop=True)
            mm(bk[2][:, 0:NE], ones[:, :], chosen[:, 0, :], start=True, stop=False)
            mm(bk[2][:, 0:NE], ones[:, :], chosen[:, 1, :], start=False, stop=True)
            tr(bk[3][0:NE, 0:P], gates[:, 0, 0:NE], ident[:, :])
            tr(bk[3][0:NE, P:2 * P], gates[:, 1, 0:NE], ident[:, :]).then_inc(rank_t, 1)
            pe.wait_ge(table_v, MOST)
            pe.wait_ge(h_v, 4)
            pe.wait_ge(late_in, 3 * 16)
            for t in range(2):
                for half in range(2):
                    last = mm(bk[4 + 2 * t + half][:, :], gatesT[:, t * P:(t + 1) * P], bdn[:, half * 512:(half + 1) * 512],
                              start=True, stop=False, skip_group_check=True)
                    if t == 0:
                        last.then_inc((gu_t, pg_t)[half], 1)

            def gather(count):
                pe.wait_ge(pick_v, count)
                for k in range(KC):
                    for t in range(2):
                        for i in range(3):
                            last = mm(bk[3][:, k * SLOTS:(k + 1) * SLOTS], parts[:, i, t, k * P:(k + 1) * P], pick[:, t, :],
                                      start=(t == 0 and i == 0), stop=(t == 1 and i == 2))
                last.then_inc(gath_t, 1)

            def sweep(p):
                if isinstance(p, int):
                    pe.wait_ge(part_a, 3)
                gather(p * (NE + 1) + 1)
                with pe.Fori(0, NE) as e:
                    pe.wait_ge(xg_a, e + (p * (NE + 1) + 1))
                    for i in range(4):
                        s = (MIX_FILLS + i) % RING
                        pe.wait_ge(filled[s], e * 16 + (p * NE * 16 + 16 * ((MIX_FILLS + i) // RING + 1)))
                        w = ring[:, s, :].rearrange("p (k n) -> p k n", k=2)
                        for kk in range(2):
                            k = 2 * i + kk
                            for up in range(2):
                                for half in range(2):
                                    last = mm(bk[up][half * SLOTS:(half + 1) * SLOTS, :], xg[:, k, :],
                                              w[:, kk, up * D + half * 512:up * D + (half + 1) * 512],
                                              start=(k == 0), stop=False, skip_group_check=True)
                        last.then_inc(used, 1)
                    pe.wait_ge(esel_v, e + (p * NE + 1))
                    for up in range(2):
                        for half in range(2):
                            last = mm(bk[up][half * SLOTS:(half + 1) * SLOTS, :], esel[:, :],
                                      bgu[:, up * D + half * 512:up * D + (half + 1) * 512],
                                      start=False, stop=True, skip_group_check=True)
                    last.then_inc(gu_t, 1)
                    pe.wait_ge(pg_v, e + (p * NE + 1))
                    for t in range(2):
                        last = tr(bk[2][:, t * P:(t + 1) * P], pg[:, t, :], ident[:, :])
                    last.then_inc(pg_t, 1)
                    gather(e + (p * (NE + 1) + 2))
                    pe.wait_ge(act_v, e + (p * NE + 1))
                    pe.wait_ge(xg_a, e + (p * (NE + 1) + 2))
                    for j in range(4):
                        last = tr(bk[3][:, j * P:(j + 1) * P], actS[:, j * P:(j + 1) * P], ident[:, :])
                    last.then_inc(at_t, 1)
                    pe.wait_ge(at_v, e + (p * NE + 1))
                    pe.wait_ge(gt_a, e + (p * NE + 1))
                    for i in range(4, 6):
                        s = (MIX_FILLS + i) % RING
                        pe.wait_ge(filled[s], e * 16 + (p * NE * 16 + 16 * ((MIX_FILLS + i) // RING + 1)))
                        w = ring[:, s, :].rearrange("p (k n) -> p k n", k=4)
                        for j in range(4):
                            for half in range(2):
                                last = mm(bk[2][half * SLOTS:(half + 1) * SLOTS, :], actT[:, j, i - 4, :],
                                          w[:, j, half * 512:(half + 1) * 512],
                                          start=(i == 4 and j == 0), stop=(i == 5 and j == 3), skip_group_check=True)
                        last.then_inc(used if i == 4 else yd_t, 1)
                    pe.wait_ge(ys_a, e + (p * NE + 1))
                    for t in range(2):
                        for half in range(2):
                            r = half * SLOTS
                            last = mm(bk[4 + 2 * t + half][:, :], gT[r:r + SLOTS, t * P:(t + 1) * P], yS[r:r + SLOTS, :],
                                      start=False, stop=False, skip_group_check=True)
                            if t == half == 0:
                                last.then_inc(used, 1)
                    last.then_inc(comb_t, 1)

            sweeps(pe, sweep, MOST)

        @block.scalar
        def _(act):
            a = nc.scalar

            def copy(out, in_):
                return a.activation(out, in_, ACT.Copy)

            act.wait_ge(x_in, 32)
            act.wait_ge(cleared, 1)
            a.activation(junk[0:META, :], meta_rows, ACT.Square, accum_out=ssx[0:META, 0:1]).then_inc(ssx_a, 1)
            for t in range(2):
                act.wait_ge(ssx_a, t + 1)
                a.activation(junk, x_rows[:, t, :], ACT.Square, accum_out=ssx[:, 1 + t:2 + t]).then_inc(ssx_a, 1)
            act.wait_ge(ssx_v, 1)
            a.activation(ssx[:, 3:6], ssx[:, 3:6], ACT.Sqrt).then_inc(ssx_a, 1)
            act.wait_ge(small_in, 64)
            a.activation(small[0:HEADS, 2:3], small[0:HEADS, 1:2], ACT.Exp).then_inc(sp_a, 1)
            act.wait_ge(pj_full, 8)
            copy(alr, bk[1][0:RANK, 0:T]).then_inc(pj_a, 1)
            act.wait_ge(sp_v, 1)
            a.activation(dta[:, 1, :], dta[:, 1, :], ACT.Exp, scale=-1.0).then_inc(sp_a, 1)
            act.wait_ge(sp_v, 2)
            a.activation(dta[:, 3, :], dta[:, 2, :], ACT.Ln).then_inc(sp_a, 1)
            act.wait_ge(dec_v, 5)
            a.activation(gb, gb, ACT.Exp, scale=-1.0).then_inc(dec_a, 1)
            act.wait_ge(dec_a, 1)
            a.activation(gb, gb, ACT.Ln, bias=1.0).then_inc(dec_a, 1)
            act.wait_ge(dec_v, 7)
            a.activation(gb, ga, ACT.Exp, scale=1.0 / TAU).then_inc(dec_a, 1)
            a.activation(gc, ga, ACT.Exp, scale=-1.0 / TAU).then_inc(dec_a, 1)
            act.wait_ge(dec_v, 9)
            a.activation(ga, ga, ACT.Exp, scale=1.0 / TAU).then_inc(dec_a, 1)
            a.activation(dec[:, :, :], dec[:, :, :], ACT.Exp, scale=1.0 / TAU).then_inc(dec_a, 1)
            for i in range(12):
                c = (8 + i) % 12
                act.wait_ge(conv_v, i + 1)
                a.activation(xbc[:, c, :], xbc[:, c, :], ACT.Silu).then_inc(silu_a, 1)
            for n in range(QQ, NPJ):
                if VV <= n < ZZ:
                    act.wait_ge(pj_full, n + 1)
                    copy(vT[:, n - VV, :], bk[n % 2][:, 0:T]).then_inc(pj_a, 1)
                for s in HEAD_STEPS.get(n, ()):
                    if s < HEADS:
                        act.wait_ge(seg_v, 3 * (s + 1))
                        a.activation(seg[:, s % 2, :], seg[:, s % 2, :], ACT.Exp).then_inc(exp_a, 1)
                if n >= ZZ:
                    act.wait_ge(pj_full, n + 1)
                    if n >= ZZ + 2:
                        act.wait_ge(z_v, n - ZZ - 1)
                    a.activation(tmp[:, n % 2, :], bk[n % 2][:, 0:SEQ], ACT.Silu).then_inc(pj_a, 1)
                if ZZ <= n < ZZ + 6:
                    g = n - ZZ
                    act.wait_ge(vt_t, g + 1)
                    copy(v_rows[:, g // 2, (g % 2) * 512:(g % 2 + 1) * 512], bk[5][:, :]).then_inc(vt_a, 1)
                for i in OT_STEPS.get(n, ()):
                    act.wait_ge(o_t, i + 1)
                    copy(mixed[:, 8 + i, :], bk[2 + i % 2][:, 0:SEQ]).then_inc(o_a, 1)
                if n == GG + 5:
                    act.wait_ge(ms_v, 3)
                    a.activation(rstd, rstd, ACT.Sqrt).then_inc(ms_a, 1)
            spare = reg_m[:, 8 * SEQ:8 * SEQ + D]
            act.wait_ge(h_v, 4)
            for t in range(2):
                a.activation(spare, x_rows[:, t, :], ACT.Square, accum_out=ssx[:, t:t + 1]).then_inc(ssx_a, 1)
                act.wait_ge(ssx_a, 5 + t)
            act.wait_ge(ssx_v, 2)
            a.activation(ssx[:, 2:4], ssx[:, 2:4], ACT.Sqrt).then_inc(ssx_a, 1)
            for i in range(4):
                act.wait_ge(xt_t, i + 1)
                copy(xnT[:, 4 * (i % 2):4 * (i % 2) + 4, (i // 2) * P:(i // 2 + 1) * P],
                     bk[i][:, :].rearrange("p (k n) -> p k n", k=4)).then_inc(xt_a, 1)
            copy(parts[:, 0, :, :], xn).then_inc(part_a, 1)
            act.wait_ge(part_v, 1)
            copy(parts[:, 1, :, :], xn).then_inc(part_a, 1)
            act.wait_ge(part_v, 2)
            copy(parts[:, 2, :, :], xn).then_inc(part_a, 1)
            act.wait_ge(top_v, 3)
            for t in range(2):
                a.activation(ge[:, t, :], m8[:, t, 0:TOPK], ACT.Exp, bias=ssx[:, 4 + t:5 + t]).then_inc(top_a, 1)

            def sweep(p):
                act.wait_ge(gath_t, p * (NE + 1) + 1)
                copy(xg, bk[3][:, :].rearrange("p (k s) -> p k s", k=KC)).then_inc(xg_a, 1)
                with act.Fori(0, NE) as e:
                    act.wait_ge(clip_v, e * 3 + (p * NE * 3 + 1))
                    a.activation(sigS, gateS, ACT.Sigmoid, scale=ALPHA).then_inc(sig_a, 1)
                    act.wait_ge(pg_t, e + (p * NE + 2))
                    copy(gT, bk[2][:, 0:2 * P]).then_inc(gt_a, 1)
                    act.wait_ge(gath_t, e + (p * (NE + 1) + 2))
                    copy(xg, bk[3][:, :].rearrange("p (k s) -> p k s", k=KC)).then_inc(xg_a, 1)
                    act.wait_ge(yd_t, e + (p * NE + 1))
                    copy(yS, bk[2][:, :]).then_inc(ys_a, 1)

            sweeps(act, sweep, MOST)
            act.wait_ge(fin_v, 1)
            for t in range(2):
                a.activation(spare, x_rows[:, t, :], ACT.Square, accum_out=ssx[:, t:t + 1]).then_inc(fin_a, 1)
                act.wait_ge(fin_a, 1 + t)
            act.wait_ge(fin_v, 2)
            a.activation(ssx[:, 2:4], ssx[:, 2:4], ACT.Sqrt).then_inc(fin_a, 1)

        @block.vector
        def _(dve):
            v = nc.vector
            links = [0]

            def link(ins):
                links[0] += 1
                ins.then_inc(v_link, 1)
                dve.wait_ge(v_link, links[0])

            v.memset(ssx[:, :], 1.0)
            v.memset(dtT, 0.0)
            v.memset(acsT[:, :], 0.0)
            v.memset(rank[:, :, :], -1.0)
            v.memset(gates[:, :, :], 0.0)
            link(v.memset(reg_v[:, KC * T:], 0.0))
            v.memset(dta[:, 1, :], 1.0).then_inc(cleared, 1)
            dve.wait_ge(par_t, 1)
            link(v.tensor_copy(par[:, :], bk[7][:, 0:P]))
            dve.wait_ge(ssx_a, 3)
            v.tensor_scalar(ssx[:, 3:6], ssx[:, 0:3], 1.0 / D, EPS, ALU.mult, ALU.add).then_inc(ssx_v, 1)
            dve.wait_ge(ssx_a, 4)
            link(v.reciprocal(ssx[:, 3:6], ssx[:, 3:6]))
            v.tensor_scalar(meta_rows, meta_rows, ssx[0:META, 3:4], None, ALU.mult).then_inc(x_norm, 1)
            for t in range(2):
                v.tensor_scalar(x_rows[:, t, :], x_rows[:, t, :], ssx[:, 4 + t:5 + t], None, ALU.mult).then_inc(x_norm, 1)
            dve.wait_ge(consts, 4)
            v.tensor_copy(spread.rearrange("p (h n) -> p h n", h=HEADS),
                          ident[0:HEADS, 0:HEADS].unsqueeze(2).broadcast_to([HEADS, HEADS, HD]))
            v.tensor_copy(headrow[:, :, :], ident[0:HEADS, 0:HEADS].unsqueeze(2).broadcast_to([HEADS, HEADS, P])).then_inc(cols_v, 1)
            for n in range(6):
                t, k0 = n // 2, 4 * (n % 2)
                w = META if t == 0 else P
                c = 0 if t == 0 else META + (t - 1) * P
                dve.wait_ge(pj_full, n + 1)
                v.tensor_tensor(uT[:, k0:k0 + 4, c:c + w], bk[n % 2][:, :].rearrange("p (k n) -> p k n", k=4)[:, :, 0:w],
                                par[:, k0:k0 + 4].unsqueeze(2).broadcast_to([P, 4, w]), ALU.mult).then_inc(pj_v, 1)
            dve.wait_ge(pj_full, 7)
            dve.wait_ge(small_in, 64)
            v.tensor_scalar(dta[:, 0, :], bk[0][0:HEADS, 0:T], small[0:HEADS, 0:1], None, ALU.add).then_inc(pj_v, 1)
            dve.wait_ge(pj_v, 7)
            v.scalar_tensor_tensor(dta[:, 1, :], dta[:, 0, :], -1.0, dta[:, 0, :], ALU.mult, ALU.max).then_inc(sp_v, 1)

            dve.wait_ge(par_t, 2)
            link(v.tensor_copy(par[:, 82:90], bk[7][:, P:P + 8]))

            def conv(n):
                c = n - B_C + 8 if n < XS else n - XS
                bank, o = bk[n % 2], xbc[:, c, :]
                dve.wait_ge(pj_full, n + 1)
                link(v.tensor_scalar(o, bank[:, 0:T], par[:, 8 + 36 + c:9 + 36 + c], par[:, 56 + c:57 + c], ALU.mult, ALU.add))
                for back in (1, 2):
                    tap = 8 + 12 * (3 - back) + c
                    link(v.scalar_tensor_tensor(o[:, back:], bank[:, 0:T - back], par[:, tap:tap + 1], o[:, back:],
                                                ALU.mult, ALU.add))
                v.scalar_tensor_tensor(o[:, 3:], bank[:, 0:T - 3], par[:, 8 + c:9 + c], o[:, 3:],
                                       ALU.mult, ALU.add).then_inc(pj_v, 1)
                dve.wait_ge(pj_v, freed(n, "V"))
                v.tensor_copy(ssx[0:1, 7:8], ssx[0:1, 6:7]).then_inc(conv_v, 1)

            conv(8)
            dve.wait_ge(sp_a, 2)
            v.tensor_scalar(dta[:, 2, :], dta[:, 1, :], 1.0, None, ALU.add).then_inc(sp_v, 1)
            conv(9)
            dve.wait_ge(sp_a, 3)
            link(v.scalar_tensor_tensor(dta[:, 1, :], dta[:, 2, :], -1.0, dta[:, 1, :], ALU.add, ALU.subtract))
            link(v.reciprocal(dta[:, 2, :], dta[:, 2, :]))
            link(v.tensor_tensor(dta[:, 1, :], dta[:, 1, :], dta[:, 2, :], ALU.mult))
            link(v.tensor_tensor(dta[:, 3, :], dta[:, 3, :], dta[:, 1, :], ALU.subtract))
            v.scalar_tensor_tensor(dtT[:, 0:T], dta[:, 0, :], 0.0, dta[:, 3, :], ALU.max, ALU.add).then_inc(cols_v, 1)
            dve.wait_ge(cols_v, 2)
            link(v.tensor_scalar(dta[:, 0, :], dtT[:, 0:T], small[0:HEADS, 2:3], -1.0, ALU.mult, ALU.mult))
            link(v.memset(dta[:, 1, :], 1.0))
            v.tensor_tensor_scan(acsT[:, 0:T], dta[:, 1, :], dta[:, 0, :], 0.0, ALU.mult, ALU.add).then_inc(cols_v, 1)
            for h in range(GH):
                dve.wait_ge(dec_t, h + 1)
                v.tensor_scalar(ga[:, h * T:(h + 1) * T], bk[2 + h % 2][:, 0:T], par[:, 76 + h:77 + h], None, ALU.add).then_inc(dec_v, 1)
            dve.wait_ge(dec_v, 4)
            v.scalar_tensor_tensor(gb, ga, -1.0, ga, ALU.mult, ALU.max).then_inc(dec_v, 1)
            conv(10)
            conv(11)
            dve.wait_ge(dec_a, 2)
            dve.wait_ge(consts, 16)
            v.scalar_tensor_tensor(gc, ga, 0.0, gb, ALU.min, ALU.subtract).then_inc(dec_v, 1)
            dve.wait_ge(dec_v, 6)
            v.tensor_tensor_scan(ga, resets, gc, 0.0, ALU.mult, ALU.add).then_inc(dec_v, 1)
            conv(12)
            dve.wait_ge(dec_a, 4)
            g_chunks = ga.rearrange("p (c n) -> p c n", n=CH)
            ends = dec[:, :, :].rearrange("p h c -> p (h c)")
            v.tensor_copy(ends, g_chunks[:, :, CH - 1]).then_inc(dec_v, 1)
            dve.wait_ge(dec_v, 8)
            v.tensor_tensor(g_chunks, ends.unsqueeze(2).broadcast_to([P, GH * NCH, CH]), g_chunks, ALU.subtract).then_inc(dec_v, 1)
            conv(13)
            conv(14)
            dve.wait_ge(cols_t, 1)
            v.tensor_copy(keycols[:, :, :].rearrange("p a h -> p (a h)"), bk[6][:, 0:6 * HEADS]).then_inc(cols_v, 1)
            for g in range(2):
                dve.wait_ge(cb_t, g + 1)
                v.tensor_copy(cb[:, g, :], bk[4 + g][:, 0:PACK]).then_inc(cb_v, 1)
            for n in range(15, 20):
                conv(n)

            def xs_rows(g):
                t, half = g // 2, g % 2
                dve.wait_ge(xs_t, g + 1)
                v.tensor_tensor(dtx[:, t, half * 512:(half + 1) * 512].rearrange("p (h n) -> p h n", h=8),
                                bk[4 + g % 2][:, :].rearrange("p (h n) -> p h n", h=8),
                                keycols[:, 3 + t, 8 * half:8 * half + 8].unsqueeze(2).broadcast_to([P, 8, HD]),
                                ALU.mult).then_inc(xs_v, 1)

            def head_step(s):
                if s < HEADS:
                    dve.wait_ge(bc_t, s + 1)
                    if s == 0:
                        dve.wait_ge(cols_v, 4)
                    if s >= 2:
                        dve.wait_ge(m_v, s - 1)
                    for t in range(3):
                        cols, q = tile_queries(t)
                        v.scalar_tensor_tensor(seg[:, s % 2, cols], bk[2 + s % 2][:, q], keycols[:, t, s:s + 1],
                                               minmask[:, cols], ALU.subtract, ALU.min).then_inc(seg_v, 1)
                if 1 <= s <= HEADS:
                    h = s - 1
                    dve.wait_ge(exp_a, h + 1)
                    if h >= 2:
                        dve.wait_ge(y_t, h - 1)
                    v.tensor_tensor(mh[:, h % 2, :], seg[:, h % 2, :], cb[:, h // 8, :], ALU.mult).then_inc(m_v, 1)
                if s >= 2 and s % 2:
                    c = (s - 3) // 2
                    dve.wait_ge(y_t, 2 * c + 2)
                    v.scalar_tensor_tensor(mixed[:, c, :], xbc[:, c, META:], par[:, 82 + c:83 + c],
                                           bk[6 + c % 2][:, 0:SEQ], ALU.mult, ALU.add).then_inc(y_v, 1)

            def decayed_keys(j):
                b = j % 2
                if j >= 3:
                    dve.wait_ge(kx_t, j - 2)
                if j >= 2:
                    dve.wait_ge(kx_v, j - 1)
                    n = CH * (j - 1)
                    v.tensor_tensor(kx[:, b, :, 0:n], kx[:, 1 - b, :, 0:n],
                                    dec[:, :, j - 1:j].broadcast_to([P, GH, n]), ALU.mult)
                v.tensor_copy(kx[:, b, :, CH * (j - 1):CH * j], by_head(ga)[:, :, CH * (j - 1):CH * j])
                v.tensor_copy(kx[:, b, :, CH * j:CH * (j + 1)], by_head(gc)[:, :, CH * j:CH * (j + 1)]).then_inc(kx_v, 1)

            for n in range(QQ, NPJ):
                if QQ <= n < KK:
                    h = n - QQ
                    dve.wait_ge(pj_full, n + 1)
                    dve.wait_ge(dec_a, 6)
                    v.scalar_tensor_tensor(qd[:, h, :], bk[n % 2][:, 0:SEQ], float(P) ** -0.5, gb[:, h * T + META:(h + 1) * T],
                                           ALU.mult, ALU.mult).then_inc(pj_v, 1)
                if KK <= n < VV:
                    h = n - KK
                    dve.wait_ge(pj_full, n + 1)
                    v.tensor_tensor(gc[:, h * T:(h + 1) * T], bk[n % 2][:, 0:T], gc[:, h * T:(h + 1) * T], ALU.mult)
                    v.tensor_tensor(ga[:, h * T:(h + 1) * T], bk[n % 2][:, 0:T], ga[:, h * T:(h + 1) * T], ALU.mult).then_inc(pj_v, 1)
                if n in (20, 21):
                    for g in range(3 * (n - 20), 3 * (n - 19)):
                        xs_rows(g)
                for s in HEAD_STEPS.get(n, ()):
                    head_step(s)
                if n == ZZ:
                    dve.wait_ge(y_t, HEADS)
                    link(v.memset(reg_x[:, :], 0.0))
                if ZZ <= n < GG:
                    c = n - ZZ
                    dve.wait_ge(pj_a, freed(n, "A"))
                    v.tensor_tensor(mixed[:, c, :], mixed[:, c, :], tmp[:, n % 2, :], ALU.mult).then_inc(z_v, 1)
                for j in GLA_STEPS.get(n, ()):
                    decayed_keys(j)
                if n == 40:
                    dve.wait_ge(kx_t, NCH - 1)
                    for h, b in enumerate((2, 3, 6, 7)):
                        v.tensor_tensor(sc[:, h, :], bk[b][:, 0:PACK], causal[:, :], ALU.mult).then_inc(sc_v, 1)
                if n == 42:
                    dve.wait_ge(vt_t, 6)
                    v.memset(bgu, 0.0).then_inc(zeroed, 1)
                if n >= GG:
                    c = n - GG
                    dve.wait_ge(pj_a, freed(n, "A"))
                    dve.wait_ge(sq_g, 9 + c)
                    v.scalar_tensor_tensor(mixed[:, 8 + c, :], mixed[:, 8 + c, :], par[:, 80 + c % 2:81 + c % 2],
                                           tmp[:, n % 2, :], ALU.mult, ALU.mult).then_inc(z_v, 1)
                if n == GG + 5:
                    dve.wait_ge(ss_t, 16)
                    for i, (b, width) in enumerate(((4, 512), (6, 256), (7, 256))):
                        v.tensor_scalar(rstd[:, 2 * i:2 * i + 2, :].rearrange("p a n -> p (a n)"), bk[b][:, :], 1.0 / width, EPS,
                                        ALU.mult, ALU.add).then_inc(ms_v, 1)
            dve.wait_ge(ms_a, 1)
            link(v.reciprocal(rstd, rstd))
            for c in range(8):
                v.scalar_tensor_tensor(mixed[:, c, :], mixed[:, c, :], par[:, 68 + c:69 + c], rstd[:, c // 4, :],
                                       ALU.mult, ALU.mult).then_inc(mix_v, 1)
            dve.wait_ge(z_v, 16)
            for c in range(8):
                v.tensor_tensor(mixed[:, 8 + c, :], mixed[:, 8 + c, :], rstd[:, 2 + c // 2, :], ALU.mult).then_inc(mix_v, 1)
            dve.wait_ge(used, MIXED_USED)
            dve.wait_ge(x_again, 16)
            for t in range(2):
                for half in range(2):
                    o = x_rows[:, t, half * 512:(half + 1) * 512]
                    v.tensor_tensor(o, bk[4 + 2 * t + half][:, :], o, ALU.add).then_inc(h_v, 1)
            dve.wait_ge(ssx_a, 6)
            v.tensor_scalar(ssx[:, 2:4], ssx[:, 0:2], 1.0 / D, EPS, ALU.mult, ALU.add).then_inc(ssx_v, 1)
            dve.wait_ge(ssx_a, 7)
            link(v.reciprocal(ssx[:, 2:4], ssx[:, 2:4]))
            dve.wait_ge(ffnw_in, 16)
            for t in range(2):
                v.scalar_tensor_tensor(xn[:, t, :], x_rows[:, t, :], ssx[:, 2 + t:3 + t], ffnw, ALU.mult, ALU.mult).then_inc(xn_v, 1)
            dve.wait_ge(xt_t, 4)
            dve.wait_ge(xn_v, 2)
            for i in range(2):
                dve.wait_ge(part_a, i + 1)
                v.tensor_tensor(xn, xn, parts[:, i, :, :], ALU.subtract).then_inc(part_v, 1)
            dve.wait_ge(lg_t, 1)
            dve.wait_ge(router_in, 32)
            link(v.tensor_tensor(lg[:, :, :], bk[0][:, 0:2 * NE].rearrange("p (t n) -> p t n", t=2),
                                 br[:, :].unsqueeze(1).broadcast_to([P, 2, NE]), ALU.add))
            v.max(m8[:, 0, :], lg[:, 0, :]).then_inc(top_v, 1)
            v.max(m8[:, 1, :], lg[:, 1, :]).then_inc(top_v, 1)
            dve.wait_ge(top_v, 2)
            v.tensor_scalar(ssx[:, 4:6], m8[:, :, 0], -1.0, None, ALU.mult).then_inc(top_v, 1)
            v.max_index(i8[:, 0, :], m8[:, 0, :], lg[:, 0, :])
            link(v.max_index(i8[:, 1, :], m8[:, 1, :], lg[:, 1, :]))
            link(v.tensor_copy(i8f[:, :, :], i8[:, :, :]))
            dve.wait_ge(top_a, 2)
            link(v.tensor_reduce(ssx[:, 0:2], ge[:, :, :], AX_X, ALU.add))
            link(v.reciprocal(ssx[:, 0:2], ssx[:, 0:2]))
            link(v.tensor_tensor(ge[:, :, :], ge[:, :, :], ssx[:, 0:2].unsqueeze(2).broadcast_to([P, 2, TOPK]), ALU.mult))
            for i in range(TOPK):
                for t in range(2):
                    if i == 0:
                        v.tensor_scalar(chosen[:, t, :], expert_no[:, :], i8f[:, t, i:i + 1], None, ALU.is_equal)
                        link(v.tensor_scalar(gates[:, t, 0:NE], expert_no[:, :], i8f[:, t, i:i + 1], ge[:, t, i:i + 1],
                                             ALU.is_equal, ALU.mult))
                    else:
                        v.scalar_tensor_tensor(chosen[:, t, :], expert_no[:, :], i8f[:, t, i:i + 1], chosen[:, t, :],
                                               ALU.is_equal, ALU.add)
                        link(v.tensor_scalar(rt[:, t, :], expert_no[:, :], i8f[:, t, i:i + 1], ge[:, t, i:i + 1],
                                             ALU.is_equal, ALU.mult))
                        last = v.tensor_tensor(gates[:, t, 0:NE], gates[:, t, 0:NE], rt[:, t, :], ALU.add)
                        if (i, t) == (TOPK - 1, 1):
                            last.then_inc(sel_v, 1)
                        else:
                            link(last)
            dve.wait_ge(rank_t, 1)
            link(v.scalar_tensor_tensor(rt[:, :, :].rearrange("p t n -> p (t n)"), bk[1][:, 0:2 * NE], 1.0,
                                        chosen[:, :, :].rearrange("p t n -> p (t n)"), ALU.add, ALU.mult))
            v.tensor_scalar(rank[:, :, 0:NE], rt[:, :, :], -1.0, None, ALU.add).then_inc(table_v, 1)
            v.tensor_reduce(ssx[:, 0:1], bk[2][:, 0:NE], AX_X, ALU.max).then_inc(table_v, 1)
            dve.wait_ge(table_v, 2)
            v.tensor_copy(most[:, :], ssx[:, 0:1]).then_inc(table_v, 1)
            v.tensor_copy(gatesT[:, :], bk[3][0:NE, 0:SEQ]).then_inc(table_v, 1)

            def build_pick(expert, inc=True):
                for t in range(2):
                    last = v.tensor_scalar(pick[:, t, :], slot_no[:, 0, :], rank[:, t, bass.ds(expert, 1)], None, ALU.is_equal)
                last.then_inc(pick_v, 1)

            def sweep(p):
                if isinstance(p, int):
                    dve.wait_ge(table_v, MOST)
                else:
                    v.tensor_scalar(rank[:, :, :], rank[:, :, :], -float(SLOTS), None, ALU.add).then_inc(shift_v, 1)
                    dve.wait_ge(shift_v, p)
                    dve.wait_ge(gath_t, p * (NE + 1))
                build_pick(0)
                with dve.Fori(0, NE) as e:
                    dve.wait_ge(gu_t, e + (p * NE + 1))
                    v.tensor_copy(esel, ident[:, bass.ds(e, 1)].broadcast_to([P, SLOTS])).then_inc(esel_v, 1)
                    dve.wait_ge(pg_t, e + (p * NE + 1))
                    for t in range(2):
                        last = v.tensor_scalar(pg[:, t, :], slot_no[:, :, :].rearrange("p a s -> p (a s)"),
                                               rank[:, t, bass.ds(e, 1)], gates[:, t, bass.ds(e, 1)], ALU.is_equal, ALU.mult)
                    last.then_inc(pg_v, 1)
                    dve.wait_ge(gath_t, e + (p * (NE + 1) + 1))
                    build_pick(e + 1)
                    dve.wait_ge(gu_t, e + (p * NE + 2))
                    v.tensor_scalar(gateS, bk[0][:, :], LIMIT, None, ALU.min).then_inc(clip_v, 1)
                    v.tensor_scalar(upS, bk[1][:, :], LIMIT, -LIMIT, ALU.min, ALU.max).then_inc(clip_v, 1)
                    dve.wait_ge(clip_v, e * 3 + (p * NE * 3 + 2))
                    v.scalar_tensor_tensor(upS, upS, 1.0, gateS, ALU.add, ALU.mult).then_inc(clip_v, 1)
                    dve.wait_ge(clip_v, e * 3 + (p * NE * 3 + 3))
                    dve.wait_ge(sig_a, e + (p * NE + 1))
                    v.tensor_tensor(actS, upS, sigS, ALU.mult).then_inc(act_v, 1)
                    dve.wait_ge(at_t, e + (p * NE + 1))
                    v.tensor_copy(actT.rearrange("p j h s -> p (j h s)"), bk[3][:, :]).then_inc(at_v, 1)
                dve.wait_ge(comb_t, p * NE + NE)

            sweeps(dve, sweep, MOST)
            for t in range(2):
                for half in range(2):
                    o = x_rows[:, t, half * 512:(half + 1) * 512]
                    last = v.tensor_tensor(o, bk[4 + 2 * t + half][:, :], o, ALU.add)
            last.then_inc(fin_v, 1)
            dve.wait_ge(fin_a, 2)
            v.tensor_scalar(ssx[:, 2:4], ssx[:, 0:2], 1.0 / D, EPS, ALU.mult, ALU.add).then_inc(fin_v, 1)
            dve.wait_ge(fin_a, 3)
            link(v.reciprocal(ssx[:, 2:4], ssx[:, 2:4]))
            dve.wait_ge(late_in, 48)
            for t in range(2):
                v.scalar_tensor_tensor(xn[:, t, :], x_rows[:, t, :], ssx[:, 2 + t:3 + t], finw, ALU.mult, ALU.mult).then_inc(fin_v, 1)


_INS = ['x', 'meta_tokens', 'mix_norm_w', 'w_in', 'conv_w', 'conv_b', 'dt_bias', 'a_log', 'd_skip', 'ssd_norm_w',
        'w_decay_up', 'b_decay', 'gla_norm_w', 'w_out', 'ffn_norm_w', 'w_router', 'b_router', 'w_gate_up',
        'b_gate_up', 'w_down', 'b_down', 'final_norm_w']
_OUTS = [((1, SEQ, D), 'float32')]


def kernel(**inputs):
    import numpy as _np
    import concourse.bacc as _bacc
    from concourse import mybir as _mybir
    from concourse.bass_utils import run_bass_kernel_spmd as _run

    nc = _bacc.Bacc("TRN2", target_bir_lowering=False, num_devices=1)
    arrays, args = {}, []
    for name in _INS:
        a = _np.ascontiguousarray(inputs[name])
        arrays[f"in_{name}_dram"] = a
        args.append(nc.dram_tensor(f"in_{name}_dram", a.shape, _mybir.dt.from_np(a.dtype), kind="ExternalInput").ap())
    for i, (shape, dtype) in enumerate(_OUTS):
        dt = _mybir.dt.from_np(_np.dtype(dtype))
        args.append(nc.dram_tensor(f"out_{i}_dram", shape, dt, kind="ExternalOutput").ap())
    hybrid_moe_kernel(nc, *args)
    r = _run(nc, [arrays], core_ids=[0])
    got = tuple(r.results[0][f"out_{i}_dram"] for i in range(len(_OUTS)))
    return got[0]
```

```python
from contextlib import ExitStack

import concourse.bass as bass
from concourse import mybir

F32 = mybir.dt.float32
F32R = mybir.dt.float32r
BF16 = mybir.dt.bfloat16
I32 = mybir.dt.int32
U32 = mybir.dt.uint32
ALU = mybir.AluOpType
ACT = mybir.ActivationFunctionType
AX_X = mybir.AxisListType.X

P = 128
D = 1024
KC = D // P
META = 16
SEQ = 256
T = META + SEQ
EPS = 1e-5
HEADS = 16
HD = 64
XBC0 = D
DT0 = XBC0 + D + 512
Q0 = DT0 + HEADS
K0 = Q0 + 512
V0 = K0 + 512
G0 = V0 + D
ALR0 = G0 + D
RANK = 16
GH = 4
CH = 16
NCH = T // CH
TAU = 16.0
NE = 32
TOPK = 4
LIMIT = 7.0
ALPHA = 1.702
SLOTS = 64
SWEEPS = SEQ // SLOTS
RING = 6
MRING = RING - 2
SPLITS = 3
SLOT = 4096
CAUSAL = 1e30

TILES = [(0, 256, 0), (256, 144, 112), (400, 16, 240)]
PACK = 416

PANELS = [XBC0 + D, XBC0, XBC0 + 512, Q0, K0, V0, V0 + 512, 0, 512, G0, G0 + 512]
NP = len(PANELS)
MIX_FILLS = NP + 4
FIRST = 8
NPJ = FIRST + 4 * NP
OWNER = "R" * 6 + "V" + "A" + "V" * 12 + "V" * 8 + "A" * 8 + "A" * 16
B_C, XS, QQ, KK, VV, ZZ, GG = 8, 12, 20, 24, 28, 36, 44
HEAD_STEPS = {n: [n - 21] for n in range(21, 33)}
HEAD_STEPS.update({33: [12, 13], 34: [14, 15], 35: [16, 17]})
GLA_STEPS = {36 + i: range(1 + 4 * i, 5 + 4 * i) for i in range(4)}
RSTD_AT = ((2, 0), (2, 1), (3, 0), (3, 1), (0, 0), (0, 1))
OT_STEPS = {41: [0, 1], 42: [2, 3, 4], 43: [5, 6, 7]}


def freed(n, owner):
    return OWNER[:n + 1].count(owner)


def hybrid_moe_kernel(nc, x, meta, mix_w, w_in, conv_w, conv_b, dt_bias, a_log, d_skip, ssd_w, w_up,
                      b_decay, gla_w, w_out, ffn_w, w_router, b_router, w_gu, b_gu, w_dn, b_dn, fin_w, out):
    with ExitStack() as ctx:
        def sb(name, shape, dt=F32):
            return ctx.enter_context(nc.sbuf_tensor(name, shape, dt))

        def sem(name):
            return ctx.enter_context(nc.semaphore(name))

        def next_address():
            return -(-nc.sbuf_base // 32) * 32

        def over(name, shape, dt, address):
            return nc.alloc_sbuf_tensor_at(name, shape, dt, offset=address)

        ring = sb("ring", [P, MRING, SLOT])
        split_at = next_address()
        wh = sb("wh", [P, SPLITS, D], F32R)
        wl = sb("wl", [P, SPLITS, D], F32R)
        ul = sb("ul", [P, KC, T], F32R)
        last_slots = over("last_slots", [P, 2, SLOT], F32, split_at)
        ident = sb("ident", [P, P])
        ones = sb("ones", [P, P])
        minmask = sb("minmask", [P, PACK])
        slot_no = sb("slot_no", [P, 2, SLOTS])
        par = sb("par", [P, P])
        small = sb("small", [P, 64])
        acsT = sb("acsT", [HEADS, 384])
        keycols = sb("keycols", [P, 6, HEADS])
        dec = sb("dec", [P, GH, NCH])
        ssx = sb("ssx", [P, 8])
        one_col = sb("one_col", [P, 2 * GH - 1])
        one_row = sb("one_row", [GH, GH, P])
        rstd = sb("rstd", [GH, 2, SEQ])
        reg_x = sb("reg_x", [P, 3 * D])
        u_at = next_address()
        uh = sb("uh", [P, KC, T], F32R)
        xnT = over("xnT", [P, KC, SEQ], F32, u_at)
        c_at = next_address()
        reg_c = sb("reg_c", [P, 12 * T + P])
        wsm_parts = over("wsm_parts", [P, 2, 368], F32R, c_at)
        reg_v = sb("reg_v", [P, KC * T + P])
        reg_r = sb("reg_r", [P, 3 * D])
        reg_q = sb("reg_q", [P, GH * SEQ])
        reg_a = sb("reg_a", [P, 2 * GH * T])
        reg_s = sb("reg_s", [P, 6 * PACK])
        reg_m = sb("reg_m", [P, 16 * SEQ])
        tmp = sb("tmp", [P, 2, SEQ])
        sq = sb("sq", [P, 2, SEQ])

        par_rows = reg_v[:, 0:P]
        u_raw = reg_a[:, :].rearrange("p (k n) -> p k n", k=KC)
        wsm = reg_s[:, 4 * T:4 * T + 368]
        junk = reg_r[:, 0:D]
        headrow = reg_r[0:HEADS, D:3 * D].rearrange("p (h n) -> p h n", h=HEADS)
        resets = reg_s[:, 0:GH * T]
        dta = reg_m[0:HEADS, 0:4 * T].rearrange("p (a n) -> p a n", a=4)
        wup = reg_m[0:RANK, 4 * T:4 * T + 512]
        spread = reg_m[0:HEADS, 4 * T + 512:4 * T + 512 + D]
        dtT = reg_q[0:HEADS, 0:384]
        alr = reg_q[0:RANK, 384:384 + T]
        x_rows = reg_x[:, 0:2 * D].rearrange("p (t n) -> p t n", t=2)
        meta_rows = reg_x[0:META, 2 * D:3 * D]
        dtx = reg_x[:, :].rearrange("p (t n) -> p t n", t=3)
        kx = reg_x[:, :].rearrange("p (b h n) -> p b h n", b=2, h=GH)
        mh = uh[:, :, 0:SEQ]
        ml = ul[:, :, 0:SEQ]
        xbc = reg_c[:, 0:12 * T].rearrange("p (c n) -> p c n", c=12)
        vT = reg_v[:, 0:KC * T].rearrange("p (c n) -> p c n", c=KC)
        v_rows = reg_r[:, :].rearrange("p (t n) -> p t n", t=3)
        qd = reg_q[:, :].rearrange("p (h n) -> p h n", h=GH)
        ga = reg_a[:, 0:GH * T]
        gc = reg_a[:, GH * T:2 * GH * T]
        gb = reg_m[:, 8 * SEQ:8 * SEQ + GH * T] if GH * T <= 8 * SEQ else None
        seg = reg_s[:, 0:2 * PACK].rearrange("p (b n) -> p b n", b=2)
        hm = reg_s[:, 2 * PACK:4 * PACK].rearrange("p (b n) -> p b n", b=2)
        cb = reg_s[:, 4 * PACK:6 * PACK].rearrange("p (b n) -> p b n", b=2)
        sc = reg_s[:, 0:4 * PACK].rearrange("p (h n) -> p h n", h=GH)
        by_query = reg_s[:, 4 * PACK:4 * PACK + 6 * P].rearrange("p (b n) -> p b n", b=2)
        mixed = reg_m[:, :].rearrange("p (c n) -> p c n", c=16)

        def by_head(ap):
            return ap.rearrange("p (h n) -> p h n", h=GH)

        xn = reg_c[:, 0:2 * D].rearrange("p (t n) -> p t n", t=2)
        ffnw = reg_c[:, 2 * D:3 * D]
        bgu = reg_v[:, 0:2 * D]
        parts = reg_r[:, :].bitcast(BF16).rearrange("p (i t n) -> p i t n", i=3, t=2)
        bdn = reg_q[0:NE, 0:D]
        finw = reg_m[:, 0:D]
        gateS, sigS, upS, actS = (reg_a[:, i * 512:(i + 1) * 512] for i in range(4))
        xg = reg_s[:, 0:512].rearrange("p (k s) -> p k s", k=KC)
        actT = reg_s[:, 512:1024].rearrange("p (j h s) -> p j h s", j=4, h=2)
        yS = reg_s[:, 1024:1536]
        gT = reg_s[:, 1536:1792]
        pg = reg_s[:, 1792:2048].rearrange("p (t s) -> p t s", t=2)
        pick = reg_s[:, 2048:2112].bitcast(BF16).rearrange("p (t s) -> p t s", t=2)
        esel = reg_s[:, 2112:2176]
        wr = tmp[:, 0, :].rearrange("p (k n) -> p k n", k=KC)
        before = tmp[:, 1, 0:P]
        br = tmp[:, 1, P:P + NE]
        expert_no = sb("expert_no", [P, NE])
        sq_flat = sq[:, :, :].rearrange("p a n -> p (a n)")
        taken = [0]

        def router_tile(width):
            taken[0] += 2 * width
            return sq_flat[:, taken[0] - 2 * width:taken[0]].rearrange("p (t n) -> p t n", t=2)

        lg = router_tile(NE)
        m8 = router_tile(8)
        i8 = router_tile(8).bitcast(U32)
        i8f = router_tile(8)
        ge = router_tile(TOPK)
        chosen = router_tile(NE)
        gates = router_tile(NE + 1)
        rank = router_tile(NE + 1)
        rt = router_tile(NE)
        gatesT = reg_m[0:NE, D:D + SEQ]
        most = sb("most", [P, 1], I32)

        bk = [ctx.enter_context(nc.psum_tensor(f"bank{i}", [P, 512], F32)) for i in range(8)]

        x_in = sem("x_in")
        par_in = sem("par_in")
        small_in = sem("small_in")
        wsm_in = sem("wsm_in")
        ffnw_in = sem("ffnw_in")
        x_again = sem("x_again")
        late_in = sem("late_in")
        finw_in = sem("finw_in")
        cleared = sem("cleared")
        router_in = sem("router_in")
        filled = [sem(f"filled{i}") for i in range(RING)]
        used = sem("used")
        consts = sem("consts")
        before_g = sem("before_g")
        zeroed = sem("zeroed")
        v_link = sem("v_link")
        a_link = sem("a_link")
        ssx_a = sem("ssx_a")
        ssx_v = sem("ssx_v")
        x_norm = sem("x_norm")
        raw_v = sem("raw_v")
        high_a = sem("high_a")
        low_v = sem("low_v")
        wsm_a = sem("wsm_a")
        wsm_v = sem("wsm_v")
        wh_a = sem("wh_a")
        wl_v = sem("wl_v")
        wl_g = sem("wl_g")
        half_t = sem("half_t")
        mh_a = sem("mh_a")
        ml_g = sem("ml_g")
        wo_t = sem("wo_t")
        par_t = sem("par_t")
        pj_full = sem("pj_full")
        pj_v = sem("pj_v")
        pj_a = sem("pj_a")
        sp_v = sem("sp_v")
        sp_a = sem("sp_a")
        cols_v = sem("cols_v")
        cols_t = sem("cols_t")
        dec_t = sem("dec_t")
        dec_v = sem("dec_v")
        dec_a = sem("dec_a")
        conv_v = sem("conv_v")
        silu_a = sem("silu_a")
        cb_t = sem("cb_t")
        cb_v = sem("cb_v")
        xs_t = sem("xs_t")
        xs_v = sem("xs_v")
        bc_t = sem("bc_t")
        seg_v = sem("seg_v")
        exp_a = sem("exp_a")
        m_v = sem("m_v")
        y_t = sem("y_t")
        y_v = sem("y_v")
        qd_v = sem("qd_v")
        vt_t = sem("vt_t")
        vt_a = sem("vt_a")
        kx_v = sem("kx_v")
        kx_t = sem("kx_t")
        sc_v = sem("sc_v")
        o_t = sem("o_t")
        o_a = sem("o_a")
        z_v = sem("z_v")
        sq_g = sem("sq_g")
        ss_t = sem("ss_t")
        rec_v = sem("rec_v")
        rstd_t = sem("rstd_t")
        byq_a = sem("byq_a")
        turn_t = sem("turn_t")
        ms_v = sem("ms_v")
        ms_a = sem("ms_a")
        mix_v = sem("mix_v")
        h_v = sem("h_v")
        xn_v = sem("xn_v")
        xt_t = sem("xt_t")
        xt_a = sem("xt_a")
        part_a = sem("part_a")
        part_v = sem("part_v")
        lg_t = sem("lg_t")
        top_v = sem("top_v")
        top_a = sem("top_a")
        sel_v = sem("sel_v")
        rank_t = sem("rank_t")
        table_v = sem("table_v")
        pick_v = sem("pick_v")
        gath_t = sem("gath_t")
        xg_a = sem("xg_a")
        esel_v = sem("esel_v")
        gu_t = sem("gu_t")
        clip_v = sem("clip_v")
        sig_a = sem("sig_a")
        act_v = sem("act_v")
        pg_v = sem("pg_v")
        pg_t = sem("pg_t")
        gt_a = sem("gt_a")
        at_t = sem("at_t")
        at_v = sem("at_v")
        yd_t = sem("yd_t")
        ys_a = sem("ys_a")
        comb_t = sem("comb_t")
        shift_v = sem("shift_v")
        fin_v = sem("fin_v")
        fin_a = sem("fin_a")
        stored = sem("stored")

        def panel_halves(n):
            m = n - FIRST
            slot = ring[:, (m // 4) % MRING, :]
            if n < NPJ:
                w = slot.rearrange("p (k c) -> p k c", k=KC)[:, :, (m % 4) * P:(m % 4 + 1) * P]
                return w[:, 0:4, :], w[:, 4:8, :]
            w = slot[:, (m % 4) * D:(m % 4 + 1) * D]
            return w[:, 0:512].rearrange("p (k c) -> p k c", k=4), w[:, 512:D].rearrange("p (k c) -> p k c", k=4)

        def halves(t, b):
            return (t[:, b, 0:512].rearrange("p (k c) -> p k c", k=4), t[:, b, 512:D].rearrange("p (k c) -> p k c", k=4))

        def chunk_slot(i):
            if i >= MRING:
                return last_slots[:, i - MRING, :], filled[i], 16
            f = MIX_FILLS + i
            return ring[:, f % MRING, :], filled[f % MRING], 16 * (f // MRING + 1)

        def key_tiles(j):
            return [t for t in range(3) if (j - 1) * CH >= TILES[t][2]]

        def tile_queries(t):
            c0, n, q0 = TILES[t]
            return slice(c0, c0 + n), slice(q0, SEQ)

        def sweeps(eng, one_sweep, most_ready):
            one_sweep(0)
            eng.wait_ge(table_v, most_ready)
            count = eng.value_load(most[0:1, 0:1])
            with eng.If(count > SLOTS):
                with eng.Fori(1, SWEEPS) as p:
                    one_sweep(p)

        ALL_CONSTS = 14
        MOST = 4
        block = ctx.enter_context(nc.Block())

        @block.sync
        def _(sp):
            sp.dma_start(x_rows, x[0].rearrange("(t p) n -> p t n", p=P)).then_inc(x_in, 16)
            sp.dma_start(meta_rows, meta).then_inc(x_in, 16)
            sp.wait_ge(cleared, 1)
            small_cols = wsm[:, 0:KC * 32].rearrange("p (k n) -> p k n", k=KC)
            sp.dma_start(small_cols[:, :, 0:HEADS],
                         w_in[0, :, DT0:Q0].rearrange("(k p) n -> p k n", p=P)).then_inc(wsm_in, 16)
            sp.dma_start(small_cols[:, :, HEADS:],
                         w_in[0, :, ALR0:ALR0 + RANK].rearrange("(k p) n -> p k n", p=P)).then_inc(wsm_in, 16)
            sp.wait_ge(par_in, 6 * 16)
            sp.wait_ge(small_in, 4 * 16)
            for f in range(MIX_FILLS):
                if f >= MRING:
                    sp.wait_ge(pj_full, FIRST + 4 * (f - MRING + 1))
                if f < NP:
                    c = PANELS[f]
                    sp.dma_start(ring[:, f % MRING, :].rearrange("p (k n) -> p k n", k=KC),
                                 w_in[0, :, c:c + 512].rearrange("(k p) n -> p k n", p=P)).then_inc(filled[f % MRING], 16)
                else:
                    r = (f - NP) * 512
                    sp.dma_start(ring[:, f % MRING, :].rearrange("p (k n) -> p k n", k=4),
                                 w_out[0, r:r + 512, :].rearrange("(k p) n -> p k n", p=P)).then_inc(filled[f % MRING], 16)

            def sweep(p):
                with sp.Fori(0, NE) as e:
                    for i in range(RING):
                        slot, full, _ = chunk_slot(i)
                        sp.wait_ge(used, e * RING + (p * NE * RING + i + 1))
                        if i >= MRING and isinstance(p, int):
                            sp.wait_ge(wo_t, 16)
                        if i < 4:
                            src = w_gu[0, bass.ds(e, 1), i * 256:(i + 1) * 256, :].rearrange("o (k p) n -> p (o k) n", p=P)
                            dst = slot.rearrange("p (k n) -> p k n", k=2)
                        else:
                            src = w_dn[0, bass.ds(e, 1), (i - 4) * 512:(i - 3) * 512, :].rearrange("o (k p) n -> p (o k) n", p=P)
                            dst = slot.rearrange("p (k n) -> p k n", k=4)
                        sp.dma_start(dst, src).then_inc(full, 16)

            sweeps(sp, sweep, MOST)
            sp.wait_ge(fin_v, 4)
            sp.dma_start(out[0].rearrange("(t p) n -> p t n", p=P), xn).then_inc(stored, 16)
            sp.wait_ge(stored, 16)

        @block.gpsimd
        def _(pool):
            g = nc.gpsimd
            g.memset(ident[:, :], 0.0).then_inc(consts, 1)
            g.memset(ones[:, :], 1.0).then_inc(consts, 1)
            g.memset(par_rows[:, :], 0.0).then_inc(consts, 1)
            pool.wait_ge(consts, 3)
            g.affine_select(out=ident[:, :], in_=ident[:, :], compare_op=ALU.not_equal, fill=1.0, base=0,
                            pattern=[[-1, P]], channel_multiplier=1).then_inc(consts, 1)
            g.memset(minmask[:, :], 0.0).then_inc(consts, 1)
            g.memset(one_col[:, :], 0.0).then_inc(consts, 1)
            g.memset(resets, 1.0).then_inc(consts, 1)
            pool.wait_ge(consts, 7)
            g.memset(one_col[:, GH - 1:GH], 1.0).then_inc(consts, 1)
            for t, base in enumerate((META, 0, 0)):
                cols, _ = tile_queries(t)
                g.affine_select(out=minmask[:, cols], in_=minmask[:, cols], compare_op=ALU.is_ge, fill=-CAUSAL, base=base,
                                pattern=[[1, TILES[t][1]]], channel_multiplier=-1).then_inc(consts, 1)
            g.affine_select(out=resets.rearrange("p (c n) -> p c n", n=CH), in_=resets.rearrange("p (c n) -> p c n", n=CH),
                            compare_op=ALU.is_gt, fill=0.0, base=0, pattern=[[0, GH * NCH], [1, CH]],
                            channel_multiplier=0).then_inc(consts, 1)
            g.iota(slot_no[:, :, :], [[0, 2], [1, SLOTS]], base=0, channel_multiplier=0,
                   allow_small_or_imprecise_dtypes=True).then_inc(consts, 1)
            g.iota(expert_no[:, :], [[1, NE]], base=0, channel_multiplier=0,
                   allow_small_or_imprecise_dtypes=True).then_inc(consts, 1)

            def low_half(n):
                b = n % SPLITS
                pool.wait_ge(wh_a, 2 * (n - FIRST) + 2)
                if FIRST + SPLITS <= n < NPJ + SPLITS:
                    pool.wait_ge(pj_full, n - SPLITS + 1)
                if n >= NPJ + SPLITS:
                    pool.wait_ge(wo_t, n - NPJ - SPLITS + 1)
                g.tensor_tensor(halves(wl, b)[1], panel_halves(n)[1], halves(wh, b)[1].bitcast(F32), ALU.subtract).then_inc(wl_g, 1)

            for n in range(FIRST, NPJ + 16):
                low_half(n)
                c = n - ZZ - 1
                if 0 <= c < 8:
                    pool.wait_ge(z_v, c + 1)
                    if c >= 2:
                        pool.wait_ge(ss_t, c - 1)
                    g.tensor_tensor(sq[:, c % 2, :], mixed[:, c, :], mixed[:, c, :], ALU.mult).then_inc(sq_g, 1)
                if n == ZZ + 1:
                    pool.wait_ge(y_v, 8)
                    g.dma_start(ffnw, ffn_w.broadcast_to([P, D])).then_inc(ffnw_in, 16)
                if n == GG - 2:
                    pool.wait_ge(kx_t, NCH - 1)
                    g.dma_start(x_rows, x[0].rearrange("(t p) n -> p t n", p=P)).then_inc(x_again, 16)
                    g.dma_start(bdn, b_dn[0]).then_inc(late_in, 16)
                if n == GG:
                    pool.wait_ge(vt_t, 6)
                    pool.wait_ge(zeroed, 1)
                    g.dma_start(bgu[0:NE, :], b_gu[0]).then_inc(late_in, 16)
                if GG + 1 <= n < GG + 5:
                    for c in (2 * (n - GG - 1), 2 * (n - GG - 1) + 1):
                        pool.wait_ge(o_a, c + 1)
                        pool.wait_ge(ss_t, c + 7)
                        g.tensor_tensor(sq[:, c % 2, :], mixed[:, 8 + c, :], mixed[:, 8 + c, :], ALU.mult).then_inc(sq_g, 1)
                if n == NPJ:
                    pool.wait_ge(z_v, 16)
                    g.dma_start(wr, w_router[0].rearrange("(k p) n -> p k n", p=P)).then_inc(router_in, 16)
                    g.dma_start(br, b_router.broadcast_to([P, NE])).then_inc(router_in, 16)
                    g.memset(before, 1.0).then_inc(before_g, 1)
                    pool.wait_ge(before_g, 1)
                    g.affine_select(out=before, in_=before, compare_op=ALU.is_gt, fill=0.0, base=0,
                                    pattern=[[1, P]], channel_multiplier=-1).then_inc(before_g, 1)
                k = n - NPJ
                if k >= 0:
                    pool.wait_ge(mh_a, k + 1)
                    if k >= 8:
                        pool.wait_ge(wo_t, k - 7)
                    g.tensor_tensor(ml[:, k % 8, :], mixed[:, k, :], mh[:, k % 8, :].bitcast(F32), ALU.subtract).then_inc(ml_g, 1)
            pool.wait_ge(wo_t, 16)
            g.dma_start(finw, fin_w.unsqueeze(0).broadcast_to([P, D])).then_inc(finw_in, 16)

        @block.tensor
        def _(pe):
            mm = nc.tensor.matmul
            tr = nc.tensor.transpose

            pe.wait_ge(consts, 4)
            pe.wait_ge(par_in, 6 * 16)
            tr(bk[7][:, 0:P], par_rows[:, :], ident[:, :]).then_inc(par_t, 1)
            for n in range(6):
                t = n // 2
                pe.wait_ge(x_norm, t + 1)
                if n >= 2:
                    pe.wait_ge(raw_v, n - 1)
                for j in range(4):
                    c = (4 * (n % 2) + j) * P
                    if t == 0:
                        last = tr(bk[n % 2][:, j * P:j * P + META], meta_rows[:, c:c + P], ident[0:META, 0:META])
                    else:
                        last = tr(bk[n % 2][:, j * P:(j + 1) * P], x_rows[:, t - 1, c:c + P], ident[:, :])
                last.then_inc(pj_full, 1)

            def bank_free(n):
                owner = OWNER[n - 2]
                pe.wait_ge({"R": raw_v, "V": pj_v, "A": pj_a}[owner], freed(n - 2, owner))

            def split_mm(o, w_parts, u_parts, first, final, marks=()):
                (w0, w1), (u0, u1) = w_parts, u_parts
                for ins, mark in zip((mm(o, w0, u0, start=first, stop=False), mm(o, w0, u1, start=False, stop=False)), marks):
                    ins.then_inc(mark, 1)
                return mm(o, w1, u0, start=False, stop=final)

            pe.wait_ge(low_v, 6)
            pe.wait_ge(wsm_v, 1)
            for n in (6, 7):
                bank_free(n)
                for k in range(KC):
                    c = slice(32 * k + 16 * (n - 6), 32 * k + 16 * (n - 6) + P)
                    last = split_mm(bk[n % 2][:, 0:T], (wsm_parts[:, 0, c], wsm_parts[:, 1, c]), (uh[:, k, :], ul[:, k, :]),
                                    k == 0, k == KC - 1)
                last.then_inc(pj_full, 1)

            pe.wait_ge(cols_v, 1)
            pe.wait_ge(small_in, 64)
            for c in range(8):
                last = mm(bk[7][:, P + c:P + c + 1], spread[:, c * P:(c + 1) * P], small[0:HEADS, 3:4], start=True, stop=True)
            last.then_inc(par_t, 1)

            def decay_up():
                pe.wait_ge(pj_a, 1)
                pe.wait_ge(small_in, 64)
                for h in range(GH):
                    if h >= 2:
                        pe.wait_ge(dec_v, h - 1)
                    mm(bk[2 + h % 2][:, 0:T], wup[:, h * P:(h + 1) * P], alr, start=True, stop=True).then_inc(dec_t, 1)

            def key_columns():
                pe.wait_ge(cols_v, 3)
                for i, src in enumerate((acsT, dtT)):
                    for t in range(3):
                        last = tr(bk[6][:, (3 * i + t) * 16:(3 * i + t + 1) * 16], src[:, t * P:(t + 1) * P], ident[0:16, 0:16])
                last.then_inc(cols_t, 1)

            def c_times_b():
                pe.wait_ge(silu_a, 4)
                for g in range(2):
                    b0 = (8 + g) * T
                    for t in range(3):
                        cols, q = tile_queries(t)
                        last = mm(bk[4 + g][:, cols], reg_c[:, b0 + t * P:b0 + (t + 1) * P],
                                  xbc[:, 10 + g, META + q.start:], start=True, stop=True)
                    last.then_inc(cb_t, 1)

            def xs_rows(g):
                t, half = g // 2, g % 2
                if g == 0:
                    pe.wait_ge(silu_a, 12)
                    pe.wait_ge(cb_v, 2)
                if g >= 2:
                    pe.wait_ge(xs_v, g - 1)
                for j in range(4):
                    c = (4 * half + j) * T + t * P
                    last = tr(bk[4 + g % 2][:, j * P:(j + 1) * P], reg_c[:, c:c + P], ident[:, :])
                last.then_inc(xs_t, 1)

            def head_step(s):
                if s < HEADS:
                    if s >= 2:
                        pe.wait_ge(seg_v, 3 * (s - 1))
                    else:
                        pe.wait_ge(dec_v, GH)
                        pe.wait_ge(cols_v, 4)
                    mm(bk[2 + s % 2][:, 0:SEQ], headrow[:, s, :], acsT[:, META:T], start=True, stop=True).then_inc(bc_t, 1)
                if s >= 2:
                    h = s - 2
                    pe.wait_ge(m_v, h + 1)
                    if h % 2 == 0 and h >= 4:
                        pe.wait_ge(y_v, h // 2 - 1)
                    if h == 0:
                        pe.wait_ge(xs_v, 6)
                    r = HD * (h % 2)
                    for t in range(3):
                        cols, q = tile_queries(t)
                        last = mm(bk[6 + h // 2 % 2][r:r + HD, q], dtx[:, t, h * HD:(h + 1) * HD], hm[:, h % 2, cols],
                                  start=(t == 0), stop=(t == 2), skip_group_check=True)
                    last.then_inc(y_t, 1)

            def v_to_rows(g):
                t, half = g // 2, g % 2
                if g == 0:
                    pe.wait_ge(pj_a, freed(VV + 7, "A"))
                else:
                    pe.wait_ge(vt_a, g)
                for j in range(4):
                    c = (4 * half + j) * T + t * P
                    last = tr(bk[5][:, j * P:(j + 1) * P], reg_v[:, c:c + P], ident[:, :])
                last.then_inc(vt_t, 1)

            def gla_scores(j):
                pe.wait_ge(kx_v, j)
                if j == 1:
                    pe.wait_ge(y_v, 8)
                if j >= 3:
                    pe.wait_ge(byq_a, j - 2)
                for h in range(GH):
                    q0 = h * SEQ + (j - 1) * CH
                    m = min(32, GH * SEQ - q0)
                    last = mm(bk[2 + j % 2][32 * h:32 * h + m, 0:(j + 1) * CH], reg_q[:, q0:q0 + m],
                              kx[:, j % 2, h, 0:(j + 1) * CH], start=True, stop=True)
                last.then_inc(kx_t, 1)

            def turn_scores(j):
                pe.wait_ge(byq_a, j)
                if j >= 3:
                    pe.wait_ge(sc_v, j - 2)
                for t in key_tiles(j):
                    last = tr(bk[6 + j % 2][:, t * P:(t + 1) * P], by_query[:, j % 2, t * P:(t + 1) * P], ident[:, :])
                last.then_inc(turn_t, 1)

            def gla_out(i):
                h = i // 2
                pe.wait_ge(sc_v, NCH - 1)
                if i == 0:
                    pe.wait_ge(vt_a, 6)
                if i >= 2:
                    pe.wait_ge(o_a, i - 1)
                for t in range(3):
                    cols, q = tile_queries(t)
                    last = mm(bk[2 + i % 2][:, q], v_rows[:, t, i * P:(i + 1) * P], sc[:, h, cols],
                              start=(t == 0), stop=(t == 2), skip_group_check=True)
                last.then_inc(o_t, 1)

            def sum_squares(c):
                pe.wait_ge(sq_g, c + 1)
                if c == 0:
                    pe.wait_ge(xs_v, 6)
                    pe.wait_ge(consts, ALL_CONSTS)
                row, b = (c // 4, 4) if c < 8 else ((c - 8) // 2, 6)
                mm(bk[b][0:GH, 0:SEQ], one_col[:, GH - 1 - row:2 * GH - 1 - row], sq[:, c % 2, :],
                   start=(c % 8 == 0), stop=(c % 8 == 7)).then_inc(ss_t, 1)

            def spread_rstd():
                pe.wait_ge(o_a, 8)
                bank_free(NPJ)
                for i, (b, half) in enumerate(RSTD_AT):
                    kind, row = (0, i) if i < 2 else (1, i - 2)
                    pe.wait_ge(rec_v, kind + 1)
                    mm(bk[b][:, half * SEQ:(half + 1) * SEQ], one_row[:, row, :], rstd[:, kind, :],
                       start=True, stop=True).then_inc(rstd_t, 1)

            for n in range(FIRST, NPJ):
                m = n - FIRST
                bank_free(n)
                t0 = 0 if n < QQ or KK <= n < ZZ else META
                for half, low in ((0, wl_v), (1, wl_g)):
                    pe.wait_ge(low, m + 1)
                    for k in range(4):
                        u = 4 * half + k
                        last = split_mm(bk[n % 2][:, 0:T - t0], (halves(wh, n % SPLITS)[half][:, k, :], halves(wl, n % SPLITS)[half][:, k, :]),
                                        (uh[:, u, t0:], ul[:, u, t0:]), u == 0, u == KC - 1)
                        if k % 2 and n in GLA_STEPS:
                            j = GLA_STEPS[n][2 * half + k // 2]
                            gla_scores(j)
                            if j > 1:
                                turn_scores(j - 1)
                            if j == NCH - 1:
                                turn_scores(j)
                    last.then_inc((half_t, pj_full)[half], 1)
                if n == 12:
                    decay_up()
                if n == 14:
                    key_columns()
                if n == 18:
                    c_times_b()
                if n in (20, 21):
                    for g in range(3 * (n - 20), 3 * (n - 19)):
                        xs_rows(g)
                for s in HEAD_STEPS.get(n, ()):
                    head_step(s)
                if ZZ <= n < ZZ + 6:
                    v_to_rows(n - ZZ)
                if ZZ + 2 <= n < ZZ + 8:
                    sum_squares(n - ZZ - 2)
                for i in OT_STEPS.get(n, ()):
                    gla_out(i)
                if n in (GG, GG + 1):
                    sum_squares(6 + n - GG)
                if GG + 2 <= n < GG + 6:
                    sum_squares(8 + 2 * (n - GG - 2))
                    sum_squares(9 + 2 * (n - GG - 2))
            spread_rstd()

            for k in range(16):
                n = NPJ + k
                b = n % SPLITS
                pe.wait_ge(ml_g, k + 1)
                for half, low in ((0, wl_v), (1, wl_g)):
                    pe.wait_ge(low, n - FIRST + 1)
                    cols = slice(half * 512, (half + 1) * 512)
                    for t in range(2):
                        toks = slice(t * P, (t + 1) * P)
                        last = split_mm(bk[4 + 2 * t + half][:, :], (mh[:, k % 8, toks], ml[:, k % 8, toks]),
                                        (wh[:, b, cols], wl[:, b, cols]), k == 0, k == 15,
                                        (used, used) if (k, half, t) == (15, 1, 1) else ())
                        if half and t == 0 and k in (3, 7, 11, 15):
                            last.then_inc(used, 1)
                    last.then_inc((half_t, wo_t)[half], 1)

            for i in range(4):
                t, half = i // 2, i % 2
                pe.wait_ge(xn_v, t + 1)
                for j in range(4):
                    c = (4 * half + j) * P
                    last = tr(bk[i][:, j * P:(j + 1) * P], xn[:, t, c:c + P], ident[:, :])
                last.then_inc(xt_t, 1)
            pe.wait_ge(xt_a, 4)
            pe.wait_ge(router_in, 32)
            for t in range(2):
                for k in range(KC):
                    last = mm(bk[0][:, t * NE:(t + 1) * NE], xnT[:, k, t * P:(t + 1) * P], wr[:, k, :],
                              start=(k == 0), stop=(k == KC - 1))
            last.then_inc(lg_t, 1)
            pe.wait_ge(sel_v, 1)
            pe.wait_ge(before_g, 2)
            mm(bk[1][:, 0:NE], before[:, :], chosen[:, 0, :], start=True, stop=True)
            mm(bk[1][:, NE:2 * NE], ones[:, :], chosen[:, 0, :], start=True, stop=False)
            mm(bk[1][:, NE:2 * NE], before[:, :], chosen[:, 1, :], start=False, stop=True)
            mm(bk[2][:, 0:NE], ones[:, :], chosen[:, 0, :], start=True, stop=False)
            mm(bk[2][:, 0:NE], ones[:, :], chosen[:, 1, :], start=False, stop=True)
            tr(bk[3][0:NE, 0:P], gates[:, 0, 0:NE], ident[:, :])
            tr(bk[3][0:NE, P:2 * P], gates[:, 1, 0:NE], ident[:, :]).then_inc(rank_t, 1)
            pe.wait_ge(table_v, MOST)
            pe.wait_ge(h_v, 4)
            pe.wait_ge(late_in, 2 * 16)
            for t in range(2):
                for half in range(2):
                    last = mm(bk[4 + 2 * t + half][:, :], gatesT[:, t * P:(t + 1) * P], bdn[:, half * 512:(half + 1) * 512],
                              start=True, stop=False, skip_group_check=True)
                    if t == 0:
                        last.then_inc((gu_t, pg_t)[half], 1)

            def gather(count):
                pe.wait_ge(pick_v, count)
                for k in range(KC):
                    for t in range(2):
                        for i in range(3):
                            last = mm(bk[3][:, k * SLOTS:(k + 1) * SLOTS], parts[:, i, t, k * P:(k + 1) * P], pick[:, t, :],
                                      start=(t == 0 and i == 0), stop=(t == 1 and i == 2))
                last.then_inc(gath_t, 1)

            def sweep(p):
                if isinstance(p, int):
                    pe.wait_ge(part_a, 3)
                gather(p * (NE + 1) + 1)
                with pe.Fori(0, NE) as e:
                    pe.wait_ge(xg_a, e + (p * (NE + 1) + 1))
                    for i in range(4):
                        slot, full, first_fill = chunk_slot(i)
                        pe.wait_ge(full, e * 16 + (p * NE * 16 + first_fill))
                        w = slot.rearrange("p (k n) -> p k n", k=2)
                        for kk in range(2):
                            k = 2 * i + kk
                            for up in range(2):
                                for half in range(2):
                                    last = mm(bk[up][half * SLOTS:(half + 1) * SLOTS, :], xg[:, k, :],
                                              w[:, kk, up * D + half * 512:up * D + (half + 1) * 512],
                                              start=(k == 0), stop=False, skip_group_check=True)
                        last.then_inc(used, 1)
                    pe.wait_ge(esel_v, e + (p * NE + 1))
                    for up in range(2):
                        for half in range(2):
                            last = mm(bk[up][half * SLOTS:(half + 1) * SLOTS, :], esel[:, :],
                                      bgu[:, up * D + half * 512:up * D + (half + 1) * 512],
                                      start=False, stop=True, skip_group_check=True)
                    last.then_inc(gu_t, 1)
                    pe.wait_ge(pg_v, e + (p * NE + 1))
                    for t in range(2):
                        last = tr(bk[2][:, t * P:(t + 1) * P], pg[:, t, :], ident[:, :])
                    last.then_inc(pg_t, 1)
                    gather(e + (p * (NE + 1) + 2))
                    pe.wait_ge(act_v, e + (p * NE + 1))
                    pe.wait_ge(xg_a, e + (p * (NE + 1) + 2))
                    for j in range(4):
                        last = tr(bk[3][:, j * P:(j + 1) * P], actS[:, j * P:(j + 1) * P], ident[:, :])
                    last.then_inc(at_t, 1)
                    pe.wait_ge(at_v, e + (p * NE + 1))
                    pe.wait_ge(gt_a, e + (p * NE + 1))
                    for i in range(4, 6):
                        slot, full, first_fill = chunk_slot(i)
                        pe.wait_ge(full, e * 16 + (p * NE * 16 + first_fill))
                        w = slot.rearrange("p (k n) -> p k n", k=4)
                        for j in range(4):
                            for half in range(2):
                                last = mm(bk[2][half * SLOTS:(half + 1) * SLOTS, :], actT[:, j, i - 4, :],
                                          w[:, j, half * 512:(half + 1) * 512],
                                          start=(i == 4 and j == 0), stop=(i == 5 and j == 3), skip_group_check=True)
                        last.then_inc(used if i == 4 else yd_t, 1)
                    pe.wait_ge(ys_a, e + (p * NE + 1))
                    for t in range(2):
                        for half in range(2):
                            r = half * SLOTS
                            last = mm(bk[4 + 2 * t + half][:, :], gT[r:r + SLOTS, t * P:(t + 1) * P], yS[r:r + SLOTS, :],
                                      start=False, stop=False, skip_group_check=True)
                            if t == half == 0:
                                last.then_inc(used, 1)
                    last.then_inc(comb_t, 1)

            sweeps(pe, sweep, MOST)

        @block.scalar
        def _(act):
            a = nc.scalar

            def copy(out, in_):
                return a.activation(out, in_, ACT.Copy)

            act.wait_ge(consts, 3)
            r = 0
            for src, n in ((mix_w.rearrange("a (c p) -> (a c) p", p=P), 8),
                           (conv_w.rearrange("a t (c p) -> (a t c) p", p=P), 48),
                           (conv_b.rearrange("a (c p) -> (a c) p", p=P), 12),
                           (ssd_w.rearrange("a (c p) -> (a c) p", p=P), 8),
                           (b_decay.rearrange("a (c p) -> (a c) p", p=P), 4),
                           (gla_w.rearrange("a (c p) -> (a c) p", p=P), 2)):
                act.dma_start(par_rows[r:r + n, :], src).then_inc(par_in, 16)
                r += n
            act.dma_start(small[0:HEADS, 0:1], dt_bias.rearrange("a h -> h a")).then_inc(small_in, 16)
            act.dma_start(small[0:HEADS, 1:2], a_log.rearrange("a h -> h a")).then_inc(small_in, 16)
            act.dma_start(small[0:HEADS, 3:4], d_skip.rearrange("a h -> h a")).then_inc(small_in, 16)
            act.dma_start(wup, w_up[0]).then_inc(small_in, 16)
            act.wait_ge(x_in, 32)
            act.wait_ge(cleared, 1)
            a.activation(junk[0:META, :], meta_rows, ACT.Square, accum_out=ssx[0:META, 0:1]).then_inc(ssx_a, 1)
            for t in range(2):
                act.wait_ge(ssx_a, t + 1)
                a.activation(junk, x_rows[:, t, :], ACT.Square, accum_out=ssx[:, 1 + t:2 + t]).then_inc(ssx_a, 1)
            act.wait_ge(ssx_v, 1)
            a.activation(ssx[:, 3:6], ssx[:, 3:6], ACT.Sqrt).then_inc(ssx_a, 1)
            act.wait_ge(small_in, 64)
            a.activation(small[0:HEADS, 2:3], small[0:HEADS, 1:2], ACT.Exp).then_inc(sp_a, 1)
            for n in range(6):
                act.wait_ge(raw_v, n + 1)
                w = META if n < 2 else P
                c = 0 if n < 2 else META + (n // 2 - 1) * P
                copy(uh[:, 4 * (n % 2):4 * (n % 2) + 4, c:c + w], u_raw[:, 4 * (n % 2):4 * (n % 2) + 4, c:c + w]).then_inc(high_a, 1)
                if n == 1:
                    act.wait_ge(wsm_in, 32)
                    copy(wsm_parts[:, 0, :], wsm).then_inc(wsm_a, 1)

            def high_halves(n):
                m = n - FIRST
                if m % 4 == 0:
                    act.wait_ge(filled[m // 4 % MRING], 16 * (m // 4 // MRING + 1))
                for half in range(2):
                    if m >= SPLITS:
                        if half == 0:
                            act.wait_ge(half_t, m - SPLITS + 1)
                        elif n - SPLITS < NPJ:
                            act.wait_ge(pj_full, n - SPLITS + 1)
                        else:
                            act.wait_ge(wo_t, n - SPLITS - NPJ + 1)
                    copy(halves(wh, n % SPLITS)[half], panel_halves(n)[half]).then_inc(wh_a, 1)

            high_halves(FIRST)
            high_halves(FIRST + 1)
            act.wait_ge(pj_full, 8)
            copy(alr, bk[1][0:RANK, 0:T]).then_inc(pj_a, 1)
            high_halves(FIRST + 2)
            act.wait_ge(sp_v, 1)
            a.activation(dta[:, 1, :], dta[:, 1, :], ACT.Exp, scale=-1.0).then_inc(sp_a, 1)
            act.wait_ge(sp_v, 2)
            a.activation(dta[:, 3, :], dta[:, 2, :], ACT.Ln).then_inc(sp_a, 1)
            for n in range(FIRST + 3, FIRST + 7):
                high_halves(n)
            act.wait_ge(dec_v, 5)
            a.activation(gb, gb, ACT.Exp, scale=-1.0).then_inc(dec_a, 1)
            act.wait_ge(dec_a, 1)
            a.activation(gb, gb, ACT.Ln, bias=1.0).then_inc(dec_a, 1)
            high_halves(FIRST + 7)
            act.wait_ge(dec_v, 7)
            a.activation(gb, ga, ACT.Exp, scale=1.0 / TAU).then_inc(dec_a, 1)
            a.activation(gc, ga, ACT.Exp, scale=-1.0 / TAU).then_inc(dec_a, 1)
            high_halves(FIRST + 8)
            high_halves(FIRST + 9)
            act.wait_ge(dec_v, 9)
            a.activation(ga, ga, ACT.Exp, scale=1.0 / TAU).then_inc(dec_a, 1)
            a.activation(dec[:, :, :], dec[:, :, :], ACT.Exp, scale=1.0 / TAU).then_inc(dec_a, 1)
            for i in range(12):
                if i in (4, 7, 10):
                    high_halves(FIRST + 9 + (i - 1) // 3)
                c = (8 + i) % 12
                act.wait_ge(conv_v, i + 1)
                a.activation(xbc[:, c, :], xbc[:, c, :], ACT.Silu).then_inc(silu_a, 1)
            high_halves(QQ + 1)
            for n in range(QQ, NPJ):
                high_halves(n + 2)
                for j in GLA_STEPS.get(n, ()):
                    act.wait_ge(kx_t, j)
                    if j >= 3:
                        act.wait_ge(turn_t, j - 2)
                    copy(by_query[:, j % 2, 0:(j + 1) * CH], bk[2 + j % 2][:, 0:(j + 1) * CH]).then_inc(byq_a, 1)
                if VV <= n < ZZ:
                    act.wait_ge(pj_full, n + 1)
                    copy(vT[:, n - VV, :], bk[n % 2][:, 0:T]).then_inc(pj_a, 1)
                for s in HEAD_STEPS.get(n, ()):
                    if s < HEADS:
                        act.wait_ge(seg_v, 3 * (s + 1))
                        a.activation(seg[:, s % 2, :], seg[:, s % 2, :], ACT.Exp).then_inc(exp_a, 1)
                if n >= ZZ:
                    act.wait_ge(pj_full, n + 1)
                    if n >= ZZ + 2:
                        act.wait_ge(z_v, n - ZZ - 1)
                    a.activation(tmp[:, n % 2, :], bk[n % 2][:, 0:SEQ], ACT.Silu).then_inc(pj_a, 1)
                if ZZ <= n < ZZ + 6:
                    g = n - ZZ
                    act.wait_ge(vt_t, g + 1)
                    copy(v_rows[:, g // 2, (g % 2) * 512:(g % 2 + 1) * 512], bk[5][:, :]).then_inc(vt_a, 1)
                for i in OT_STEPS.get(n, ()):
                    act.wait_ge(o_t, i + 1)
                    copy(mixed[:, 8 + i, :], bk[2 + i % 2][:, 0:SEQ]).then_inc(o_a, 1)
                if n == GG + 5:
                    for i in range(2):
                        act.wait_ge(ms_v, i + 1)
                        a.activation(rstd[:, i, :], rstd[:, i, :], ACT.Sqrt).then_inc(ms_a, 1)
            for k in range(16):
                act.wait_ge(mix_v, k + 1)
                if k >= 8:
                    act.wait_ge(wo_t, k - 7)
                copy(mh[:, k % 8, :], mixed[:, k, :]).then_inc(mh_a, 1)
                if k < 14:
                    high_halves(NPJ + k + 2)
            spare = reg_m[:, 8 * SEQ:8 * SEQ + D]
            act.wait_ge(h_v, 4)
            for t in range(2):
                a.activation(spare, x_rows[:, t, :], ACT.Square, accum_out=ssx[:, t:t + 1]).then_inc(ssx_a, 1)
                act.wait_ge(ssx_a, 5 + t)
            act.wait_ge(ssx_v, 2)
            a.activation(ssx[:, 2:4], ssx[:, 2:4], ACT.Sqrt).then_inc(ssx_a, 1)
            for i in range(4):
                act.wait_ge(xt_t, i + 1)
                copy(xnT[:, 4 * (i % 2):4 * (i % 2) + 4, (i // 2) * P:(i // 2 + 1) * P],
                     bk[i][:, :].rearrange("p (k n) -> p k n", k=4)).then_inc(xt_a, 1)
            copy(parts[:, 0, :, :], xn).then_inc(part_a, 1)
            act.wait_ge(part_v, 1)
            copy(parts[:, 1, :, :], xn).then_inc(part_a, 1)
            act.wait_ge(part_v, 2)
            copy(parts[:, 2, :, :], xn).then_inc(part_a, 1)
            act.wait_ge(top_v, 3)
            for t in range(2):
                a.activation(ge[:, t, :], m8[:, t, 0:TOPK], ACT.Exp, bias=ssx[:, 4 + t:5 + t]).then_inc(top_a, 1)

            def sweep(p):
                act.wait_ge(gath_t, p * (NE + 1) + 1)
                copy(xg, bk[3][:, :].rearrange("p (k s) -> p k s", k=KC)).then_inc(xg_a, 1)
                with act.Fori(0, NE) as e:
                    act.wait_ge(clip_v, e * 3 + (p * NE * 3 + 1))
                    a.activation(sigS, gateS, ACT.Sigmoid, scale=ALPHA).then_inc(sig_a, 1)
                    act.wait_ge(pg_t, e + (p * NE + 2))
                    copy(gT, bk[2][:, 0:2 * P]).then_inc(gt_a, 1)
                    act.wait_ge(gath_t, e + (p * (NE + 1) + 2))
                    copy(xg, bk[3][:, :].rearrange("p (k s) -> p k s", k=KC)).then_inc(xg_a, 1)
                    act.wait_ge(yd_t, e + (p * NE + 1))
                    copy(yS, bk[2][:, :]).then_inc(ys_a, 1)

            sweeps(act, sweep, MOST)
            act.wait_ge(fin_v, 1)
            for t in range(2):
                a.activation(spare, x_rows[:, t, :], ACT.Square, accum_out=ssx[:, t:t + 1]).then_inc(fin_a, 1)
                act.wait_ge(fin_a, 1 + t)
            act.wait_ge(fin_v, 2)
            a.activation(ssx[:, 2:4], ssx[:, 2:4], ACT.Sqrt).then_inc(fin_a, 1)

        @block.vector
        def _(dve):
            v = nc.vector
            links = [0]

            def link(ins):
                links[0] += 1
                ins.then_inc(v_link, 1)
                dve.wait_ge(v_link, links[0])

            v.memset(ssx[:, :], 1.0)
            v.memset(dtT, 0.0)
            v.memset(acsT[:, :], 0.0)
            link(v.memset(reg_v[:, KC * T:], 0.0))
            link(v.memset(wsm[:, KC * 32:], 0.0))
            v.memset(dta[:, 1, :], 1.0).then_inc(cleared, 1)
            dve.wait_ge(par_t, 1)
            link(v.tensor_copy(par[:, :], bk[7][:, 0:P]))
            dve.wait_ge(ssx_a, 3)
            v.tensor_scalar(ssx[:, 3:6], ssx[:, 0:3], 1.0 / D, EPS, ALU.mult, ALU.add).then_inc(ssx_v, 1)
            dve.wait_ge(ssx_a, 4)
            link(v.reciprocal(ssx[:, 3:6], ssx[:, 3:6]))
            v.tensor_scalar(meta_rows, meta_rows, ssx[0:META, 3:4], None, ALU.mult).then_inc(x_norm, 1)
            for t in range(2):
                v.tensor_scalar(x_rows[:, t, :], x_rows[:, t, :], ssx[:, 4 + t:5 + t], None, ALU.mult).then_inc(x_norm, 1)
            dve.wait_ge(consts, 4)
            v.tensor_copy(spread.rearrange("p (h n) -> p h n", h=HEADS),
                          ident[0:HEADS, 0:HEADS].unsqueeze(2).broadcast_to([HEADS, HEADS, HD]))
            v.tensor_copy(one_row[:, :, :], ident[0:GH, 0:GH].unsqueeze(2).broadcast_to([GH, GH, P]))
            v.tensor_copy(headrow[:, :, :], ident[0:HEADS, 0:HEADS].unsqueeze(2).broadcast_to([HEADS, HEADS, P])).then_inc(cols_v, 1)
            def low_u(n):
                k0, c, w = 4 * (n % 2), 0 if n < 2 else META + (n // 2 - 1) * P, META if n < 2 else P
                dve.wait_ge(high_a, n + 1)
                v.tensor_tensor(ul[:, k0:k0 + 4, c:c + w], u_raw[:, k0:k0 + 4, c:c + w],
                                uh[:, k0:k0 + 4, c:c + w].bitcast(F32), ALU.subtract).then_inc(low_v, 1)

            def low_half(n):
                m, b = n - FIRST, n % SPLITS
                dve.wait_ge(wh_a, 2 * m + 1)
                if m >= SPLITS:
                    dve.wait_ge(half_t, m - SPLITS + 1)
                v.tensor_tensor(halves(wl, b)[0], panel_halves(n)[0], halves(wh, b)[0].bitcast(F32), ALU.subtract).then_inc(wl_v, 1)

            for n in range(6):
                t, k0 = n // 2, 4 * (n % 2)
                w = META if t == 0 else P
                c = 0 if t == 0 else META + (t - 1) * P
                dve.wait_ge(pj_full, n + 1)
                v.tensor_tensor(u_raw[:, k0:k0 + 4, c:c + w], bk[n % 2][:, :].rearrange("p (k n) -> p k n", k=4)[:, :, 0:w],
                                par[:, k0:k0 + 4].unsqueeze(2).broadcast_to([P, 4, w]), ALU.mult).then_inc(raw_v, 1)
                if n >= 1:
                    low_u(n - 1)
                if n == 2:
                    dve.wait_ge(wsm_a, 1)
                    v.tensor_tensor(wsm_parts[:, 1, :], wsm, wsm_parts[:, 0, :].bitcast(F32), ALU.subtract).then_inc(wsm_v, 1)
            low_u(5)
            low_half(FIRST)
            low_half(FIRST + 1)
            dve.wait_ge(pj_full, 7)
            dve.wait_ge(small_in, 64)
            v.tensor_scalar(dta[:, 0, :], bk[0][0:HEADS, 0:T], small[0:HEADS, 0:1], None, ALU.add).then_inc(pj_v, 1)
            dve.wait_ge(pj_v, 1)
            v.scalar_tensor_tensor(dta[:, 1, :], dta[:, 0, :], -1.0, dta[:, 0, :], ALU.mult, ALU.max).then_inc(sp_v, 1)

            dve.wait_ge(par_t, 2)
            link(v.tensor_copy(par[:, 82:90], bk[7][:, P:P + 8]))

            def conv(n):
                low_half(n + 1) if n > FIRST else None
                c = n - B_C + 8 if n < XS else n - XS
                bank, o = bk[n % 2], xbc[:, c, :]
                dve.wait_ge(pj_full, n + 1)
                link(v.tensor_scalar(o, bank[:, 0:T], par[:, 8 + 36 + c:9 + 36 + c], par[:, 56 + c:57 + c], ALU.mult, ALU.add))
                for back in (1, 2):
                    tap = 8 + 12 * (3 - back) + c
                    link(v.scalar_tensor_tensor(o[:, back:], bank[:, 0:T - back], par[:, tap:tap + 1], o[:, back:],
                                                ALU.mult, ALU.add))
                v.scalar_tensor_tensor(o[:, 3:], bank[:, 0:T - 3], par[:, 8 + c:9 + c], o[:, 3:],
                                       ALU.mult, ALU.add).then_inc(pj_v, 1)
                dve.wait_ge(pj_v, freed(n, "V"))
                v.tensor_copy(ssx[0:1, 7:8], ssx[0:1, 6:7]).then_inc(conv_v, 1)

            for n in (8, 9):
                conv(n)
            dve.wait_ge(sp_a, 2)
            v.tensor_scalar(dta[:, 2, :], dta[:, 1, :], 1.0, None, ALU.add).then_inc(sp_v, 1)
            conv(10)
            dve.wait_ge(sp_a, 3)
            link(v.scalar_tensor_tensor(dta[:, 1, :], dta[:, 2, :], -1.0, dta[:, 1, :], ALU.add, ALU.subtract))
            link(v.reciprocal(dta[:, 2, :], dta[:, 2, :]))
            link(v.tensor_tensor(dta[:, 1, :], dta[:, 1, :], dta[:, 2, :], ALU.mult))
            link(v.tensor_tensor(dta[:, 3, :], dta[:, 3, :], dta[:, 1, :], ALU.subtract))
            v.scalar_tensor_tensor(dtT[:, 0:T], dta[:, 0, :], 0.0, dta[:, 3, :], ALU.max, ALU.add).then_inc(cols_v, 1)
            conv(11)
            dve.wait_ge(cols_v, 2)
            link(v.tensor_scalar(dta[:, 0, :], dtT[:, 0:T], small[0:HEADS, 2:3], -1.0, ALU.mult, ALU.mult))
            link(v.memset(dta[:, 1, :], 1.0))
            v.tensor_tensor_scan(acsT[:, 0:T], dta[:, 1, :], dta[:, 0, :], 0.0, ALU.mult, ALU.add).then_inc(cols_v, 1)
            conv(12)
            for h in range(GH):
                dve.wait_ge(dec_t, h + 1)
                v.tensor_scalar(ga[:, h * T:(h + 1) * T], bk[2 + h % 2][:, 0:T], par[:, 76 + h:77 + h], None, ALU.add).then_inc(dec_v, 1)
            dve.wait_ge(dec_v, 4)
            v.scalar_tensor_tensor(gb, ga, -1.0, ga, ALU.mult, ALU.max).then_inc(dec_v, 1)
            conv(13)
            dve.wait_ge(dec_a, 2)
            dve.wait_ge(consts, ALL_CONSTS)
            v.scalar_tensor_tensor(gc, ga, 0.0, gb, ALU.min, ALU.subtract).then_inc(dec_v, 1)
            dve.wait_ge(dec_v, 6)
            v.tensor_tensor_scan(ga, resets, gc, 0.0, ALU.mult, ALU.add).then_inc(dec_v, 1)
            conv(14)
            dve.wait_ge(cols_t, 1)
            v.tensor_copy(keycols[:, :, :].rearrange("p a h -> p (a h)"), bk[6][:, 0:6 * HEADS]).then_inc(cols_v, 1)
            conv(15)
            dve.wait_ge(dec_a, 4)
            g_chunks = ga.rearrange("p (c n) -> p c n", n=CH)
            ends = dec[:, :, :].rearrange("p h c -> p (h c)")
            v.tensor_copy(ends, g_chunks[:, :, CH - 1]).then_inc(dec_v, 1)
            dve.wait_ge(dec_v, 8)
            v.tensor_tensor(g_chunks, ends.unsqueeze(2).broadcast_to([P, GH * NCH, CH]), g_chunks, ALU.subtract).then_inc(dec_v, 1)
            for n in (16, 17, 18):
                conv(n)
            for g in range(2):
                dve.wait_ge(cb_t, g + 1)
                v.tensor_copy(cb[:, g, :], bk[4 + g][:, 0:PACK]).then_inc(cb_v, 1)
            conv(19)
            low_half(QQ + 1)

            def xs_rows(g):
                t, half = g // 2, g % 2
                dve.wait_ge(xs_t, g + 1)
                v.tensor_tensor(dtx[:, t, half * 512:(half + 1) * 512].rearrange("p (h n) -> p h n", h=8),
                                bk[4 + g % 2][:, :].rearrange("p (h n) -> p h n", h=8),
                                keycols[:, 3 + t, 8 * half:8 * half + 8].unsqueeze(2).broadcast_to([P, 8, HD]),
                                ALU.mult).then_inc(xs_v, 1)

            def head_step(s):
                if s < HEADS:
                    dve.wait_ge(bc_t, s + 1)
                    if s == 0:
                        dve.wait_ge(cols_v, 4)
                    if s >= 2:
                        dve.wait_ge(m_v, s - 1)
                    for t in range(3):
                        cols, q = tile_queries(t)
                        v.scalar_tensor_tensor(seg[:, s % 2, cols], bk[2 + s % 2][:, q], keycols[:, t, s:s + 1],
                                               minmask[:, cols], ALU.subtract, ALU.min).then_inc(seg_v, 1)
                if 1 <= s <= HEADS:
                    h = s - 1
                    dve.wait_ge(exp_a, h + 1)
                    if h >= 2:
                        dve.wait_ge(y_t, h - 1)
                    v.tensor_tensor(hm[:, h % 2, :], seg[:, h % 2, :], cb[:, h // 8, :], ALU.mult).then_inc(m_v, 1)
                if s >= 2 and s % 2:
                    c = (s - 3) // 2
                    dve.wait_ge(y_t, 2 * c + 2)
                    v.scalar_tensor_tensor(mixed[:, c, :], xbc[:, c, META:], par[:, 82 + c:83 + c],
                                           bk[6 + c % 2][:, 0:SEQ], ALU.mult, ALU.add).then_inc(y_v, 1)

            def decayed_keys(j):
                b = j % 2
                if j >= 3:
                    dve.wait_ge(kx_t, j - 2)
                if j >= 2:
                    dve.wait_ge(kx_v, j - 1)
                    n = CH * (j - 1)
                    v.tensor_tensor(kx[:, b, :, 0:n], kx[:, 1 - b, :, 0:n],
                                    dec[:, :, j - 1:j].broadcast_to([P, GH, n]), ALU.mult)
                v.tensor_copy(kx[:, b, :, CH * (j - 1):CH * j], by_head(ga)[:, :, CH * (j - 1):CH * j])
                v.tensor_copy(kx[:, b, :, CH * j:CH * (j + 1)], by_head(gc)[:, :, CH * j:CH * (j + 1)]).then_inc(kx_v, 1)

            def causal_scores(j):
                dve.wait_ge(turn_t, j)
                for t in key_tiles(j):
                    c = TILES[t][0] + (j - 1) * CH - TILES[t][2]
                    last = v.scalar_tensor_tensor(sc[:, :, c:c + CH], minmask[:, c:c + CH].unsqueeze(1).broadcast_to([P, GH, CH]), 0.0,
                                                  bk[6 + j % 2][:, t * P:(t + 1) * P].rearrange("p (h n) -> p h n", h=GH)[:, :, 0:CH],
                                                  ALU.is_ge, ALU.mult)
                last.then_inc(sc_v, 1)

            for n in range(QQ, NPJ):
                low_half(n + 2)
                if QQ <= n < KK:
                    h = n - QQ
                    dve.wait_ge(pj_full, n + 1)
                    dve.wait_ge(dec_a, 6)
                    v.scalar_tensor_tensor(qd[:, h, :], bk[n % 2][:, 0:SEQ], float(P) ** -0.5, gb[:, h * T + META:(h + 1) * T],
                                           ALU.mult, ALU.mult).then_inc(pj_v, 1)
                if KK <= n < VV:
                    h = n - KK
                    dve.wait_ge(pj_full, n + 1)
                    v.tensor_tensor(gc[:, h * T:(h + 1) * T], bk[n % 2][:, 0:T], gc[:, h * T:(h + 1) * T], ALU.mult)
                    v.tensor_tensor(ga[:, h * T:(h + 1) * T], bk[n % 2][:, 0:T], ga[:, h * T:(h + 1) * T], ALU.mult).then_inc(pj_v, 1)
                if n in (20, 21):
                    for g in range(3 * (n - 20), 3 * (n - 19)):
                        xs_rows(g)
                for s in HEAD_STEPS.get(n, ()):
                    head_step(s)
                if n == ZZ:
                    dve.wait_ge(y_t, HEADS)
                for j in GLA_STEPS.get(n, ()):
                    decayed_keys(j)
                    if j > 2:
                        causal_scores(j - 2)
                if n == 40:
                    causal_scores(NCH - 2)
                    causal_scores(NCH - 1)
                if ZZ <= n < GG:
                    c = n - ZZ
                    dve.wait_ge(pj_a, freed(n, "A"))
                    v.tensor_tensor(mixed[:, c, :], mixed[:, c, :], tmp[:, n % 2, :], ALU.mult).then_inc(z_v, 1)
                if n == 42:
                    dve.wait_ge(vt_t, 6)
                    v.memset(bgu, 0.0).then_inc(zeroed, 1)
                if n == GG + 6:
                    for i in range(2):
                        dve.wait_ge(ms_a, i + 1)
                        v.reciprocal(rstd[:, i, :], rstd[:, i, :]).then_inc(rec_v, 1)
                if n >= GG:
                    c = n - GG
                    dve.wait_ge(pj_a, freed(n, "A"))
                    dve.wait_ge(sq_g, 9 + c)
                    v.scalar_tensor_tensor(mixed[:, 8 + c, :], mixed[:, 8 + c, :], par[:, 80 + c % 2:81 + c % 2],
                                           tmp[:, n % 2, :], ALU.mult, ALU.mult).then_inc(z_v, 1)
                if n == GG + 5:
                    dve.wait_ge(ss_t, 16)
                    for i, (b, width) in enumerate(((4, 512), (6, 256))):
                        v.tensor_scalar(rstd[:, i, :], bk[b][0:GH, 0:SEQ], 1.0 / width, EPS,
                                        ALU.mult, ALU.add).then_inc(ms_v, 1)
            for c in range(16):
                i = c // 4 if c < 8 else c // 2 - 2
                b, half = RSTD_AT[i]
                dve.wait_ge(rstd_t, (i | 1) + 1)
                r = bk[b][:, half * SEQ:(half + 1) * SEQ]
                if c < 8:
                    v.scalar_tensor_tensor(mixed[:, c, :], mixed[:, c, :], par[:, 68 + c:69 + c], r,
                                           ALU.mult, ALU.mult).then_inc(mix_v, 1)
                else:
                    if c == 8:
                        dve.wait_ge(z_v, 16)
                    v.tensor_tensor(mixed[:, c, :], mixed[:, c, :], r, ALU.mult).then_inc(mix_v, 1)
                if c >= 2:
                    low_half(NPJ + c)
            dve.wait_ge(ss_t, 16)
            v.memset(rank[:, :, :], -1.0)
            link(v.memset(gates[:, :, :], 0.0))
            dve.wait_ge(wo_t, 16)
            dve.wait_ge(x_again, 16)
            for t in range(2):
                for half in range(2):
                    o = x_rows[:, t, half * 512:(half + 1) * 512]
                    v.tensor_tensor(o, bk[4 + 2 * t + half][:, :], o, ALU.add).then_inc(h_v, 1)
            dve.wait_ge(ssx_a, 6)
            v.tensor_scalar(ssx[:, 2:4], ssx[:, 0:2], 1.0 / D, EPS, ALU.mult, ALU.add).then_inc(ssx_v, 1)
            dve.wait_ge(ssx_a, 7)
            link(v.reciprocal(ssx[:, 2:4], ssx[:, 2:4]))
            dve.wait_ge(ffnw_in, 16)
            for t in range(2):
                v.scalar_tensor_tensor(xn[:, t, :], x_rows[:, t, :], ssx[:, 2 + t:3 + t], ffnw, ALU.mult, ALU.mult).then_inc(xn_v, 1)
            dve.wait_ge(xt_t, 4)
            dve.wait_ge(xn_v, 2)
            for i in range(2):
                dve.wait_ge(part_a, i + 1)
                v.tensor_tensor(xn, xn, parts[:, i, :, :], ALU.subtract).then_inc(part_v, 1)
            dve.wait_ge(lg_t, 1)
            dve.wait_ge(router_in, 32)
            link(v.tensor_tensor(lg[:, :, :], bk[0][:, 0:2 * NE].rearrange("p (t n) -> p t n", t=2),
                                 br[:, :].unsqueeze(1).broadcast_to([P, 2, NE]), ALU.add))
            v.max(m8[:, 0, :], lg[:, 0, :]).then_inc(top_v, 1)
            v.max(m8[:, 1, :], lg[:, 1, :]).then_inc(top_v, 1)
            dve.wait_ge(top_v, 2)
            v.tensor_scalar(ssx[:, 4:6], m8[:, :, 0], -1.0, None, ALU.mult).then_inc(top_v, 1)
            v.max_index(i8[:, 0, :], m8[:, 0, :], lg[:, 0, :])
            link(v.max_index(i8[:, 1, :], m8[:, 1, :], lg[:, 1, :]))
            link(v.tensor_copy(i8f[:, :, :], i8[:, :, :]))
            dve.wait_ge(top_a, 2)
            link(v.tensor_reduce(ssx[:, 0:2], ge[:, :, :], AX_X, ALU.add))
            link(v.reciprocal(ssx[:, 0:2], ssx[:, 0:2]))
            link(v.tensor_tensor(ge[:, :, :], ge[:, :, :], ssx[:, 0:2].unsqueeze(2).broadcast_to([P, 2, TOPK]), ALU.mult))
            for i in range(TOPK):
                for t in range(2):
                    if i == 0:
                        v.tensor_scalar(chosen[:, t, :], expert_no[:, :], i8f[:, t, i:i + 1], None, ALU.is_equal)
                        link(v.tensor_scalar(gates[:, t, 0:NE], expert_no[:, :], i8f[:, t, i:i + 1], ge[:, t, i:i + 1],
                                             ALU.is_equal, ALU.mult))
                    else:
                        v.scalar_tensor_tensor(chosen[:, t, :], expert_no[:, :], i8f[:, t, i:i + 1], chosen[:, t, :],
                                               ALU.is_equal, ALU.add)
                        link(v.tensor_scalar(rt[:, t, :], expert_no[:, :], i8f[:, t, i:i + 1], ge[:, t, i:i + 1],
                                             ALU.is_equal, ALU.mult))
                        last = v.tensor_tensor(gates[:, t, 0:NE], gates[:, t, 0:NE], rt[:, t, :], ALU.add)
                        if (i, t) == (TOPK - 1, 1):
                            last.then_inc(sel_v, 1)
                        else:
                            link(last)
            dve.wait_ge(rank_t, 1)
            link(v.scalar_tensor_tensor(rt[:, :, :].rearrange("p t n -> p (t n)"), bk[1][:, 0:2 * NE], 1.0,
                                        chosen[:, :, :].rearrange("p t n -> p (t n)"), ALU.add, ALU.mult))
            v.tensor_scalar(rank[:, :, 0:NE], rt[:, :, :], -1.0, None, ALU.add).then_inc(table_v, 1)
            v.tensor_reduce(ssx[:, 0:1], bk[2][:, 0:NE], AX_X, ALU.max).then_inc(table_v, 1)
            dve.wait_ge(table_v, 2)
            v.tensor_copy(most[:, :], ssx[:, 0:1]).then_inc(table_v, 1)
            v.tensor_copy(gatesT[:, :], bk[3][0:NE, 0:SEQ]).then_inc(table_v, 1)

            def build_pick(expert, inc=True):
                for t in range(2):
                    last = v.tensor_scalar(pick[:, t, :], slot_no[:, 0, :], rank[:, t, bass.ds(expert, 1)], None, ALU.is_equal)
                last.then_inc(pick_v, 1)

            def sweep(p):
                if isinstance(p, int):
                    dve.wait_ge(table_v, MOST)
                else:
                    v.tensor_scalar(rank[:, :, :], rank[:, :, :], -float(SLOTS), None, ALU.add).then_inc(shift_v, 1)
                    dve.wait_ge(shift_v, p)
                    dve.wait_ge(gath_t, p * (NE + 1))
                build_pick(0)
                with dve.Fori(0, NE) as e:
                    dve.wait_ge(gu_t, e + (p * NE + 1))
                    v.tensor_copy(esel, ident[:, bass.ds(e, 1)].broadcast_to([P, SLOTS])).then_inc(esel_v, 1)
                    dve.wait_ge(pg_t, e + (p * NE + 1))
                    for t in range(2):
                        last = v.tensor_scalar(pg[:, t, :], slot_no[:, :, :].rearrange("p a s -> p (a s)"),
                                               rank[:, t, bass.ds(e, 1)], gates[:, t, bass.ds(e, 1)], ALU.is_equal, ALU.mult)
                    last.then_inc(pg_v, 1)
                    dve.wait_ge(gath_t, e + (p * (NE + 1) + 1))
                    build_pick(e + 1)
                    dve.wait_ge(gu_t, e + (p * NE + 2))
                    v.tensor_scalar(gateS, bk[0][:, :], LIMIT, None, ALU.min).then_inc(clip_v, 1)
                    v.tensor_scalar(upS, bk[1][:, :], LIMIT, -LIMIT, ALU.min, ALU.max).then_inc(clip_v, 1)
                    dve.wait_ge(clip_v, e * 3 + (p * NE * 3 + 2))
                    v.scalar_tensor_tensor(upS, upS, 1.0, gateS, ALU.add, ALU.mult).then_inc(clip_v, 1)
                    dve.wait_ge(clip_v, e * 3 + (p * NE * 3 + 3))
                    dve.wait_ge(sig_a, e + (p * NE + 1))
                    v.tensor_tensor(actS, upS, sigS, ALU.mult).then_inc(act_v, 1)
                    dve.wait_ge(at_t, e + (p * NE + 1))
                    v.tensor_copy(actT.rearrange("p j h s -> p (j h s)"), bk[3][:, :]).then_inc(at_v, 1)
                dve.wait_ge(comb_t, p * NE + NE)

            sweeps(dve, sweep, MOST)
            for t in range(2):
                for half in range(2):
                    o = x_rows[:, t, half * 512:(half + 1) * 512]
                    last = v.tensor_tensor(o, bk[4 + 2 * t + half][:, :], o, ALU.add)
            last.then_inc(fin_v, 1)
            dve.wait_ge(fin_a, 2)
            v.tensor_scalar(ssx[:, 2:4], ssx[:, 0:2], 1.0 / D, EPS, ALU.mult, ALU.add).then_inc(fin_v, 1)
            dve.wait_ge(fin_a, 3)
            link(v.reciprocal(ssx[:, 2:4], ssx[:, 2:4]))
            dve.wait_ge(finw_in, 16)
            for t in range(2):
                v.scalar_tensor_tensor(xn[:, t, :], x_rows[:, t, :], ssx[:, 2 + t:3 + t], finw, ALU.mult, ALU.mult).then_inc(fin_v, 1)


_INS = ['x', 'meta_tokens', 'mix_norm_w', 'w_in', 'conv_w', 'conv_b', 'dt_bias', 'a_log', 'd_skip', 'ssd_norm_w',
        'w_decay_up', 'b_decay', 'gla_norm_w', 'w_out', 'ffn_norm_w', 'w_router', 'b_router', 'w_gate_up',
        'b_gate_up', 'w_down', 'b_down', 'final_norm_w']
_OUTS = [((1, SEQ, D), 'float32')]


def kernel(**inputs):
    import numpy as _np
    import concourse.bacc as _bacc
    from concourse import mybir as _mybir
    from concourse.bass_utils import run_bass_kernel_spmd as _run

    nc = _bacc.Bacc("TRN2", target_bir_lowering=False, num_devices=1)
    arrays, args = {}, []
    for name in _INS:
        a = _np.ascontiguousarray(inputs[name])
        arrays[f"in_{name}_dram"] = a
        args.append(nc.dram_tensor(f"in_{name}_dram", a.shape, _mybir.dt.from_np(a.dtype), kind="ExternalInput").ap())
    for i, (shape, dtype) in enumerate(_OUTS):
        dt = _mybir.dt.from_np(_np.dtype(dtype))
        args.append(nc.dram_tensor(f"out_{i}_dram", shape, dt, kind="ExternalOutput").ap())
    hybrid_moe_kernel(nc, *args)
    r = _run(nc, [arrays], core_ids=[0])
    got = tuple(r.results[0][f"out_{i}_dram"] for i in range(len(_OUTS)))
    return got[0]
```

```python
from contextlib import ExitStack

import concourse.bass as bass
from concourse import mybir

F32 = mybir.dt.float32
F32R = mybir.dt.float32r
BF16 = mybir.dt.bfloat16
I32 = mybir.dt.int32
U32 = mybir.dt.uint32
ALU = mybir.AluOpType
ACT = mybir.ActivationFunctionType
AX_X = mybir.AxisListType.X

P = 128
D = 1024
KC = D // P
META = 16
SEQ = 256
T = META + SEQ
EPS = 1e-5
HEADS = 16
HD = 64
XBC0 = D
DT0 = XBC0 + D + 512
Q0 = DT0 + HEADS
K0 = Q0 + 512
V0 = K0 + 512
G0 = V0 + D
ALR0 = G0 + D
RANK = 16
GH = 4
CH = 16
NCH = T // CH
TAU = 16.0
NE = 32
TOPK = 4
LIMIT = 7.0
ALPHA = 1.702
SLOTS = 64
SWEEPS = SEQ // SLOTS
RING = 6
MRING = RING - 2
SPLITS = 3
SLOT = 4096
CAUSAL = 1e30

TILES = [(0, 256, 0), (256, 144, 112), (400, 16, 240)]
PACK = 416

PANELS = [XBC0 + D, XBC0, XBC0 + 512, Q0, K0, V0, V0 + 512, 0, 512, G0, G0 + 512]
NP = len(PANELS)
MIX_FILLS = NP + 4
FIRST = 8
NPJ = FIRST + 4 * NP
OWNER = "R" * 6 + "V" + "A" + "V" * 12 + "V" * 8 + "A" * 8 + "A" * 16
B_C, XS, QQ, KK, VV, ZZ, GG = 8, 12, 20, 24, 28, 36, 44
HEAD_STEPS = {n: [n - 21] for n in range(21, 33)}
HEAD_STEPS.update({33: [12, 13], 34: [14, 15], 35: [16, 17, 18]})
GLA_STEPS = {36 + i: range(1 + 4 * i, 5 + 4 * i) for i in range(4)}
RSTD_AT = ((2, 0), (2, 1), (3, 0), (3, 1), (0, 0), (0, 1))
OT_STEPS = {41: [0, 1], 42: [2, 3, 4], 43: [5, 6, 7]}


def freed(n, owner):
    return OWNER[:n + 1].count(owner)


def hybrid_moe_kernel(nc, x, meta, mix_w, w_in, conv_w, conv_b, dt_bias, a_log, d_skip, ssd_w, w_up,
                      b_decay, gla_w, w_out, ffn_w, w_router, b_router, w_gu, b_gu, w_dn, b_dn, fin_w, out):
    with ExitStack() as ctx:
        def sb(name, shape, dt=F32):
            return ctx.enter_context(nc.sbuf_tensor(name, shape, dt))

        def sem(name):
            return ctx.enter_context(nc.semaphore(name))

        def next_address():
            return -(-nc.sbuf_base // 32) * 32

        def over(name, shape, dt, address):
            return nc.alloc_sbuf_tensor_at(name, shape, dt, offset=address)

        ring = sb("ring", [P, MRING, SLOT])
        split_at = next_address()
        wh = sb("wh", [P, SPLITS, D], F32R)
        wl = sb("wl", [P, SPLITS, D], F32R)
        ul = sb("ul", [P, KC, T], F32R)
        last_slots = over("last_slots", [P, 2, SLOT], F32, split_at)
        ident = sb("ident", [P, P])
        ones = sb("ones", [P, P])
        minmask = sb("minmask", [P, PACK])
        slot_no = sb("slot_no", [P, 2, SLOTS])
        par = sb("par", [P, P])
        small = sb("small", [P, 64])
        acsT = sb("acsT", [HEADS, 384])
        keycols = sb("keycols", [P, 6, HEADS])
        dec = sb("dec", [P, GH, NCH])
        ssx = sb("ssx", [P, 8])
        one_col = sb("one_col", [P, 2 * GH - 1])
        one_row = sb("one_row", [GH, GH, P])
        rstd = sb("rstd", [GH, 2, SEQ])
        sq_gla = sb("sq_gla", [P, 2, SEQ])
        reg_x = sb("reg_x", [P, 3 * D])
        u_at = next_address()
        uh = sb("uh", [P, KC, T], F32R)
        xnT = over("xnT", [P, KC, SEQ], F32, u_at)
        c_at = next_address()
        reg_c = sb("reg_c", [P, 12 * T + P])
        wsm_parts = over("wsm_parts", [P, 2, 368], F32R, c_at)
        reg_v = sb("reg_v", [P, KC * T + P])
        reg_r = sb("reg_r", [P, 3 * D])
        reg_q = sb("reg_q", [P, GH * SEQ])
        reg_a = sb("reg_a", [P, 2 * GH * T])
        reg_s = sb("reg_s", [P, 6 * PACK])
        reg_m = sb("reg_m", [P, 16 * SEQ])
        tmp = sb("tmp", [P, 2, SEQ])
        sq = sb("sq", [P, 2, SEQ])

        par_rows = reg_v[:, 0:P]
        u_raw = reg_a[:, :].rearrange("p (k n) -> p k n", k=KC)
        wsm = reg_s[:, 4 * T:4 * T + 368]
        junk = reg_r[:, 0:D]
        headrow = reg_r[0:HEADS, D:3 * D].rearrange("p (h n) -> p h n", h=HEADS)
        resets = reg_s[:, 0:GH * T]
        dta = reg_m[0:HEADS, 0:4 * T].rearrange("p (a n) -> p a n", a=4)
        wup = reg_m[0:RANK, 4 * T:4 * T + 512]
        spread = reg_m[0:HEADS, 4 * T + 512:4 * T + 512 + D]
        dtT = reg_q[0:HEADS, 0:384]
        alr = reg_q[0:RANK, 384:384 + T]
        x_rows = reg_x[:, 0:2 * D].rearrange("p (t n) -> p t n", t=2)
        meta_rows = reg_x[0:META, 2 * D:3 * D]
        dtx = reg_x[:, :].rearrange("p (t n) -> p t n", t=3)
        kx = reg_x[:, :].rearrange("p (b h n) -> p b h n", b=2, h=GH)
        mh = uh[:, :, 0:SEQ]
        ml = ul[:, :, 0:SEQ]
        xbc = reg_c[:, 0:12 * T].rearrange("p (c n) -> p c n", c=12)
        vT = reg_v[:, 0:KC * T].rearrange("p (c n) -> p c n", c=KC)
        v_rows = reg_r[:, :].rearrange("p (t n) -> p t n", t=3)
        qd = reg_q[:, :].rearrange("p (h n) -> p h n", h=GH)
        ga = reg_a[:, 0:GH * T]
        gc = reg_a[:, GH * T:2 * GH * T]
        gb = reg_m[:, 8 * SEQ:8 * SEQ + GH * T] if GH * T <= 8 * SEQ else None
        seg = reg_s[:, 0:2 * PACK].rearrange("p (b n) -> p b n", b=2)
        hm = [reg_s[:, 2 * PACK:3 * PACK], reg_s[:, 3 * PACK:4 * PACK],
              tmp[:, :, :].rearrange("p a n -> p (a n)")[:, 0:PACK], sq[:, :, :].rearrange("p a n -> p (a n)")[:, 0:PACK]]
        cb = reg_s[:, 4 * PACK:6 * PACK].rearrange("p (b n) -> p b n", b=2)
        sc = reg_s[:, 0:4 * PACK].rearrange("p (h n) -> p h n", h=GH)
        by_query = reg_s[:, 4 * PACK:4 * PACK + 6 * P].rearrange("p (b n) -> p b n", b=2)
        mixed = reg_m[:, :].rearrange("p (c n) -> p c n", c=16)

        def by_head(ap):
            return ap.rearrange("p (h n) -> p h n", h=GH)

        xn = reg_c[:, 0:2 * D].rearrange("p (t n) -> p t n", t=2)
        ffnw = reg_c[:, 2 * D:3 * D]
        bgu = reg_v[:, 0:2 * D]
        parts = reg_r[:, :].bitcast(BF16).rearrange("p (i t n) -> p i t n", i=3, t=2)
        resid = reg_m[:, 2 * D:4 * D].rearrange("p (t n) -> p t n", t=2)
        is_choice = reg_a[:, 0:2 * TOPK * NE].rearrange("p (c n) -> p c n", n=NE)
        gate_of = reg_a[:, 2 * TOPK * NE:4 * TOPK * NE].rearrange("p (c n) -> p c n", n=NE)
        bdn = reg_q[:, 0:512]
        finw = reg_m[:, 0:D]
        gateS, sigS, upS, actS = (reg_a[:, i * 512:(i + 1) * 512] for i in range(4))
        xg = reg_s[:, 0:512].rearrange("p (k s) -> p k s", k=KC)
        actT = reg_s[:, 512:1024].rearrange("p (j h s) -> p j h s", j=4, h=2)
        yS = reg_s[:, 1024:1536]
        gT = reg_s[:, 1536:1792]
        pg = reg_s[:, 1792:2048].rearrange("p (t s) -> p t s", t=2)
        pick = reg_s[:, 2048:2112].bitcast(BF16).rearrange("p (t s) -> p t s", t=2)
        esel = reg_s[:, 2112:2176]
        wr = tmp[:, 0, :].rearrange("p (k n) -> p k n", k=KC)
        before = tmp[:, 1, 0:P]
        br = tmp[:, 1, P:P + NE]
        expert_no = sb("expert_no", [P, NE])
        sq_flat = sq[:, :, :].rearrange("p a n -> p (a n)")
        taken = [0]

        def router_tile(width):
            taken[0] += 2 * width
            return sq_flat[:, taken[0] - 2 * width:taken[0]].rearrange("p (t n) -> p t n", t=2)

        lg = router_tile(NE)
        m8 = router_tile(8)
        i8 = router_tile(8).bitcast(U32)
        i8f = router_tile(TOPK)
        ge = router_tile(TOPK)
        chosen = router_tile(NE)
        gates = router_tile(NE + 1)
        rank = router_tile(NE + 1)
        rt = router_tile(NE)
        gatesT = reg_m[:, D:D + P]
        most = sb("most", [P, 1], I32)

        bk = [ctx.enter_context(nc.psum_tensor(f"bank{i}", [P, 512], F32)) for i in range(8)]

        x_in = [sem(f"x_in{i}") for i in range(3)]
        par_in = sem("par_in")
        small_in = sem("small_in")
        wsm_in = sem("wsm_in")
        ffnw_in = sem("ffnw_in")
        x_again = sem("x_again")
        late_in = sem("late_in")
        finw_in = sem("finw_in")
        cleared = sem("cleared")
        router_in = sem("router_in")
        filled = [sem(f"filled{i}") for i in range(RING)]
        used = sem("used")
        consts = sem("consts")
        before_g = sem("before_g")
        zeroed = sem("zeroed")
        v_link = sem("v_link")
        ssx_a = sem("ssx_a")
        ssx_v = sem("ssx_v")
        x_norm = sem("x_norm")
        raw_v = sem("raw_v")
        high_a = sem("high_a")
        low_v = sem("low_v")
        wsm_a = sem("wsm_a")
        wsm_v = sem("wsm_v")
        wh_a = sem("wh_a")
        wl_v = sem("wl_v")
        wl_g = sem("wl_g")
        half_t = sem("half_t")
        mh_a = sem("mh_a")
        ml_g = sem("ml_g")
        wo_t = sem("wo_t")
        par_t = sem("par_t")
        pj_full = sem("pj_full")
        pj_v = sem("pj_v")
        pj_a = sem("pj_a")
        sp_v = sem("sp_v")
        sp_a = sem("sp_a")
        cols_v = sem("cols_v")
        cols_t = sem("cols_t")
        dec_t = sem("dec_t")
        dec_v = sem("dec_v")
        dec_a = sem("dec_a")
        tap_a = sem("tap_a")
        silu_a = sem("silu_a")
        cb_t = sem("cb_t")
        cb_v = sem("cb_v")
        xs_t = sem("xs_t")
        xs_v = sem("xs_v")
        bc_t = sem("bc_t")
        seg_v = sem("seg_v")
        exp_a = sem("exp_a")
        m_v = sem("m_v")
        y_t = sem("y_t")
        y_v = sem("y_v")
        vt_t = sem("vt_t")
        vt_a = sem("vt_a")
        kx_v = sem("kx_v")
        kx_t = sem("kx_t")
        sc_v = sem("sc_v")
        o_t = sem("o_t")
        o_a = sem("o_a")
        z_v = sem("z_v")
        part_g = sem("part_g")
        tile_t = sem("tile_t")
        xt_v = sem("xt_v")
        rank_v = sem("rank_v")
        gates_v = sem("gates_v")
        gates_t = sem("gates_t")
        sqg_a = sem("sqg_a")
        ssg_t = sem("ssg_t")
        sq_g = sem("sq_g")
        ss_t = sem("ss_t")
        rec_v = sem("rec_v")
        rstd_t = sem("rstd_t")
        byq_a = sem("byq_a")
        turn_t = sem("turn_t")
        ms_v = sem("ms_v")
        ms_a = sem("ms_a")
        mix_v = sem("mix_v")
        h_v = sem("h_v")
        xn_v = sem("xn_v")
        xt_t = sem("xt_t")
        xt_a = sem("xt_a")
        part_a = sem("part_a")
        part_v = sem("part_v")
        lg_t = sem("lg_t")
        top_v = sem("top_v")
        top_a = sem("top_a")
        sel_v = sem("sel_v")
        rank_t = sem("rank_t")
        table_v = sem("table_v")
        pick_v = sem("pick_v")
        gath_t = sem("gath_t")
        xg_a = sem("xg_a")
        esel_v = sem("esel_v")
        gu_t = sem("gu_t")
        clip_v = sem("clip_v")
        sig_a = sem("sig_a")
        act_v = sem("act_v")
        pg_v = sem("pg_v")
        pg_t = sem("pg_t")
        gt_a = sem("gt_a")
        at_t = sem("at_t")
        at_v = sem("at_v")
        yd_t = sem("yd_t")
        ys_a = sem("ys_a")
        done_t = sem("done_t")
        out_v = sem("out_v")
        comb0_t = sem("comb0_t")
        comb_t = sem("comb_t")
        shift_v = sem("shift_v")
        fin_v = sem("fin_v")
        fin_a = sem("fin_a")
        stored = sem("stored")

        def panel_halves(n):
            m = n - FIRST
            slot = ring[:, (m // 4) % MRING, :]
            if n < NPJ:
                w = slot.rearrange("p (k c) -> p k c", k=KC)[:, :, (m % 4) * P:(m % 4 + 1) * P]
                return w[:, 0:4, :], w[:, 4:8, :]
            w = slot[:, (m % 4) * D:(m % 4 + 1) * D]
            return w[:, 0:512].rearrange("p (k c) -> p k c", k=4), w[:, 512:D].rearrange("p (k c) -> p k c", k=4)

        def halves(t, b):
            return (t[:, b, 0:512].rearrange("p (k c) -> p k c", k=4), t[:, b, 512:D].rearrange("p (k c) -> p k c", k=4))

        def token_group(t):
            return (META + t * P, P) if t < 2 else (0, META)

        def conv_chunk(n):
            return n - B_C + 8 if n < XS else n - XS

        def chunk_slot(i):
            if i >= MRING:
                return last_slots[:, i - MRING, :], filled[i], 16
            f = MIX_FILLS + i
            return ring[:, f % MRING, :], filled[f % MRING], 16 * (f // MRING + 1)

        def key_tiles(j):
            return [t for t in range(3) if (j - 1) * CH >= TILES[t][2]]

        def tile_queries(t):
            c0, n, q0 = TILES[t]
            return slice(c0, c0 + n), slice(q0, SEQ)

        def sweeps(eng, one_sweep, most_ready):
            one_sweep(0)
            eng.wait_ge(table_v, most_ready)
            count = eng.value_load(most[0:1, 0:1])
            with eng.If(count > SLOTS):
                with eng.Fori(1, SWEEPS) as p:
                    one_sweep(p)

        ALL_CONSTS = 14
        BRIDGE = 9
        MOST = 3
        block = ctx.enter_context(nc.Block())

        @block.sync
        def _(sp):
            for t in range(2):
                sp.dma_start(x_rows[:, t, :], x[0, t * P:(t + 1) * P, :]).then_inc(x_in[t], 16)
            sp.dma_start(meta_rows, meta).then_inc(x_in[2], 16)
            sp.wait_ge(cleared, 1)
            small_cols = wsm[:, 0:KC * 32].rearrange("p (k n) -> p k n", k=KC)
            sp.dma_start(small_cols[:, :, 0:HEADS],
                         w_in[0, :, DT0:Q0].rearrange("(k p) n -> p k n", p=P)).then_inc(wsm_in, 16)
            sp.dma_start(small_cols[:, :, HEADS:],
                         w_in[0, :, ALR0:ALR0 + RANK].rearrange("(k p) n -> p k n", p=P)).then_inc(wsm_in, 16)
            sp.dma_start(small[0:HEADS, 0:1], dt_bias.rearrange("a h -> h a")).then_inc(small_in, 16)
            sp.dma_start(small[0:HEADS, 1:2], a_log.rearrange("a h -> h a")).then_inc(small_in, 16)
            sp.dma_start(small[0:HEADS, 3:4], d_skip.rearrange("a h -> h a")).then_inc(small_in, 16)
            sp.dma_start(wup, w_up[0]).then_inc(small_in, 16)
            sp.wait_ge(par_in, 6 * 16)
            sp.wait_ge(small_in, 4 * 16)
            for f in range(MIX_FILLS):
                if f == NP + 1:
                    sp.wait_ge(y_v, 8)
                    sp.dma_start(ffnw, ffn_w.broadcast_to([P, D])).then_inc(ffnw_in, 16)
                    sp.wait_ge(kx_t, NCH - 1)
                    sp.dma_start(x_rows, x[0].rearrange("(t p) n -> p t n", p=P)).then_inc(x_again, 16)
                if f == NP + 3:
                    for r in range(4):
                        sp.dma_start(bdn[NE * r:NE * (r + 1), :], b_dn[0, :, (r % 2) * 512:(r % 2 + 1) * 512]).then_inc(late_in, 16)
                    sp.wait_ge(vt_t, 6)
                    sp.wait_ge(zeroed, 1)
                    sp.dma_start(bgu[0:NE, :], b_gu[0]).then_inc(late_in, 16)
                if f >= MRING:
                    sp.wait_ge(pj_full, FIRST + 4 * (f - MRING + 1))
                if f < NP:
                    c = PANELS[f]
                    sp.dma_start(ring[:, f % MRING, :].rearrange("p (k n) -> p k n", k=KC),
                                 w_in[0, :, c:c + 512].rearrange("(k p) n -> p k n", p=P)).then_inc(filled[f % MRING], 16)
                else:
                    r = (f - NP) * 512
                    sp.dma_start(ring[:, f % MRING, :].rearrange("p (k n) -> p k n", k=4),
                                 w_out[0, r:r + 512, :].rearrange("(k p) n -> p k n", p=P)).then_inc(filled[f % MRING], 16)
            sp.wait_ge(z_v, 16)
            sp.dma_start(wr, w_router[0].rearrange("(k p) n -> p k n", p=P)).then_inc(router_in, 16)
            sp.dma_start(br, b_router.broadcast_to([P, NE])).then_inc(router_in, 16)

            def sweep(p):
                with sp.Fori(0, NE) as e:
                    for i in range(RING):
                        slot, full, _ = chunk_slot(i)
                        sp.wait_ge(used, e * RING + (p * NE * RING + i + 1))
                        if i >= MRING and isinstance(p, int):
                            sp.wait_ge(wo_t, 16)
                        if i < 4:
                            src = w_gu[0, bass.ds(e, 1), i * 256:(i + 1) * 256, :].rearrange("o (k p) n -> p (o k) n", p=P)
                            dst = slot.rearrange("p (k n) -> p k n", k=2)
                        else:
                            src = w_dn[0, bass.ds(e, 1), (i - 4) * 512:(i - 3) * 512, :].rearrange("o (k p) n -> p (o k) n", p=P)
                            dst = slot.rearrange("p (k n) -> p k n", k=4)
                        sp.dma_start(dst, src).then_inc(full, 16)

            sweeps(sp, sweep, MOST)
            for t in range(2):
                sp.wait_ge(out_v, t + 1)
                sp.dma_start(out[0, t * P:(t + 1) * P, :], xn[:, t, :]).then_inc(stored, 16)
            sp.wait_ge(stored, 2 * 16)

        @block.gpsimd
        def _(pool):
            g = nc.gpsimd
            g.memset(ident[:, :], 0.0).then_inc(consts, 1)
            g.memset(ones[:, :], 1.0).then_inc(consts, 1)
            g.memset(par_rows[:, :], 0.0).then_inc(consts, 1)
            pool.wait_ge(consts, 3)
            g.affine_select(out=ident[:, :], in_=ident[:, :], compare_op=ALU.not_equal, fill=1.0, base=0,
                            pattern=[[-1, P]], channel_multiplier=1).then_inc(consts, 1)
            g.memset(minmask[:, :], 0.0).then_inc(consts, 1)
            g.memset(one_col[:, :], 0.0).then_inc(consts, 1)
            g.memset(resets, 1.0).then_inc(consts, 1)
            pool.wait_ge(consts, 7)
            g.memset(one_col[:, GH - 1:GH], 1.0).then_inc(consts, 1)
            for t, base in enumerate((META, 0, 0)):
                cols, _ = tile_queries(t)
                g.affine_select(out=minmask[:, cols], in_=minmask[:, cols], compare_op=ALU.is_ge, fill=-CAUSAL, base=base,
                                pattern=[[1, TILES[t][1]]], channel_multiplier=-1).then_inc(consts, 1)
            g.affine_select(out=resets.rearrange("p (c n) -> p c n", n=CH), in_=resets.rearrange("p (c n) -> p c n", n=CH),
                            compare_op=ALU.is_gt, fill=0.0, base=0, pattern=[[0, GH * NCH], [1, CH]],
                            channel_multiplier=0).then_inc(consts, 1)
            g.iota(slot_no[:, :, :], [[0, 2], [1, SLOTS]], base=0, channel_multiplier=0,
                   allow_small_or_imprecise_dtypes=True).then_inc(consts, 1)
            g.iota(expert_no[:, :], [[1, NE]], base=0, channel_multiplier=0,
                   allow_small_or_imprecise_dtypes=True).then_inc(consts, 1)

            def low_half(n):
                b = n % SPLITS
                pool.wait_ge(wh_a, 2 * (n - FIRST) + 2)
                if FIRST + SPLITS <= n < NPJ + SPLITS:
                    pool.wait_ge(pj_full, n - SPLITS + 1)
                if n >= NPJ + SPLITS:
                    pool.wait_ge(wo_t, n - NPJ - SPLITS + 1)
                g.tensor_tensor(halves(wl, b)[1], panel_halves(n)[1], halves(wh, b)[1].bitcast(F32), ALU.subtract).then_inc(wl_g, 1)

            for n in range(FIRST, NPJ + 16):
                low_half(n)
                c = n - ZZ - 2
                if 0 <= c < 8:
                    pool.wait_ge(z_v, c + 1)
                    if c >= 2:
                        pool.wait_ge(ss_t, c - 1)
                    g.tensor_tensor(sq[:, c % 2, :], mixed[:, c, :], mixed[:, c, :], ALU.mult).then_inc(sq_g, 1)
                if n == NPJ + 4:
                    pool.wait_ge(z_v, 16)
                    g.memset(before, 1.0).then_inc(before_g, 1)
                    pool.wait_ge(before_g, 1)
                    g.affine_select(out=before, in_=before, compare_op=ALU.is_gt, fill=0.0, base=0,
                                    pattern=[[1, P]], channel_multiplier=-1).then_inc(before_g, 1)
                k = n - NPJ
                if k >= 0:
                    pool.wait_ge(mh_a, k + 1)
                    if k >= 8:
                        pool.wait_ge(wo_t, k - 7)
                    g.tensor_tensor(ml[:, k % 8, :], mixed[:, k, :], mh[:, k % 8, :].bitcast(F32), ALU.subtract).then_inc(ml_g, 1)
            pool.wait_ge(wo_t, 16)
            g.dma_start(finw, fin_w.unsqueeze(0).broadcast_to([P, D])).then_inc(finw_in, 16)
            pool.wait_ge(part_v, 2)
            pool.wait_ge(part_a, 4)
            g.tensor_tensor(parts[:, 2, 1, :], resid[:, 1, :], parts[:, 1, 1, :], ALU.subtract).then_inc(part_g, 1)

        @block.tensor
        def _(pe):
            mm = nc.tensor.matmul
            tr = nc.tensor.transpose

            pe.wait_ge(consts, 4)
            pe.wait_ge(par_in, 6 * 16)
            tr(bk[7][:, 0:P], par_rows[:, :], ident[:, :]).then_inc(par_t, 1)
            for n in range(6):
                t = n // 2
                pe.wait_ge(x_norm, t + 1)
                if n >= 2:
                    pe.wait_ge(raw_v, n - 1)
                for j in range(4):
                    c = (4 * (n % 2) + j) * P
                    if t == 2:
                        last = tr(bk[n % 2][:, j * P:j * P + META], meta_rows[:, c:c + P], ident[0:META, 0:META])
                    else:
                        last = tr(bk[n % 2][:, j * P:(j + 1) * P], x_rows[:, t, c:c + P], ident[:, :])
                last.then_inc(pj_full, 1)

            def bank_free(n):
                owner = OWNER[n - 2]
                pe.wait_ge({"R": raw_v, "V": pj_v, "A": pj_a}[owner], freed(n - 2, owner))

            def split_mm(o, w_parts, u_parts, first, final, marks=()):
                (w0, w1), (u0, u1) = w_parts, u_parts
                for ins, mark in zip((mm(o, w0, u0, start=first, stop=False), mm(o, w0, u1, start=False, stop=False)), marks):
                    ins.then_inc(mark, 1)
                return mm(o, w1, u0, start=False, stop=final)

            pe.wait_ge(low_v, 6)
            pe.wait_ge(wsm_v, 1)
            for n in (6, 7):
                bank_free(n)
                for k in range(KC):
                    c = slice(32 * k + 16 * (n - 6), 32 * k + 16 * (n - 6) + P)
                    last = split_mm(bk[n % 2][:, 0:T], (wsm_parts[:, 0, c], wsm_parts[:, 1, c]), (uh[:, k, :], ul[:, k, :]),
                                    k == 0, k == KC - 1)
                last.then_inc(pj_full, 1)

            pe.wait_ge(cols_v, 1)
            pe.wait_ge(small_in, 64)
            for c in range(8):
                last = mm(bk[7][:, P + c:P + c + 1], spread[:, c * P:(c + 1) * P], small[0:HEADS, 3:4], start=True, stop=True)
            last.then_inc(par_t, 1)

            def decay_up():
                pe.wait_ge(pj_a, 1)
                pe.wait_ge(small_in, 64)
                for h in range(GH):
                    mm(bk[2 + h][:, 0:T], wup[:, h * P:(h + 1) * P], alr, start=True, stop=True).then_inc(dec_t, 1)

            def key_columns():
                pe.wait_ge(cols_v, 3)
                for i, src in enumerate((acsT, dtT)):
                    for t in range(3):
                        last = tr(bk[6][:, (3 * i + t) * 16:(3 * i + t + 1) * 16], src[:, t * P:(t + 1) * P], ident[0:16, 0:16])
                last.then_inc(cols_t, 1)

            def c_times_b():
                pe.wait_ge(silu_a, 4)
                pe.wait_ge(dec_v, GH)
                for g in range(2):
                    b0 = (8 + g) * T
                    for t in range(3):
                        cols, q = tile_queries(t)
                        last = mm(bk[4 + g][:, cols], reg_c[:, b0 + t * P:b0 + (t + 1) * P],
                                  xbc[:, 10 + g, META + q.start:], start=True, stop=True)
                    last.then_inc(cb_t, 1)

            def xs_rows(g):
                t, half = g // 2, g % 2
                if g == 0:
                    pe.wait_ge(silu_a, 12)
                    pe.wait_ge(cb_v, 2)
                if g >= 2:
                    pe.wait_ge(xs_v, g - 1)
                for j in range(4):
                    c = (4 * half + j) * T + t * P
                    last = tr(bk[4 + g % 2][:, j * P:(j + 1) * P], reg_c[:, c:c + P], ident[:, :])
                last.then_inc(xs_t, 1)

            def head_step(s):
                if s < HEADS:
                    if s >= 2:
                        pe.wait_ge(seg_v, 3 * (s - 1))
                    else:
                        pe.wait_ge(dec_v, GH)
                        pe.wait_ge(cols_v, 4)
                    mm(bk[2 + s % 2][:, 0:SEQ], headrow[:, s, :], acsT[:, META:T], start=True, stop=True).then_inc(bc_t, 1)
                if s >= 4 and s % 2 == 0:
                    pair = (s - 4, s - 3)
                    pe.wait_ge(m_v, s - 2)
                    if s >= 8:
                        pe.wait_ge(y_v, (s - 6) // 2)
                    if s == 4:
                        pe.wait_ge(xs_v, 6)
                    for t in range(3):
                        cols, q = tile_queries(t)
                        for h in pair:
                            r = HD * (h % 2)
                            ins = mm(bk[6 + h // 2 % 2][r:r + HD, q], dtx[:, t, h * HD:(h + 1) * HD], hm[h % 4][:, cols],
                                     start=(t == 0), stop=(t == 2), skip_group_check=True)
                            if t == 2:
                                ins.then_inc(y_t, 1)

            def v_to_rows(g):
                t, half = g // 2, g % 2
                if g == 0:
                    pe.wait_ge(pj_a, freed(VV + 7, "A"))
                else:
                    pe.wait_ge(vt_a, g)
                for j in range(4):
                    c = (4 * half + j) * T + t * P
                    last = tr(bk[5][:, j * P:(j + 1) * P], reg_v[:, c:c + P], ident[:, :])
                last.then_inc(vt_t, 1)

            def gla_scores(j):
                pe.wait_ge(kx_v, j)
                if j == 1:
                    pe.wait_ge(y_v, 8)
                if j >= 3:
                    pe.wait_ge(byq_a, j - 2)
                for h in range(GH):
                    q0 = h * SEQ + (j - 1) * CH
                    m = min(32, GH * SEQ - q0)
                    last = mm(bk[2 + j % 2][32 * h:32 * h + m, 0:(j + 1) * CH], reg_q[:, q0:q0 + m],
                              kx[:, j % 2, h, 0:(j + 1) * CH], start=True, stop=True)
                last.then_inc(kx_t, 1)

            def turn_scores(j):
                pe.wait_ge(byq_a, j)
                if j >= 3:
                    pe.wait_ge(sc_v, j - 2)
                for t in key_tiles(j):
                    last = tr(bk[6 + j % 2][:, t * P:(t + 1) * P], by_query[:, j % 2, t * P:(t + 1) * P], ident[:, :])
                last.then_inc(turn_t, 1)

            def gla_out(i):
                h = i // 2
                pe.wait_ge(sc_v, NCH - 1)
                if i >= 2:
                    sum_gla_squares(i - 2)
                if i == 0:
                    pe.wait_ge(vt_a, 6)
                if i >= 2:
                    pe.wait_ge(o_a, i - 1)
                for t in range(3):
                    cols, q = tile_queries(t)
                    last = mm(bk[2 + i % 2][:, q], v_rows[:, t, i * P:(i + 1) * P], sc[:, h, cols],
                              start=(t == 0), stop=(t == 2), skip_group_check=True)
                last.then_inc(o_t, 1)

            def sum_squares(c):
                pe.wait_ge(sq_g, c + 1)
                if c == 0:
                    pe.wait_ge(xs_v, 6)
                    pe.wait_ge(consts, ALL_CONSTS)
                row = c // 4
                mm(bk[4][0:GH, 0:SEQ], one_col[:, GH - 1 - row:2 * GH - 1 - row], sq[:, c % 2, :],
                   start=(c == 0), stop=(c == 7)).then_inc(ss_t, 1)

            def sum_gla_squares(i):
                pe.wait_ge(sqg_a, i + 1)
                row = i // 2
                mm(bk[6][0:GH, 0:SEQ], one_col[:, GH - 1 - row:2 * GH - 1 - row], sq_gla[:, i % 2, :],
                   start=(i == 0), stop=(i == 7)).then_inc(ssg_t, 1)

            def spread_rstd(which):
                pe.wait_ge(o_a, 8)
                for i in which:
                    b, half = RSTD_AT[i]
                    kind, row = (0, i) if i < 2 else (1, i - 2)
                    pe.wait_ge(rec_v, kind + 1)
                    mm(bk[b][:, half * SEQ:(half + 1) * SEQ], one_row[:, row, :], rstd[:, kind, :],
                       start=True, stop=True).then_inc(rstd_t, 1)

            for n in range(FIRST, NPJ):
                m = n - FIRST
                bank_free(n)
                t0 = 0 if n < QQ or KK <= n < ZZ else META
                for half, low in ((0, wl_v), (1, wl_g)):
                    pe.wait_ge(low, m + 1)
                    for k in range(4):
                        u = 4 * half + k
                        last = split_mm(bk[n % 2][:, 0:T - t0], (halves(wh, n % SPLITS)[half][:, k, :], halves(wl, n % SPLITS)[half][:, k, :]),
                                        (uh[:, u, t0:], ul[:, u, t0:]), u == 0, u == KC - 1)
                        if k % 2 and n in GLA_STEPS:
                            j = GLA_STEPS[n][2 * half + k // 2]
                            gla_scores(j)
                            if j > 1:
                                turn_scores(j - 1)
                            if j == NCH - 1:
                                turn_scores(j)
                    last.then_inc((half_t, pj_full)[half], 1)
                if n == 12:
                    decay_up()
                if n == 14:
                    key_columns()
                if n == 19:
                    c_times_b()
                if n in (20, 21):
                    for g in range(3 * (n - 20), 3 * (n - 19)):
                        xs_rows(g)
                for s in HEAD_STEPS.get(n, ()):
                    head_step(s)
                if ZZ <= n < ZZ + 6:
                    v_to_rows(n - ZZ)
                if ZZ + 3 <= n < ZZ + 11:
                    sum_squares(n - ZZ - 3)
                for i in OT_STEPS.get(n, ()):
                    gla_out(i)
                if n == GG:
                    sum_gla_squares(6)
                    sum_gla_squares(7)
                if n == GG + 5:
                    spread_rstd(range(4))
            bank_free(NPJ)
            spread_rstd((4, 5))

            for k in range(16):
                n = NPJ + k
                b = n % SPLITS
                pe.wait_ge(ml_g, k + 1)
                order = [(half, t) for half in range(2) for t in range(2)] if k < 15 else [(half, t) for t in range(2) for half in range(2)]
                for i, (half, t) in enumerate(order):
                    pe.wait_ge((wl_v, wl_g)[half], n - FIRST + 1)
                    cols, toks = slice(half * 512, (half + 1) * 512), slice(t * P, (t + 1) * P)
                    marks = ((), (), (used,), (used, used))[i] if k == 15 else ()
                    last = split_mm(bk[4 + 2 * t + half][:, :], (mh[:, k % 8, toks], ml[:, k % 8, toks]),
                                    (wh[:, b, cols], wl[:, b, cols]), k == 0, k == 15, marks)
                    if i == 1:
                        last.then_inc(half_t if k < 15 else tile_t, 1)
                    if i == 2 and k in (3, 7, 11):
                        last.then_inc(used, 1)
                    if i == 3:
                        last.then_inc(wo_t, 1)

            for i in range(BRIDGE):
                mm(bk[0][:, 0:PACK], ident[:, :], minmask[:, :], start=True, stop=True)
            for i in range(4):
                t, half = i // 2, i % 2
                pe.wait_ge(xn_v, t + 1)
                for j in range(4):
                    c = (4 * half + j) * P
                    last = tr(bk[i][:, j * P:(j + 1) * P], xn[:, t, c:c + P], ident[:, :])
                last.then_inc(xt_t, 1)
            pe.wait_ge(router_in, 32)
            for t, sem_x in enumerate((xt_a, xt_v)):
                pe.wait_ge(sem_x, 2)
                for k in range(KC):
                    last = mm(bk[0][:, t * NE:(t + 1) * NE], xnT[:, k, t * P:(t + 1) * P], wr[:, k, :],
                              start=(k == 0), stop=(k == KC - 1))
            last.then_inc(lg_t, 1)
            for i in range(3):
                mm(bk[3][:, 0:PACK], ident[:, :], minmask[:, :], start=True, stop=True)
            pe.wait_ge(sel_v, 1)
            pe.wait_ge(before_g, 2)
            mm(bk[1][:, 0:NE], before[:, :], chosen[:, 0, :], start=True, stop=True)
            mm(bk[1][:, NE:2 * NE], ones[:, :], chosen[:, 0, :], start=True, stop=False)
            mm(bk[1][:, NE:2 * NE], before[:, :], chosen[:, 1, :], start=False, stop=True)
            mm(bk[2][:, 0:NE], ones[:, :], chosen[:, 0, :], start=True, stop=False)
            mm(bk[2][:, 0:NE], ones[:, :], chosen[:, 1, :], start=False, stop=True).then_inc(rank_t, 1)
            mm(bk[3][:, 0:PACK], ident[:, :], minmask[:, :], start=True, stop=True)

            def open_outputs():
                pe.wait_ge(gates_v, 1)
                for r in range(4):
                    last = mm(bk[0][NE * r:NE * (r + 1), 0:P], gates[:, r // 2, 0:NE], ident[:, :], start=True, stop=True)
                last.then_inc(gates_t, 1)
                pe.wait_ge(table_v, MOST)
                pe.wait_ge(h_v, 4)
                pe.wait_ge(late_in, 5 * 16)
                for t in range(2):
                    for half in range(2):
                        rows = slice(NE * (2 * t + half), NE * (2 * t + half + 1))
                        last = mm(bk[4 + 2 * t + half][:, :], gatesT[rows, :], bdn[rows, :],
                                  start=True, stop=False, skip_group_check=True)
                        if t == 0:
                            last.then_inc((gu_t, pg_t)[half], 1)

            def gather(count):
                pe.wait_ge(pick_v, count)
                for k in range(KC):
                    for t in range(2):
                        for i in range(3):
                            last = mm(bk[3][:, k * SLOTS:(k + 1) * SLOTS], parts[:, i, t, k * P:(k + 1) * P], pick[:, t, :],
                                      start=(t == 0 and i == 0), stop=(t == 1 and i == 2))
                last.then_inc(gath_t, 1)

            def sweep(p):
                if isinstance(p, int):
                    pe.wait_ge(part_a, 4)
                    pe.wait_ge(part_v, 3)
                    pe.wait_ge(part_g, 1)
                gather(p * (NE + 1) + 1)
                if isinstance(p, int):
                    open_outputs()
                with pe.Fori(0, NE) as e:
                    pe.wait_ge(xg_a, e + (p * (NE + 1) + 1))
                    for i in range(4):
                        slot, full, first_fill = chunk_slot(i)
                        pe.wait_ge(full, e * 16 + (p * NE * 16 + first_fill))
                        w = slot.rearrange("p (k n) -> p k n", k=2)
                        for kk in range(2):
                            k = 2 * i + kk
                            for up in range(2):
                                for half in range(2):
                                    last = mm(bk[up][half * SLOTS:(half + 1) * SLOTS, :], xg[:, k, :],
                                              w[:, kk, up * D + half * 512:up * D + (half + 1) * 512],
                                              start=(k == 0), stop=False, skip_group_check=True)
                        last.then_inc(used, 1)
                    pe.wait_ge(esel_v, e + (p * NE + 1))
                    for up in range(2):
                        for half in range(2):
                            last = mm(bk[up][half * SLOTS:(half + 1) * SLOTS, :], esel[:, :],
                                      bgu[:, up * D + half * 512:up * D + (half + 1) * 512],
                                      start=False, stop=True, skip_group_check=True)
                    last.then_inc(gu_t, 1)
                    pe.wait_ge(pg_v, e + (p * NE + 1))
                    for t in range(2):
                        last = tr(bk[2][:, t * P:(t + 1) * P], pg[:, t, :], ident[:, :])
                    last.then_inc(pg_t, 1)
                    gather(e + (p * (NE + 1) + 2))
                    pe.wait_ge(act_v, e + (p * NE + 1))
                    pe.wait_ge(xg_a, e + (p * (NE + 1) + 2))
                    for j in range(4):
                        last = tr(bk[3][:, j * P:(j + 1) * P], actS[:, j * P:(j + 1) * P], ident[:, :])
                    last.then_inc(at_t, 1)
                    pe.wait_ge(at_v, e + (p * NE + 1))
                    pe.wait_ge(gt_a, e + (p * NE + 1))
                    for i in range(4, 6):
                        slot, full, first_fill = chunk_slot(i)
                        pe.wait_ge(full, e * 16 + (p * NE * 16 + first_fill))
                        w = slot.rearrange("p (k n) -> p k n", k=4)
                        for j in range(4):
                            for half in range(2):
                                last = mm(bk[2][half * SLOTS:(half + 1) * SLOTS, :], actT[:, j, i - 4, :],
                                          w[:, j, half * 512:(half + 1) * 512],
                                          start=(i == 4 and j == 0), stop=(i == 5 and j == 3), skip_group_check=True)
                        last.then_inc(used if i == 4 else yd_t, 1)
                    pe.wait_ge(ys_a, e + (p * NE + 1))
                    for t in range(2):
                        for half in range(2):
                            r = half * SLOTS
                            last = mm(bk[4 + 2 * t + half][:, :], gT[r:r + SLOTS, t * P:(t + 1) * P], yS[r:r + SLOTS, :],
                                      start=False, stop=False, skip_group_check=True)
                            if t == half == 0:
                                last.then_inc(used, 1)
                            if (t, half) == (0, 1):
                                last.then_inc(comb0_t, 1)
                    last.then_inc(comb_t, 1)

            sweeps(pe, sweep, MOST)
            mm(bk[0][:, 0:1], ident[:, :], ones[:, 0:1], start=True, stop=True).then_inc(done_t, 1)

        @block.scalar
        def _(act):
            a = nc.scalar

            def copy(out, in_):
                return a.activation(out, in_, ACT.Copy)

            warmed = [0]

            def table_for(function):
                warmed[0] += 1
                a.activation(small[0:1, 8 + warmed[0]:9 + warmed[0]], ones[0:1, 0:1], function)

            act.wait_ge(consts, 3)
            r = 0
            for src, n in ((mix_w.rearrange("a (c p) -> (a c) p", p=P), 8),
                           (conv_w.rearrange("a t (c p) -> (a t c) p", p=P), 48),
                           (conv_b.rearrange("a (c p) -> (a c) p", p=P), 12),
                           (ssd_w.rearrange("a (c p) -> (a c) p", p=P), 8),
                           (b_decay.rearrange("a (c p) -> (a c) p", p=P), 4),
                           (gla_w.rearrange("a (c p) -> (a c) p", p=P), 2)):
                act.dma_start(par_rows[r:r + n, :], src).then_inc(par_in, 16)
                r += n
            table_for(ACT.Sqrt)
            act.wait_ge(cleared, 1)

            def row_squares(i):
                act.wait_ge(x_in[i], 16)
                if i < 2:
                    a.activation(junk, x_rows[:, i, :], ACT.Square, accum_out=ssx[:, i:i + 1]).then_inc(ssx_a, 1)
                else:
                    a.activation(junk[0:META, :], meta_rows, ACT.Square, accum_out=ssx[0:META, 2:3]).then_inc(ssx_a, 1)

            def row_root(i):
                act.wait_ge(ssx_v, i + 1)
                a.activation(ssx[:, 3 + i:4 + i], ssx[:, 3 + i:4 + i], ACT.Sqrt).then_inc(ssx_a, 1)

            row_squares(0)
            act.wait_ge(ssx_a, 1)
            row_squares(1)
            row_root(0)
            act.wait_ge(ssx_a, 2)
            row_squares(2)
            row_root(1)
            row_root(2)
            act.wait_ge(small_in, 64)
            a.activation(small[0:HEADS, 2:3], small[0:HEADS, 1:2], ACT.Exp).then_inc(sp_a, 1)
            for n in range(6):
                act.wait_ge(raw_v, n + 1)
                c, w = token_group(n // 2)
                copy(uh[:, 4 * (n % 2):4 * (n % 2) + 4, c:c + w], u_raw[:, 4 * (n % 2):4 * (n % 2) + 4, c:c + w]).then_inc(high_a, 1)
                if n == 1:
                    act.wait_ge(wsm_in, 32)
                    copy(wsm_parts[:, 0, :], wsm).then_inc(wsm_a, 1)

            def high_halves(n):
                m = n - FIRST
                if m % 4 == 0:
                    act.wait_ge(filled[m // 4 % MRING], 16 * (m // 4 // MRING + 1))
                for half in range(2):
                    if m >= SPLITS:
                        if half == 0:
                            act.wait_ge(half_t, m - SPLITS + 1)
                        elif n - SPLITS < NPJ:
                            act.wait_ge(pj_full, n - SPLITS + 1)
                        else:
                            act.wait_ge(wo_t, n - SPLITS - NPJ + 1)
                    copy(halves(wh, n % SPLITS)[half], panel_halves(n)[half]).then_inc(wh_a, 1)

            high_halves(FIRST)
            high_halves(FIRST + 1)
            act.wait_ge(pj_full, 8)
            copy(alr, bk[1][0:RANK, 0:T]).then_inc(pj_a, 1)
            high_halves(FIRST + 2)
            for n in range(B_C, QQ):
                c = conv_chunk(n)
                act.wait_ge(pj_full, n + 1)
                a.activation(xbc[:, c, :], bk[n % 2][:, 0:T], ACT.Identity, scale=par[:, 44 + c:45 + c],
                             bias=par[:, 56 + c:57 + c]).then_inc(tap_a, 1)
                if n == 8:
                    act.wait_ge(sp_v, 1)
                    a.activation(dta[:, 1, :], dta[:, 1, :], ACT.Exp, scale=-1.0).then_inc(sp_a, 1)
                if n == 10:
                    act.wait_ge(sp_v, 2)
                    a.activation(dta[:, 3, :], dta[:, 2, :], ACT.Ln).then_inc(sp_a, 1)
                if n == 13:
                    act.wait_ge(dec_v, 5)
                    a.activation(gb, gb, ACT.Exp, scale=-1.0).then_inc(dec_a, 1)
                if n == 14:
                    act.wait_ge(dec_a, 1)
                    a.activation(gb, gb, ACT.Ln, bias=1.0).then_inc(dec_a, 1)
                if n + 3 <= QQ + 1:
                    high_halves(n + 3)
                if n == 15:
                    act.wait_ge(dec_v, 7)
                    a.activation(gb, ga, ACT.Exp, scale=1.0 / TAU).then_inc(dec_a, 1)
                    a.activation(gc, ga, ACT.Exp, scale=-1.0 / TAU).then_inc(dec_a, 1)
                if n == 17:
                    act.wait_ge(dec_v, 9)
                    a.activation(ga, ga, ACT.Exp, scale=1.0 / TAU).then_inc(dec_a, 1)
                    a.activation(dec[:, :, :], dec[:, :, :], ACT.Exp, scale=1.0 / TAU).then_inc(dec_a, 1)
                if n >= 17:
                    for i in range(4 * (n - 17), 4 * (n - 16)):
                        o = xbc[:, conv_chunk(B_C + i), :]
                        act.wait_ge(pj_v, freed(B_C + i, "V"))
                        a.activation(o, o, ACT.Silu).then_inc(silu_a, 1)
            for n in range(QQ, NPJ):
                if n not in GLA_STEPS:
                    high_halves(n + 2)
                for j in GLA_STEPS.get(n, ()):
                    if j % 4 == 3:
                        high_halves(n + 2)
                    act.wait_ge(kx_t, j)
                    if j >= 3:
                        act.wait_ge(turn_t, j - 2)
                    copy(by_query[:, j % 2, 0:(j + 1) * CH], bk[2 + j % 2][:, 0:(j + 1) * CH]).then_inc(byq_a, 1)
                if VV <= n < ZZ:
                    act.wait_ge(pj_full, n + 1)
                    copy(vT[:, n - VV, :], bk[n % 2][:, 0:T]).then_inc(pj_a, 1)
                for s in HEAD_STEPS.get(n, ()):
                    if s < HEADS:
                        act.wait_ge(seg_v, 3 * (s + 1))
                        a.activation(seg[:, s % 2, :], seg[:, s % 2, :], ACT.Exp).then_inc(exp_a, 1)
                if n >= ZZ:
                    act.wait_ge(pj_full, n + 1)
                    if n >= ZZ + 2:
                        act.wait_ge(z_v, n - ZZ - 1)
                    a.activation(tmp[:, n % 2, :], bk[n % 2][:, 0:SEQ], ACT.Silu).then_inc(pj_a, 1)
                if ZZ <= n < ZZ + 6:
                    g = n - ZZ
                    act.wait_ge(vt_t, g + 1)
                    copy(v_rows[:, g // 2, (g % 2) * 512:(g % 2 + 1) * 512], bk[5][:, :]).then_inc(vt_a, 1)
                for i in OT_STEPS.get(n, ()):
                    act.wait_ge(o_t, i + 1)
                    if i >= 2:
                        act.wait_ge(ssg_t, i - 1)
                    a.activation(sq_gla[:, i % 2, :], bk[2 + i % 2][:, 0:SEQ], ACT.Square).then_inc(sqg_a, 1)
                    copy(mixed[:, 8 + i, :], bk[2 + i % 2][:, 0:SEQ]).then_inc(o_a, 1)
                if n == GG + 3:
                    for i in range(2):
                        act.wait_ge(ms_v, i + 1)
                        a.activation(rstd[:, i, :], rstd[:, i, :], ACT.Sqrt).then_inc(ms_a, 1)
            for k in range(16):
                act.wait_ge(mix_v, k + 1)
                if k >= 8:
                    act.wait_ge(wo_t, k - 7)
                copy(mh[:, k % 8, :], mixed[:, k, :]).then_inc(mh_a, 1)
                if k < 14:
                    high_halves(NPJ + k + 2)
            spare = reg_r[:, 2 * D:3 * D]
            table_for(ACT.Sqrt)
            for t in range(2):
                act.wait_ge(h_v, 2 * t + 2)
                a.activation(spare, x_rows[:, t, :], ACT.Square, accum_out=ssx[:, t:t + 1]).then_inc(ssx_a, 1)
                act.wait_ge(ssx_v, 4 + t)
                a.activation(ssx[:, 2 + t:3 + t], ssx[:, 2 + t:3 + t], ACT.Sqrt).then_inc(ssx_a, 1)
            for i in range(2):
                act.wait_ge(xt_t, i + 1)
                copy(xnT[:, 4 * i:4 * i + 4, 0:P], bk[i][:, :].rearrange("p (k n) -> p k n", k=4)).then_inc(xt_a, 1)
            for t in range(2):
                act.wait_ge(xn_v, t + 1)
                copy(parts[:, 0, t, :], xn[:, t, :]).then_inc(part_a, 1)
            table_for(ACT.Exp)
            for t in range(2):
                act.wait_ge(part_v, t + 1)
                copy(parts[:, 1, t, :], resid[:, t, :]).then_inc(part_a, 1)
            act.wait_ge(top_v, 3)
            for t in range(2):
                a.activation(ge[:, t, :], m8[:, t, 0:TOPK], ACT.Exp, bias=ssx[:, 4 + t:5 + t]).then_inc(top_a, 1)

            table_for(ACT.Sigmoid)

            def sweep(p):
                act.wait_ge(gath_t, p * (NE + 1) + 1)
                copy(xg, bk[3][:, :].rearrange("p (k s) -> p k s", k=KC)).then_inc(xg_a, 1)
                with act.Fori(0, NE) as e:
                    act.wait_ge(clip_v, e * 3 + (p * NE * 3 + 1))
                    a.activation(sigS, gateS, ACT.Sigmoid, scale=ALPHA).then_inc(sig_a, 1)
                    act.wait_ge(pg_t, e + (p * NE + 2))
                    copy(gT, bk[2][:, 0:2 * P]).then_inc(gt_a, 1)
                    act.wait_ge(gath_t, e + (p * (NE + 1) + 2))
                    copy(xg, bk[3][:, :].rearrange("p (k s) -> p k s", k=KC)).then_inc(xg_a, 1)
                    act.wait_ge(yd_t, e + (p * NE + 1))
                    copy(yS, bk[2][:, :]).then_inc(ys_a, 1)

            sweeps(act, sweep, MOST)
            table_for(ACT.Sqrt)
            for t in range(2):
                act.wait_ge(fin_v, 1 + t)
                a.activation(spare, x_rows[:, t, :], ACT.Square, accum_out=ssx[:, t:t + 1]).then_inc(fin_a, 1)
                act.wait_ge(fin_v, 3 + t)
                a.activation(ssx[:, 2 + t:3 + t], ssx[:, 2 + t:3 + t], ACT.Sqrt).then_inc(fin_a, 1)

        @block.vector
        def _(dve):
            v = nc.vector
            links = [0]

            def link(ins):
                links[0] += 1
                ins.then_inc(v_link, 1)
                dve.wait_ge(v_link, links[0])

            v.memset(ssx[:, :], 1.0)
            v.memset(dtT, 0.0)
            v.memset(acsT[:, :], 0.0)
            link(v.memset(reg_v[:, KC * T:], 0.0))
            link(v.memset(wsm[:, KC * 32:], 0.0))
            v.memset(dta[:, 1, :], 1.0).then_inc(cleared, 1)
            dve.wait_ge(par_t, 1)
            link(v.tensor_copy(par[:, :], bk[7][:, 0:P]))

            def row_mean(i):
                dve.wait_ge(ssx_a, (1, 2, 4)[i])
                v.tensor_scalar(ssx[:, 3 + i:4 + i], ssx[:, i:i + 1], 1.0 / D, EPS, ALU.mult, ALU.add).then_inc(ssx_v, 1)

            def row_scale(i):
                dve.wait_ge(ssx_a, (3, 5, 6)[i])
                link(v.reciprocal(ssx[:, 3 + i:4 + i], ssx[:, 3 + i:4 + i]))
                rows, n = (x_rows[:, i, :], P) if i < 2 else (meta_rows, META)
                v.tensor_scalar(rows, rows, ssx[0:n, 3 + i:4 + i], None, ALU.mult).then_inc(x_norm, 1)

            row_mean(0)
            row_mean(1)
            row_scale(0)
            row_mean(2)
            row_scale(1)
            row_scale(2)
            def low_u(n):
                k0, (c, w) = 4 * (n % 2), token_group(n // 2)
                dve.wait_ge(high_a, n + 1)
                v.tensor_tensor(ul[:, k0:k0 + 4, c:c + w], u_raw[:, k0:k0 + 4, c:c + w],
                                uh[:, k0:k0 + 4, c:c + w].bitcast(F32), ALU.subtract).then_inc(low_v, 1)

            def low_half(n):
                m, b = n - FIRST, n % SPLITS
                dve.wait_ge(wh_a, 2 * m + 1)
                if m >= SPLITS:
                    dve.wait_ge(half_t, m - SPLITS + 1)
                v.tensor_tensor(halves(wl, b)[0], panel_halves(n)[0], halves(wh, b)[0].bitcast(F32), ALU.subtract).then_inc(wl_v, 1)

            for n in range(6):
                t, k0 = n // 2, 4 * (n % 2)
                c, w = token_group(t)
                dve.wait_ge(pj_full, n + 1)
                v.tensor_tensor(u_raw[:, k0:k0 + 4, c:c + w], bk[n % 2][:, :].rearrange("p (k n) -> p k n", k=4)[:, :, 0:w],
                                par[:, k0:k0 + 4].unsqueeze(2).broadcast_to([P, 4, w]), ALU.mult).then_inc(raw_v, 1)
                if n >= 1:
                    low_u(n - 1)
                if n == 2:
                    dve.wait_ge(wsm_a, 1)
                    v.tensor_tensor(wsm_parts[:, 1, :], wsm, wsm_parts[:, 0, :].bitcast(F32), ALU.subtract).then_inc(wsm_v, 1)
            low_u(5)
            low_half(FIRST)
            low_half(FIRST + 1)
            dve.wait_ge(consts, 4)
            v.tensor_copy(spread.rearrange("p (h n) -> p h n", h=HEADS),
                          ident[0:HEADS, 0:HEADS].unsqueeze(2).broadcast_to([HEADS, HEADS, HD]))
            v.tensor_copy(one_row[:, :, :], ident[0:GH, 0:GH].unsqueeze(2).broadcast_to([GH, GH, P]))
            v.tensor_copy(headrow[:, :, :], ident[0:HEADS, 0:HEADS].unsqueeze(2).broadcast_to([HEADS, HEADS, P])).then_inc(cols_v, 1)
            dve.wait_ge(pj_full, 7)
            dve.wait_ge(small_in, 64)
            v.tensor_scalar(dta[:, 0, :], bk[0][0:HEADS, 0:T], small[0:HEADS, 0:1], None, ALU.add).then_inc(pj_v, 1)
            dve.wait_ge(pj_v, 1)
            v.scalar_tensor_tensor(dta[:, 1, :], dta[:, 0, :], -1.0, dta[:, 0, :], ALU.mult, ALU.max).then_inc(sp_v, 1)

            dve.wait_ge(par_t, 2)
            link(v.tensor_copy(par[:, 82:90], bk[7][:, P:P + 8]))

            def conv(n):
                c = conv_chunk(n)
                bank, o = bk[n % 2], xbc[:, c, :]
                dve.wait_ge(tap_a, n - B_C + 1)
                for back in (1, 2, 3):
                    tap = 8 + 12 * (3 - back) + c
                    ins = v.scalar_tensor_tensor(o[:, back:], bank[:, 0:T - back], par[:, tap:tap + 1], o[:, back:],
                                                 ALU.mult, ALU.add)
                    if back < 3:
                        link(ins)
                    else:
                        ins.then_inc(pj_v, 1)
                low_half(n + 2)

            for n in (8, 9):
                conv(n)
            dve.wait_ge(sp_a, 2)
            v.tensor_scalar(dta[:, 2, :], dta[:, 1, :], 1.0, None, ALU.add).then_inc(sp_v, 1)
            conv(10)
            dve.wait_ge(sp_a, 3)
            link(v.scalar_tensor_tensor(dta[:, 1, :], dta[:, 2, :], -1.0, dta[:, 1, :], ALU.add, ALU.subtract))
            link(v.reciprocal(dta[:, 2, :], dta[:, 2, :]))
            link(v.tensor_tensor(dta[:, 1, :], dta[:, 1, :], dta[:, 2, :], ALU.mult))
            link(v.tensor_tensor(dta[:, 3, :], dta[:, 3, :], dta[:, 1, :], ALU.subtract))
            v.scalar_tensor_tensor(dtT[:, 0:T], dta[:, 0, :], 0.0, dta[:, 3, :], ALU.max, ALU.add).then_inc(cols_v, 1)
            conv(11)
            dve.wait_ge(cols_v, 2)
            link(v.tensor_scalar(dta[:, 0, :], dtT[:, 0:T], small[0:HEADS, 2:3], -1.0, ALU.mult, ALU.mult))
            link(v.memset(dta[:, 1, :], 1.0))
            v.tensor_tensor_scan(acsT[:, 0:T], dta[:, 1, :], dta[:, 0, :], 0.0, ALU.mult, ALU.add).then_inc(cols_v, 1)
            conv(12)
            for h in range(GH):
                dve.wait_ge(dec_t, h + 1)
                v.tensor_scalar(ga[:, h * T:(h + 1) * T], bk[2 + h][:, 0:T], par[:, 76 + h:77 + h], None, ALU.add).then_inc(dec_v, 1)
            dve.wait_ge(dec_v, 4)
            v.scalar_tensor_tensor(gb, ga, -1.0, ga, ALU.mult, ALU.max).then_inc(dec_v, 1)
            conv(13)
            conv(14)
            dve.wait_ge(dec_a, 2)
            dve.wait_ge(consts, ALL_CONSTS)
            v.scalar_tensor_tensor(gc, ga, 0.0, gb, ALU.min, ALU.subtract).then_inc(dec_v, 1)
            dve.wait_ge(dec_v, 6)
            v.tensor_tensor_scan(ga, resets, gc, 0.0, ALU.mult, ALU.add).then_inc(dec_v, 1)
            dve.wait_ge(cols_t, 1)
            v.tensor_copy(keycols[:, :, :].rearrange("p a h -> p (a h)"), bk[6][:, 0:6 * HEADS]).then_inc(cols_v, 1)
            conv(15)
            conv(16)
            dve.wait_ge(dec_a, 4)
            g_chunks = ga.rearrange("p (c n) -> p c n", n=CH)
            ends = dec[:, :, :].rearrange("p h c -> p (h c)")
            v.tensor_copy(ends, g_chunks[:, :, CH - 1]).then_inc(dec_v, 1)
            dve.wait_ge(dec_v, 8)
            v.tensor_tensor(g_chunks, ends.unsqueeze(2).broadcast_to([P, GH * NCH, CH]), g_chunks, ALU.subtract).then_inc(dec_v, 1)
            for n in (17, 18):
                conv(n)
            conv(19)
            for g in range(2):
                dve.wait_ge(cb_t, g + 1)
                v.tensor_copy(cb[:, g, :], bk[4 + g][:, 0:PACK]).then_inc(cb_v, 1)

            def xs_rows(g):
                t, half = g // 2, g % 2
                dve.wait_ge(xs_t, g + 1)
                v.tensor_tensor(dtx[:, t, half * 512:(half + 1) * 512].rearrange("p (h n) -> p h n", h=8),
                                bk[4 + g % 2][:, :].rearrange("p (h n) -> p h n", h=8),
                                keycols[:, 3 + t, 8 * half:8 * half + 8].unsqueeze(2).broadcast_to([P, 8, HD]),
                                ALU.mult).then_inc(xs_v, 1)

            def head_step(s):
                if s < HEADS:
                    dve.wait_ge(bc_t, s + 1)
                    if s == 0:
                        dve.wait_ge(cols_v, 4)
                    if s >= 2:
                        dve.wait_ge(m_v, s - 1)
                    for t in range(3):
                        cols, q = tile_queries(t)
                        v.scalar_tensor_tensor(seg[:, s % 2, cols], bk[2 + s % 2][:, q], keycols[:, t, s:s + 1],
                                               minmask[:, cols], ALU.subtract, ALU.min).then_inc(seg_v, 1)
                if 1 <= s <= HEADS:
                    h = s - 1
                    dve.wait_ge(exp_a, h + 1)
                    if h >= 4:
                        dve.wait_ge(y_t, h - 3)
                    v.tensor_tensor(hm[h % 4], seg[:, h % 2, :], cb[:, h // 8, :], ALU.mult).then_inc(m_v, 1)
                if s >= 4 and s % 2 == 0:
                    c = (s - 4) // 2
                    dve.wait_ge(y_t, 2 * c + 2)
                    v.scalar_tensor_tensor(mixed[:, c, :], xbc[:, c, META:], par[:, 82 + c:83 + c],
                                           bk[6 + c % 2][:, 0:SEQ], ALU.mult, ALU.add).then_inc(y_v, 1)

            def decayed_keys(j):
                b = j % 2
                if j >= 3:
                    dve.wait_ge(kx_t, j - 2)
                if j >= 2:
                    dve.wait_ge(kx_v, j - 1)
                    n = CH * (j - 1)
                    v.tensor_tensor(kx[:, b, :, 0:n], kx[:, 1 - b, :, 0:n],
                                    dec[:, :, j - 1:j].broadcast_to([P, GH, n]), ALU.mult)
                v.tensor_copy(kx[:, b, :, CH * (j - 1):CH * j], by_head(ga)[:, :, CH * (j - 1):CH * j])
                v.tensor_copy(kx[:, b, :, CH * j:CH * (j + 1)], by_head(gc)[:, :, CH * j:CH * (j + 1)]).then_inc(kx_v, 1)

            def causal_scores(j):
                dve.wait_ge(turn_t, j)
                for t in key_tiles(j):
                    c = TILES[t][0] + (j - 1) * CH - TILES[t][2]
                    last = v.scalar_tensor_tensor(sc[:, :, c:c + CH], minmask[:, c:c + CH].unsqueeze(1).broadcast_to([P, GH, CH]), 0.0,
                                                  bk[6 + j % 2][:, t * P:(t + 1) * P].rearrange("p (h n) -> p h n", h=GH)[:, :, 0:CH],
                                                  ALU.is_ge, ALU.mult)
                last.then_inc(sc_v, 1)

            def mix(c):
                i = c // 4 if c < 8 else c // 2 - 2
                b, half = RSTD_AT[i]
                dve.wait_ge(rstd_t, (i | 1) + 1)
                r = bk[b][:, half * SEQ:(half + 1) * SEQ]
                if c < 8:
                    v.scalar_tensor_tensor(mixed[:, c, :], mixed[:, c, :], par[:, 68 + c:69 + c], r,
                                           ALU.mult, ALU.mult).then_inc(mix_v, 1)
                else:
                    v.tensor_tensor(mixed[:, c, :], mixed[:, c, :], r, ALU.mult).then_inc(mix_v, 1)

            def gate_ssd(c):
                dve.wait_ge(pj_a, freed(ZZ + c, "A"))
                v.tensor_tensor(mixed[:, c, :], mixed[:, c, :], tmp[:, c % 2, :], ALU.mult).then_inc(z_v, 1)

            for n in range(QQ, NPJ):
                if n not in GLA_STEPS:
                    low_half(n + 2)
                if QQ <= n < KK:
                    h = n - QQ
                    dve.wait_ge(pj_full, n + 1)
                    dve.wait_ge(dec_a, 6)
                    v.scalar_tensor_tensor(qd[:, h, :], bk[n % 2][:, 0:SEQ], float(P) ** -0.5, gb[:, h * T + META:(h + 1) * T],
                                           ALU.mult, ALU.mult).then_inc(pj_v, 1)
                if KK <= n < VV:
                    h = n - KK
                    dve.wait_ge(pj_full, n + 1)
                    v.tensor_tensor(gc[:, h * T:(h + 1) * T], bk[n % 2][:, 0:T], gc[:, h * T:(h + 1) * T], ALU.mult)
                    v.tensor_tensor(ga[:, h * T:(h + 1) * T], bk[n % 2][:, 0:T], ga[:, h * T:(h + 1) * T], ALU.mult).then_inc(pj_v, 1)
                if n in (20, 21):
                    for g in range(3 * (n - 20), 3 * (n - 19)):
                        xs_rows(g)
                for s in HEAD_STEPS.get(n, ()):
                    head_step(s)
                if n == ZZ:
                    dve.wait_ge(y_t, HEADS)
                for j in GLA_STEPS.get(n, ()):
                    decayed_keys(j)
                    if j > 2:
                        causal_scores(j - 2)
                    if j % 4 == 3:
                        low_half(n + 2)
                    if j % 4 == 2 and n > ZZ:
                        gate_ssd(n - ZZ - 1)
                if n == 40:
                    causal_scores(NCH - 2)
                    causal_scores(NCH - 1)
                if ZZ + 4 <= n < GG or n == ZZ + 3:
                    gate_ssd(n - ZZ)
                if n == 42:
                    dve.wait_ge(vt_t, 6)
                    v.memset(bgu, 0.0).then_inc(zeroed, 1)
                if n == GG + 4:
                    for i in range(2):
                        dve.wait_ge(ms_a, i + 1)
                        v.reciprocal(rstd[:, i, :], rstd[:, i, :]).then_inc(rec_v, 1)
                if n >= GG:
                    c = n - GG
                    dve.wait_ge(pj_a, freed(n, "A"))
                    dve.wait_ge(o_a, c + 1)
                    v.scalar_tensor_tensor(mixed[:, 8 + c, :], mixed[:, 8 + c, :], par[:, 80 + c % 2:81 + c % 2],
                                           tmp[:, n % 2, :], ALU.mult, ALU.mult).then_inc(z_v, 1)
                if n == GG + 3:
                    dve.wait_ge(ss_t, 8)
                    dve.wait_ge(ssg_t, 8)
                    for i, (b, width) in enumerate(((4, 512), (6, 256))):
                        v.tensor_scalar(rstd[:, i, :], bk[b][0:GH, 0:SEQ], 1.0 / width, EPS,
                                        ALU.mult, ALU.add).then_inc(ms_v, 1)
                if n >= GG + 6:
                    for c in range(4 * (n - GG - 6), 4 * (n - GG - 6) + 4):
                        mix(c)
            for c in range(8, 16):
                if c == 8:
                    dve.wait_ge(z_v, 16)
                mix(c)
                low_half(NPJ + c - 6)
            for n in range(NPJ + 10, NPJ + 16):
                low_half(n)
            dve.wait_ge(ss_t, 8)
            v.memset(rank[:, :, :], -1.0)
            link(v.memset(gates[:, :, :], 0.0))
            dve.wait_ge(x_again, 16)
            for t, (done, count) in enumerate(((tile_t, 1), (wo_t, 16))):
                dve.wait_ge(done, count)
                for half in range(2):
                    o = x_rows[:, t, half * 512:(half + 1) * 512]
                    v.tensor_tensor(o, bk[4 + 2 * t + half][:, :], o, ALU.add).then_inc(h_v, 1)
            dve.wait_ge(ffnw_in, 16)
            for t in range(2):
                r = ssx[:, 2 + t:3 + t]
                dve.wait_ge(ssx_a, 7 + 2 * t)
                v.tensor_scalar(r, ssx[:, t:t + 1], 1.0 / D, EPS, ALU.mult, ALU.add).then_inc(ssx_v, 1)
                dve.wait_ge(ssx_a, 8 + 2 * t)
                link(v.reciprocal(r, r))
                v.scalar_tensor_tensor(xn[:, t, :], x_rows[:, t, :], r, ffnw, ALU.mult, ALU.mult).then_inc(xn_v, 1)
            for i in range(2):
                dve.wait_ge(xt_t, 3 + i)
                v.tensor_copy(xnT[:, 4 * i:4 * i + 4, P:2 * P],
                              bk[2 + i][:, :].rearrange("p (k n) -> p k n", k=4)).then_inc(xt_v, 1)
            dve.wait_ge(xn_v, 2)
            for t in range(2):
                dve.wait_ge(part_a, t + 1)
                v.tensor_tensor(resid[:, t, :], xn[:, t, :], parts[:, 0, t, :], ALU.subtract).then_inc(part_v, 1)
            dve.wait_ge(lg_t, 1)
            dve.wait_ge(router_in, 32)
            link(v.tensor_tensor(lg, bk[0][:, 0:2 * NE].rearrange("p (t n) -> p t n", t=2),
                                 br.unsqueeze(1).broadcast_to([P, 2, NE]), ALU.add))
            v.max(m8[:, 0, :], lg[:, 0, :]).then_inc(top_v, 1)
            v.max(m8[:, 1, :], lg[:, 1, :]).then_inc(top_v, 1)
            dve.wait_ge(top_v, 2)
            v.tensor_scalar(ssx[:, 4:6], m8[:, :, 0], -1.0, None, ALU.mult).then_inc(top_v, 1)
            v.max_index(i8[:, 0, :], m8[:, 0, :], lg[:, 0, :])
            link(v.max_index(i8[:, 1, :], m8[:, 1, :], lg[:, 1, :]))
            link(v.tensor_copy(i8f, i8[:, :, 0:TOPK]))
            link(v.tensor_tensor(is_choice, expert_no[:, :].unsqueeze(1).broadcast_to([P, 2 * TOPK, NE]),
                                 i8f.rearrange("p t c -> p (t c)").unsqueeze(2).broadcast_to([P, 2 * TOPK, NE]), ALU.is_equal))
            v.tensor_reduce(chosen, is_choice.rearrange("p (t c) n -> p t n c", t=2), AX_X, ALU.add).then_inc(sel_v, 1)
            dve.wait_ge(part_a, 3)
            v.tensor_tensor(parts[:, 2, 0, :], resid[:, 0, :], parts[:, 1, 0, :], ALU.subtract).then_inc(part_v, 1)
            dve.wait_ge(rank_t, 1)
            link(v.scalar_tensor_tensor(rt.rearrange("p t n -> p (t n)"), bk[1][:, 0:2 * NE], 1.0,
                                        chosen.rearrange("p t n -> p (t n)"), ALU.add, ALU.mult))
            v.tensor_scalar(rank[:, :, 0:NE], rt, -1.0, None, ALU.add).then_inc(rank_v, 1)

            def gates_and_most():
                dve.wait_ge(top_a, 2)
                link(v.tensor_reduce(ssx[:, 0:2], ge, AX_X, ALU.add))
                link(v.reciprocal(ssx[:, 0:2], ssx[:, 0:2]))
                link(v.tensor_tensor(ge, ge, ssx[:, 0:2].unsqueeze(2).broadcast_to([P, 2, TOPK]), ALU.mult))
                link(v.tensor_tensor(gate_of, is_choice,
                                     ge.rearrange("p t c -> p (t c)").unsqueeze(2).broadcast_to([P, 2 * TOPK, NE]), ALU.mult))
                v.tensor_reduce(gates[:, :, 0:NE], gate_of.rearrange("p (t c) n -> p t n c", t=2), AX_X, ALU.add).then_inc(gates_v, 1)
                v.tensor_reduce(ssx[:, 6:7], bk[2][:, 0:NE], AX_X, ALU.max).then_inc(table_v, 1)
                dve.wait_ge(table_v, 1)
                v.tensor_copy(most[:, :], ssx[:, 6:7]).then_inc(table_v, 1)
                dve.wait_ge(gates_t, 1)
                v.tensor_copy(gatesT, bk[0][:, 0:P]).then_inc(table_v, 1)

            def build_pick(expert, inc=True):
                for t in range(2):
                    last = v.tensor_scalar(pick[:, t, :], slot_no[:, 0, :], rank[:, t, bass.ds(expert, 1)], None, ALU.is_equal)
                last.then_inc(pick_v, 1)

            def sweep(p):
                if isinstance(p, int):
                    dve.wait_ge(rank_v, 1)
                else:
                    v.tensor_scalar(rank[:, :, :], rank[:, :, :], -float(SLOTS), None, ALU.add).then_inc(shift_v, 1)
                    dve.wait_ge(shift_v, p)
                    dve.wait_ge(gath_t, p * (NE + 1))
                build_pick(0)
                if isinstance(p, int):
                    gates_and_most()
                    dve.wait_ge(gates_v, 1)
                with dve.Fori(0, NE) as e:
                    dve.wait_ge(gu_t, e + (p * NE + 1))
                    v.tensor_copy(esel, ident[:, bass.ds(e, 1)].broadcast_to([P, SLOTS])).then_inc(esel_v, 1)
                    dve.wait_ge(pg_t, e + (p * NE + 1))
                    for t in range(2):
                        last = v.tensor_scalar(pg[:, t, :], slot_no[:, :, :].rearrange("p a s -> p (a s)"),
                                               rank[:, t, bass.ds(e, 1)], gates[:, t, bass.ds(e, 1)], ALU.is_equal, ALU.mult)
                    last.then_inc(pg_v, 1)
                    dve.wait_ge(gath_t, e + (p * (NE + 1) + 1))
                    build_pick(e + 1)
                    dve.wait_ge(gu_t, e + (p * NE + 2))
                    v.tensor_scalar(gateS, bk[0][:, :], LIMIT, None, ALU.min).then_inc(clip_v, 1)
                    v.tensor_scalar(upS, bk[1][:, :], LIMIT, -LIMIT, ALU.min, ALU.max).then_inc(clip_v, 1)
                    dve.wait_ge(clip_v, e * 3 + (p * NE * 3 + 2))
                    v.scalar_tensor_tensor(upS, upS, 1.0, gateS, ALU.add, ALU.mult).then_inc(clip_v, 1)
                    dve.wait_ge(clip_v, e * 3 + (p * NE * 3 + 3))
                    dve.wait_ge(sig_a, e + (p * NE + 1))
                    v.tensor_tensor(actS, upS, sigS, ALU.mult).then_inc(act_v, 1)
                    dve.wait_ge(at_t, e + (p * NE + 1))
                    v.tensor_copy(actT.rearrange("p j h s -> p (j h s)"), bk[3][:, :]).then_inc(at_v, 1)
                dve.wait_ge(comb0_t, p * NE + NE)

            sweeps(dve, sweep, MOST)
            for t in range(2):
                if t == 1:
                    dve.wait_ge(done_t, 1)
                for half in range(2):
                    o = x_rows[:, t, half * 512:(half + 1) * 512]
                    last = v.tensor_tensor(o, bk[4 + 2 * t + half][:, :], o, ALU.add)
                last.then_inc(fin_v, 1)
            dve.wait_ge(finw_in, 16)
            for t in range(2):
                r = ssx[:, 2 + t:3 + t]
                dve.wait_ge(fin_a, 1 + 2 * t)
                v.tensor_scalar(r, ssx[:, t:t + 1], 1.0 / D, EPS, ALU.mult, ALU.add).then_inc(fin_v, 1)
                dve.wait_ge(fin_a, 2 + 2 * t)
                link(v.reciprocal(r, r))
                v.scalar_tensor_tensor(xn[:, t, :], x_rows[:, t, :], r, finw, ALU.mult, ALU.mult).then_inc(out_v, 1)


_INS = ['x', 'meta_tokens', 'mix_norm_w', 'w_in', 'conv_w', 'conv_b', 'dt_bias', 'a_log', 'd_skip', 'ssd_norm_w',
        'w_decay_up', 'b_decay', 'gla_norm_w', 'w_out', 'ffn_norm_w', 'w_router', 'b_router', 'w_gate_up',
        'b_gate_up', 'w_down', 'b_down', 'final_norm_w']
_OUTS = [((1, SEQ, D), 'float32')]


def kernel(**inputs):
    import numpy as _np
    import concourse.bacc as _bacc
    from concourse import mybir as _mybir
    from concourse.bass_utils import run_bass_kernel_spmd as _run

    nc = _bacc.Bacc("TRN2", target_bir_lowering=False, num_devices=1)
    arrays, args = {}, []
    for name in _INS:
        a = _np.ascontiguousarray(inputs[name])
        arrays[f"in_{name}_dram"] = a
        args.append(nc.dram_tensor(f"in_{name}_dram", a.shape, _mybir.dt.from_np(a.dtype), kind="ExternalInput").ap())
    for i, (shape, dtype) in enumerate(_OUTS):
        dt = _mybir.dt.from_np(_np.dtype(dtype))
        args.append(nc.dram_tensor(f"out_{i}_dram", shape, dt, kind="ExternalOutput").ap())
    hybrid_moe_kernel(nc, *args)
    r = _run(nc, [arrays], core_ids=[0])
    got = tuple(r.results[0][f"out_{i}_dram"] for i in range(len(_OUTS)))
    return got[0]
```
